# Optimizing a Trainium2 kernel written in Bass

```python
import functools
import jax, jax.numpy as jnp
from jax import lax
import numpy as np

D_MODEL = 1024
BATCH = 1
SEQ = 1024
DEPTH = 1
DEC_BATCH = 8
DEC_SEQ = 8
PAST_LEN = 8192
PAGE_SIZE = 128

GDN_HEADS = 4
GDN_DK = 128
GDN_DV = 128
CONV_W = 4
GDN_CHUNK = 64
MLA_HEADS = 4
Q_LORA = 256
KV_LORA = 256
QK_NOPE = 128
QK_ROPE = 64
V_DIM = 128
ROPE_THETA = 10000.0
QBLK = 128
N_EXPERTS = 64
TOP_K = 8
N_GROUPS = 8
TOPK_GROUPS = 4
D_EXPERT = 256
D_SHARED = 256
ROUTED_SCALE = 2.5
EXPERT_BLOCK = 128
PLE_DIM = 256
EPS = 1e-6

GDN_QK_W = GDN_HEADS * GDN_DK
GDN_V_W = GDN_HEADS * GDN_DV
CONV_CH = 2 * GDN_QK_W + GDN_V_W
MLA_V_W = MLA_HEADS * V_DIM
MIX_WIDTH = GDN_V_W + MLA_V_W
MLA_Q_W = MLA_HEADS * (QK_NOPE + QK_ROPE)
MLA_SCALE = (QK_NOPE + QK_ROPE) ** -0.5
IN_SIZES = (CONV_CH, GDN_V_W, GDN_HEADS, GDN_HEADS, Q_LORA, KV_LORA, QK_ROPE)
IN_SPLITS = [int(s) for s in np.cumsum(IN_SIZES)[:-1]]
IN_WIDTH = int(sum(IN_SIZES))

kernel_name = 'hybrid_gdn_mla_moe_ple_step'

def rmsnorm(x, g):
    xf = x.astype(jnp.float32)
    y = xf * lax.rsqrt(jnp.mean(xf * xf, axis=-1, keepdims=True) + EPS)
    return (y * g.astype(jnp.float32)).astype(x.dtype)

def l2norm(x):
    return x * lax.rsqrt(jnp.sum(x * x, axis=-1, keepdims=True) + EPS)

def rope(x, pos):
    half = x.shape[-1] // 2
    inv = ROPE_THETA ** (-jnp.arange(half, dtype=jnp.float32) / half)
    ang = pos.astype(jnp.float32)[:, None] * inv[None, :]
    cos = jnp.cos(ang)[None, :, None, :]
    sin = jnp.sin(ang)[None, :, None, :]
    xf = x.astype(jnp.float32)
    x1, x2 = xf[..., :half], xf[..., half:]
    return jnp.concatenate([x1 * cos - x2 * sin, x2 * cos + x1 * sin], axis=-1).astype(x.dtype)

def short_conv(x_new, buf, w):
    t = x_new.shape[1]
    xx = jnp.concatenate([buf.astype(x_new.dtype), x_new], axis=1)
    y = sum(xx[:, j:j + t] * w[j] for j in range(CONV_W))
    return jax.nn.silu(y), xx[:, t:]

def gated_delta_chunked(q, k, v, beta, g, s0):
    b, t, h, dk = q.shape
    dv = v.shape[-1]
    n = -(-t // GDN_CHUNK)
    pad = n * GDN_CHUNK - t

    def to_chunks(x):
        x = jnp.pad(x, [(0, 0), (0, pad)] + [(0, 0)] * (x.ndim - 2))
        x = jnp.moveaxis(x, 2, 1)
        return x.reshape((b, h, n, GDN_CHUNK) + x.shape[3:])

    qc, kc, vc, bc, gc = (to_chunks(a) for a in (q, k, v, beta, g))
    gc = jnp.cumsum(gc, axis=-1)
    idx = jnp.arange(GDN_CHUNK)
    incl = idx[:, None] >= idx[None, :]
    strict = idx[:, None] > idx[None, :]
    decay = jnp.exp(jnp.where(incl, gc[..., :, None] - gc[..., None, :], -jnp.inf))
    kb = kc * bc[..., None]
    lower = jnp.where(strict, jnp.einsum('bhncd,bhnsd->bhncs', kb, kc) * decay, 0.0)
    m = lower + jnp.eye(GDN_CHUNK, dtype=lower.dtype)
    rhs = jnp.concatenate([vc * bc[..., None], kb * jnp.exp(gc)[..., None]], axis=-1)
    sol = lax.linalg.triangular_solve(m, rhs, left_side=True, lower=True, unit_diagonal=True)
    u, w = sol[..., :dv], sol[..., dv:]
    qk = jnp.where(incl, jnp.einsum('bhncd,bhnsd->bhncs', qc, kc) * decay, 0.0)

    def step(s, xs):
        q_i, k_i, u_i, w_i, g_i, qk_i = xs
        v_new = u_i - jnp.einsum('bhcd,bhde->bhce', w_i, s)
        o_i = (jnp.einsum('bhcd,bhde->bhce', q_i * jnp.exp(g_i)[..., None], s)
               + jnp.einsum('bhcs,bhse->bhce', qk_i, v_new))
        g_last = g_i[..., -1]
        s = (s * jnp.exp(g_last)[..., None, None]
             + jnp.einsum('bhcd,bhce->bhde', k_i * jnp.exp(g_last[..., None] - g_i)[..., None], v_new))
        return s, o_i

    xs = tuple(jnp.moveaxis(a, 2, 0) for a in (qc, kc, u, w, gc, qk))
    s_fin, o = lax.scan(step, s0, xs)
    o = jnp.moveaxis(o, 0, 2).reshape(b, h, n * GDN_CHUNK, dv)[:, :, :t]
    return jnp.moveaxis(o, 1, 2), s_fin

def mla_prompt_attend(q_lat, q_rope, ckv, krope):
    b, s, h, r = q_lat.shape
    nb = s // QBLK
    ql = jnp.moveaxis(q_lat.reshape(b, nb, QBLK, h, r), 1, 0)
    qr = jnp.moveaxis(q_rope.reshape(b, nb, QBLK, h, -1), 1, 0)
    kpos = jnp.arange(s)

    def block(args):
        ql_b, qr_b, i = args
        sc = (jnp.einsum('bthr,bsr->bhts', ql_b, ckv)
              + jnp.einsum('bthe,bse->bhts', qr_b, krope)).astype(jnp.float32) * MLA_SCALE
        qpos = i * QBLK + jnp.arange(QBLK)
        sc = jnp.where(kpos[None, :] <= qpos[:, None], sc, -jnp.inf)
        p = jax.nn.softmax(sc, axis=-1).astype(ckv.dtype)
        return jnp.einsum('bhts,bsr->bthr', p, ckv)

    o = lax.map(block, (ql, qr, jnp.arange(nb)))
    return jnp.moveaxis(o, 0, 1).reshape(b, s, h, r)

def mla_paged_attend(q_lat, q_rope, ckv, krope, cache_ckv, cache_krope, page_table):
    b, t = q_lat.shape[:2]
    past = page_table.shape[1] * cache_ckv.shape[1]
    ckv_past = cache_ckv[page_table].reshape(b, past, -1)
    kr_past = cache_krope[page_table].reshape(b, past, -1)
    s_past = (jnp.einsum('bthr,bsr->bhts', q_lat, ckv_past)
              + jnp.einsum('bthe,bse->bhts', q_rope, kr_past)).astype(jnp.float32) * MLA_SCALE
    s_new = (jnp.einsum('bthr,bsr->bhts', q_lat, ckv)
             + jnp.einsum('bthe,bse->bhts', q_rope, krope)).astype(jnp.float32) * MLA_SCALE
    causal = jnp.tril(jnp.ones((t, t), dtype=bool))
    s_new = jnp.where(causal, s_new, -jnp.inf)
    p = jax.nn.softmax(jnp.concatenate([s_past, s_new], axis=-1), axis=-1).astype(ckv.dtype)
    return (jnp.einsum('bhts,bsr->bthr', p[..., :past], ckv_past)
            + jnp.einsum('bhts,bsr->bthr', p[..., past:], ckv))

def swiglu(x, wg, wu, wd):
    return (jax.nn.silu(x @ wg) * (x @ wu)) @ wd

def route(x2, w_router, router_bias):
    n = x2.shape[0]
    scores = jax.nn.sigmoid((x2 @ w_router).astype(jnp.float32))
    biased = scores + router_bias.astype(jnp.float32)
    grouped = biased.reshape(n, N_GROUPS, N_EXPERTS // N_GROUPS)
    group_score = lax.top_k(grouped, 2)[0].sum(-1)
    _, gidx = lax.top_k(group_score, TOPK_GROUPS)
    gmask = jax.nn.one_hot(gidx, N_GROUPS, dtype=jnp.float32).sum(1) > 0
    emask = jnp.repeat(gmask, N_EXPERTS // N_GROUPS, axis=1)
    _, idx = lax.top_k(jnp.where(emask, biased, -jnp.inf), TOP_K)
    w = jnp.take_along_axis(scores, idx, axis=1)
    w = w / (w.sum(-1, keepdims=True) + 1e-20) * ROUTED_SCALE
    return idx, w

def routed_experts(x2, idx, wts, wg, wu, wd):
    n, d = x2.shape
    a = n * TOP_K
    flat_e = idx.reshape(a)
    flat_tok = (jnp.arange(a, dtype=jnp.int32) // TOP_K).astype(jnp.int32)
    flat_w = wts.reshape(a)
    order = jnp.argsort(flat_e)
    se = flat_e[order]
    counts = jnp.bincount(flat_e, length=N_EXPERTS)
    pcounts = (counts + EXPERT_BLOCK - 1) // EXPERT_BLOCK * EXPERT_BLOCK
    start = jnp.cumsum(counts) - counts
    pend = jnp.cumsum(pcounts)
    pstart = pend - pcounts
    dest = pstart[se] + jnp.arange(a) - start[se]
    nblk = (a + N_EXPERTS * (EXPERT_BLOCK - 1) + EXPERT_BLOCK - 1) // EXPERT_BLOCK
    rows = nblk * EXPERT_BLOCK
    row_tok = jnp.full((rows,), n, jnp.int32).at[dest].set(flat_tok[order])
    row_w = jnp.zeros((rows,), jnp.float32).at[dest].set(flat_w[order])
    blk_e = jnp.minimum(jnp.searchsorted(pend, jnp.arange(nblk) * EXPERT_BLOCK, side='right'),
                        N_EXPERTS - 1)
    xpad = jnp.concatenate([x2, jnp.zeros((1, d), x2.dtype)], axis=0)

    def step(out, args):
        tok, rw, e = args
        xb = xpad[tok]
        yb = swiglu(xb, wg[e], wu[e], wd[e]) * rw[:, None].astype(x2.dtype)
        return out.at[tok].add(yb), None

    out, _ = lax.scan(step, jnp.zeros((n + 1, d), x2.dtype),
                      (row_tok.reshape(nblk, EXPERT_BLOCK), row_w.reshape(nblk, EXPERT_BLOCK), blk_e))
    return out[:n]

def moe_ffn(x, w_router, router_bias, w_exp_gate, w_exp_up, w_exp_down, w_sh_gate, w_sh_up, w_sh_down):
    b, t, d = x.shape
    x2 = x.reshape(b * t, d)
    idx, wts = route(x2, w_router, router_bias)
    y = routed_experts(x2, idx, wts, w_exp_gate, w_exp_up, w_exp_down) + swiglu(x2, w_sh_gate, w_sh_up, w_sh_down)
    return y.reshape(b, t, d)

def hybrid_layer(h, p_l, pos, gdn_state, conv_buf, attend, lw):
    b, t, _ = h.shape
    f32 = jnp.float32
    u = rmsnorm(h, lw['g_mix'])
    proj = u @ lw['w_in']
    qkv_pre, z, b_in, a_in, c_q, c_kv, k_r = jnp.split(proj, IN_SPLITS, axis=-1)

    qkv, conv_new = short_conv(qkv_pre, conv_buf, lw['gdn_conv_w'])
    q, k, v = jnp.split(qkv, [GDN_QK_W, 2 * GDN_QK_W], axis=-1)
    q = l2norm(q.reshape(b, t, GDN_HEADS, GDN_DK).astype(f32)) * GDN_DK ** -0.5
    k = l2norm(k.reshape(b, t, GDN_HEADS, GDN_DK).astype(f32))
    v = v.reshape(b, t, GDN_HEADS, GDN_DV).astype(f32)
    beta = jax.nn.sigmoid(b_in.astype(f32))
    g = -jnp.exp(lw['gdn_a_log'].astype(f32)) * jax.nn.softplus(a_in.astype(f32) + lw['gdn_dt_bias'].astype(f32))
    o, gdn_new = gated_delta_chunked(q, k, v, beta, g, gdn_state.astype(f32))
    o = rmsnorm(o, lw['gdn_norm']) * jax.nn.silu(z.reshape(b, t, GDN_HEADS, GDN_DV).astype(f32))
    o_gdn = o.reshape(b, t, GDN_V_W).astype(h.dtype)

    qh = (rmsnorm(c_q, lw['mla_g_q']) @ lw['mla_w_uq']).reshape(b, t, MLA_HEADS, QK_NOPE + QK_ROPE)
    q_nope, q_rope = qh[..., :QK_NOPE], rope(qh[..., QK_NOPE:], pos)
    ckv = rmsnorm(c_kv, lw['mla_g_kv'])
    krope = rope(k_r[:, :, None, :], pos)[:, :, 0]
    q_lat = jnp.einsum('bthn,rhn->bthr', q_nope, lw['mla_w_uk'])
    o_lat = attend(q_lat, q_rope, ckv, krope)
    o_mla = jnp.einsum('bthr,rhv->bthv', o_lat, lw['mla_w_uv']).reshape(b, t, MLA_V_W)

    h = h + jnp.concatenate([o_gdn, o_mla], axis=-1) @ lw['w_out']
    h = h + moe_ffn(rmsnorm(h, lw['g_ffn']), lw['w_router'], lw['router_bias'],
                    lw['w_exp_gate'], lw['w_exp_up'], lw['w_exp_down'],
                    lw['w_sh_gate'], lw['w_sh_up'], lw['w_sh_down'])
    gate = jax.nn.sigmoid(rmsnorm(h, lw['g_ple']) @ lw['w_ple_gate'])
    h = h + gate * (p_l.astype(h.dtype) @ lw['w_ple_proj'])
    return h, ckv, krope, gdn_new, conv_new

def setup_inputs(seed: int = 0) -> dict:
    key = jax.random.key(seed)
    ks = iter(jax.random.split(key, 48))
    f32 = jnp.float32

    def nrm(shape, scale):
        return jax.random.normal(next(ks), shape, f32) * scale

    def gain(shape):
        return 1.0 + nrm(shape, 0.02)

    n_pages = PAST_LEN // PAGE_SIZE
    n_pool = (DEC_BATCH * n_pages * 5) // 4
    x_prompt = nrm((BATCH, SEQ, D_MODEL), 1.0)
    x_sample = nrm((DEC_BATCH, DEC_SEQ, D_MODEL), 1.0)
    p_prompt = nrm((DEPTH, BATCH, SEQ, PLE_DIM), 1.0)
    p_sample = nrm((DEPTH, DEC_BATCH, DEC_SEQ, PLE_DIM), 1.0)
    cache_ckv = nrm((DEPTH, n_pool, PAGE_SIZE, KV_LORA), 1.0)
    cache_krope = nrm((DEPTH, n_pool, PAGE_SIZE, QK_ROPE), 1.0)
    state_gdn = nrm((DEPTH, DEC_BATCH, GDN_HEADS, GDN_DK, GDN_DV), 0.05)
    state_conv = nrm((DEPTH, DEC_BATCH, CONV_W - 1, CONV_CH), 1.0)
    page_table = jax.random.permutation(next(ks), n_pool)[:DEC_BATCH * n_pages].reshape(
        DEC_BATCH, n_pages).astype(jnp.int32)
    a_log = jnp.log(jax.random.uniform(next(ks), (DEPTH, GDN_HEADS), f32, 1.0, 16.0))
    dt = jnp.exp(jax.random.uniform(next(ks), (DEPTH, GDN_HEADS), f32, np.log(1e-3), np.log(1e-1)))
    dt_bias = dt + jnp.log(-jnp.expm1(-dt))
    return {
        'x_prompt': x_prompt,
        'x_sample': x_sample,
        'p_prompt': p_prompt,
        'p_sample': p_sample,
        'cache_ckv': cache_ckv,
        'cache_krope': cache_krope,
        'state_gdn': state_gdn,
        'state_conv': state_conv,
        'page_table': page_table,
        'g_mix': gain((DEPTH, D_MODEL)),
        'w_in': nrm((DEPTH, D_MODEL, IN_WIDTH), D_MODEL ** -0.5),
        'gdn_conv_w': nrm((DEPTH, CONV_W, CONV_CH), CONV_W ** -0.5),
        'gdn_a_log': a_log,
        'gdn_dt_bias': dt_bias,
        'gdn_norm': gain((DEPTH, GDN_DV)),
        'mla_g_q': gain((DEPTH, Q_LORA)),
        'mla_w_uq': nrm((DEPTH, Q_LORA, MLA_Q_W), Q_LORA ** -0.5),
        'mla_g_kv': gain((DEPTH, KV_LORA)),
        'mla_w_uk': nrm((DEPTH, KV_LORA, MLA_HEADS, QK_NOPE), KV_LORA ** -0.5),
        'mla_w_uv': nrm((DEPTH, KV_LORA, MLA_HEADS, V_DIM), KV_LORA ** -0.5),
        'w_out': nrm((DEPTH, MIX_WIDTH, D_MODEL), MIX_WIDTH ** -0.5),
        'g_ffn': gain((DEPTH, D_MODEL)),
        'w_router': nrm((DEPTH, D_MODEL, N_EXPERTS), D_MODEL ** -0.5),
        'router_bias': nrm((DEPTH, N_EXPERTS), 0.01),
        'w_exp_gate': nrm((DEPTH, N_EXPERTS, D_MODEL, D_EXPERT), D_MODEL ** -0.5),
        'w_exp_up': nrm((DEPTH, N_EXPERTS, D_MODEL, D_EXPERT), D_MODEL ** -0.5),
        'w_exp_down': nrm((DEPTH, N_EXPERTS, D_EXPERT, D_MODEL), D_EXPERT ** -0.5),
        'w_sh_gate': nrm((DEPTH, D_MODEL, D_SHARED), D_MODEL ** -0.5),
        'w_sh_up': nrm((DEPTH, D_MODEL, D_SHARED), D_MODEL ** -0.5),
        'w_sh_down': nrm((DEPTH, D_SHARED, D_MODEL), D_SHARED ** -0.5),
        'g_ple': gain((DEPTH, D_MODEL)),
        'w_ple_gate': nrm((DEPTH, D_MODEL, D_MODEL), D_MODEL ** -0.5),
        'w_ple_proj': nrm((DEPTH, PLE_DIM, D_MODEL), PLE_DIM ** -0.5),
        'g_final': gain((D_MODEL,)),
    }

def reference(x_prompt, x_sample, p_prompt, p_sample, cache_ckv, cache_krope, state_gdn, state_conv,
              page_table, g_mix, w_in, gdn_conv_w, gdn_a_log, gdn_dt_bias, gdn_norm, mla_g_q, mla_w_uq,
              mla_g_kv, mla_w_uk, mla_w_uv, w_out, g_ffn, w_router, router_bias, w_exp_gate, w_exp_up,
              w_exp_down, w_sh_gate, w_sh_up, w_sh_down, g_ple, w_ple_gate, w_ple_proj, g_final):
    hp, hs = x_prompt, x_sample
    bp, tp = hp.shape[0], hp.shape[1]
    ts = hs.shape[1]
    past = page_table.shape[1] * cache_ckv.shape[2]
    pos_p = jnp.arange(tp)
    pos_s = past + jnp.arange(ts)
    ckv_p, kr_p, gdn_p, conv_p = [], [], [], []
    ckv_s, kr_s, gdn_s, conv_s = [], [], [], []
    for i in range(DEPTH):
        lw = dict(g_mix=g_mix[i], w_in=w_in[i], gdn_conv_w=gdn_conv_w[i], gdn_a_log=gdn_a_log[i],
                  gdn_dt_bias=gdn_dt_bias[i], gdn_norm=gdn_norm[i], mla_g_q=mla_g_q[i], mla_w_uq=mla_w_uq[i],
                  mla_g_kv=mla_g_kv[i], mla_w_uk=mla_w_uk[i], mla_w_uv=mla_w_uv[i], w_out=w_out[i],
                  g_ffn=g_ffn[i], w_router=w_router[i], router_bias=router_bias[i], w_exp_gate=w_exp_gate[i],
                  w_exp_up=w_exp_up[i], w_exp_down=w_exp_down[i], w_sh_gate=w_sh_gate[i], w_sh_up=w_sh_up[i],
                  w_sh_down=w_sh_down[i], g_ple=g_ple[i], w_ple_gate=w_ple_gate[i], w_ple_proj=w_ple_proj[i])
        gdn0 = jnp.zeros((bp, GDN_HEADS, GDN_DK, GDN_DV), state_gdn.dtype)
        conv0 = jnp.zeros((bp, CONV_W - 1, CONV_CH), state_conv.dtype)
        hp, c1, k1, s1, v1 = hybrid_layer(hp, p_prompt[i], pos_p, gdn0, conv0, mla_prompt_attend, lw)
        attend_s = functools.partial(mla_paged_attend, cache_ckv=cache_ckv[i], cache_krope=cache_krope[i],
                                     page_table=page_table)
        hs, c2, k2, s2, v2 = hybrid_layer(hs, p_sample[i], pos_s, state_gdn[i], state_conv[i], attend_s, lw)
        ckv_p.append(c1); kr_p.append(k1); gdn_p.append(s1.astype(state_gdn.dtype)); conv_p.append(v1.astype(state_conv.dtype))
        ckv_s.append(c2); kr_s.append(k2); gdn_s.append(s2.astype(state_gdn.dtype)); conv_s.append(v2.astype(state_conv.dtype))
    y_prompt = rmsnorm(hp, g_final)
    y_sample = rmsnorm(hs, g_final)
    return (y_prompt, y_sample,
            jnp.stack(ckv_p), jnp.stack(kr_p), jnp.stack(gdn_p), jnp.stack(conv_p),
            jnp.stack(ckv_s), jnp.stack(kr_s), jnp.stack(gdn_s), jnp.stack(conv_s))


_drawn_inputs = setup_inputs


def setup_inputs(seed=0):
    import zlib

    import numpy as np

    out = dict(_drawn_inputs(seed))
    spreads = {}
    factors = {'mla_g_q': 3.429, 'g_ple': 46.153, 'g_final': 8.036}
    for name, (base, spread) in spreads.items():
        noise = np.random.default_rng([zlib.crc32(name.encode()), seed]).standard_normal(out[name].shape)
        drawn = base * np.exp(spread * noise) if base else spread * noise
        out[name] = __import__('jax').numpy.asarray(drawn.astype(out[name].dtype))
    for name, factor in factors.items():
        out[name] = (out[name] * factor).astype(out[name].dtype)
    return out
```

```python
from contextlib import ExitStack

import numpy as np
import concourse.bass as bass
from concourse import mybir

F32 = mybir.dt.float32
I32 = mybir.dt.int32
ALU = mybir.AluOpType
ACT = mybir.ActivationFunctionType
AX_X = mybir.AxisListType.X

P = 128
D = 1024
KD = D // P
TP = 8
NT = TP + 1
SB, ST = 8, 8
SR = SB * ST
H = 4
DK = 128
CC = 3 * H
R = 256
RO = 64
ZW, LW, TW = H * DK, 2 * R, RO + 2 * H
NW = ZW + LW + TW
PAGE = 128
NPAGE = 64
EPS = 1e-6
MLA_SCALE = float(DK + RO) ** -0.5
NEG = -1e30
E = 64
TOPK = 8
NG = 8
GW = E // NG
TOPG = 4
DE = 256
CAP = 192
SLOTS = 6 * CAP
LV = 7


class Ctx:

    def __init__(self, nc, stack):
        self.nc, self.stack = nc, stack

    def sb(self, name, shape, dt=F32):
        return self.stack.enter_context(self.nc.sbuf_tensor(name, shape, dt))

    def ps(self, name, shape, dt=F32):
        return self.stack.enter_context(self.nc.psum_tensor(name, shape, dt))


class Semaphores:

    def __init__(self, nc):
        self.nc, self.stack, self.taken = nc, ExitStack(), []

    def sem(self, name):
        self.taken.append(self.stack.enter_context(self.nc.semaphore(name)))
        return self.taken[-1]

    def __enter__(self):
        return self

    def __exit__(self, *error):
        if error[0] is None:
            nums = sorted(t.num for t in self.taken)
            runs = [[nums[0], nums[0] + 1]]
            for n in nums[1:]:
                if n == runs[-1][1]:
                    runs[-1][1] = n + 1
                else:
                    runs.append([n, n + 1])
            with self.nc.Block() as block:

                @block.gpsimd
                def _(pool):
                    for a, b in runs:
                        pool.dma_reset(range(a, b))
                        pool.sem_clear(range(a, b))

        self.stack.close()


def tiles(eng, n, body, first=0):
    assert n % 2 == 0 and first == 0
    with eng.Fori(0, n // 2) as r:
        for u in range(2):
            body(r * 2 + u, u, r)


def bc(ap, shape):
    return ap.to_broadcast(shape)



def phase_project(nc, d):
    with ExitStack() as st, Semaphores(nc) as s:
        c = Ctx(nc, st)
        wn = c.sb("p1_wn", [P, KD, NW])
        wq = c.sb("p1_wq", [P, KD, CC * P])
        ident = c.sb("p1_ident", [P, P])
        g_bc = c.sb("p1_g", [P, D])
        cw = c.sb("p1_cw", [P, CC, 4])
        xb = c.sb("p1_x", [P, 2, D])
        sq = c.sb("p1_sq", [P, D])
        ss = c.sb("p1_ss", [P, 2])
        eps = c.sb("p1_eps", [P, 1])
        un = c.sb("p1_un", [P, D])
        uT = c.sb("p1_uT", [P, 2, KD, P])
        nat = c.sb("p1_nat", [P, NW])
        qx = c.sb("p1_qx", [P, CC, P + 3])
        qs = c.sb("p1_qs", [P, CC, SB, ST + 3])
        sc = c.sb("p1_sc", [P, CC, SB, 3])
        cy = c.sb("p1_cy", [P, CC, P])
        sy = c.sb("p1_sy", [P, CC, P])
        pT = c.ps("p1_pT", [P, KD, P])
        pN = c.ps("p1_pN", [P, 3, 512])
        pQ = c.ps("p1_pQ", [P, 3, 4, P])

        consts_in = s.sem("p1_consts_in")
        w_in = [s.sem(f"p1_w_in{n}") for n in range(2)]
        state_in = s.sem("p1_state_in")
        x_in = [s.sem(f"p1_x_in{u}") for u in range(2)]
        eps_ready = s.sem("p1_eps_ready")
        rs_ready = s.sem("p1_rs_ready")
        u_ready = s.sem("p1_u_ready")
        u_turned = s.sem("p1_u_turned")
        uT_ready = s.sem("p1_uT_ready")
        nat_done = s.sem("p1_nat_done")
        nat_out = s.sem("p1_nat_out")
        nat_stored = s.sem("p1_nat_stored")
        qkv_done = s.sem("p1_qkv_done")
        qkv_out = s.sem("p1_qkv_out")
        conv_done = s.sem("p1_conv_done")
        silu_done = s.sem("p1_silu_done")
        y_stored = s.sem("p1_y_stored")
        tails_ready = s.sem("p1_tails_ready")
        tails_stored = s.sem("p1_tails_stored")
        cols = [(0, ZW), (ZW, LW), (ZW + LW, TW)]

        with nc.Block() as block:

            @block.sync
            def _(sp):
                def load(t, u):
                    sp.dma_start(xb[:, u, :], d["x"][t]).then_inc(x_in[u], 16)

                load(0, 0)
                load(1, 1)
                sp.dma_start(ident[:], d["ident"]).then_inc(consts_in, 16)
                sp.dma_start(g_bc[:], d["g_mix"].partition_broadcast(P)).then_inc(consts_in, 16)
                sp.dma_start(cw[:], d["conv_w"]).then_inc(consts_in, 16)
                sp.dma_start(wn[:], d["w_nat"]).then_inc(w_in[0], 16)
                sp.dma_start(wq[:], d["w_qkv"]).then_inc(w_in[1], 16)
                sp.dma_start(sc[:], d["state_conv"]).then_inc(state_in, 16)

                def reload(t, u, r):
                    sp.wait_ge(u_ready, t + 1)
                    load(t + 2, u)

                def store(t, u, r):
                    sp.wait_ge(nat_out, 3 * t + 3)
                    sp.dma_start(d["nat"][t], nat[:]).then_inc(nat_stored, 16)
                    sp.wait_ge(silu_done, t + 1)
                    sp.dma_start(d["yT"][t], sy[:]).then_inc(y_stored, 16)

                def step(t, u, r):
                    reload(t, u, r)
                    store(t, u, r)

                tiles(sp, TP - 2, step)
                step(TP - 2, 0, 0)
                store(TP - 1, 1, 0)
                sp.dma_start(d["conv_p"], qx[:, :, P:P + 3]).then_inc(tails_stored, 16)
                sp.wait_ge(tails_ready, 1)
                sp.dma_start(d["conv_s"], sc[:]).then_inc(tails_stored, 16)
                store(TP, 0, 0)
                sp.wait_ge(nat_stored, 16 * NT)
                sp.wait_ge(y_stored, 16 * NT)
                sp.wait_ge(tails_stored, 32)

            @block.scalar
            def _(act):
                def norm(t, u, r):
                    act.wait_ge(x_in[u], 16 * r + 16)
                    act.activation(sq[:], xb[:, u, :], ACT.Square, accum_out=ss[:, u:u + 1])
                    act.drain()
                    act.activation(ss[:, u:u + 1], ss[:, u:u + 1], ACT.Sqrt, bias=eps[:], scale=1.0 / D).then_inc(rs_ready, 1)
                    act.wait_ge(u_turned, t + 1)
                    for a in range(2):
                        act.copy(uT[:, u, 4 * a:4 * a + 4, :], pT[:, 4 * a:4 * a + 4, :]).then_inc(uT_ready, 1)

                def out(t, u, r):
                    act.wait_ge(nat_stored, 16 * t)
                    for n, (at, w) in enumerate(cols):
                        act.wait_ge(nat_done, 3 * t + n + 1)
                        act.copy(nat[:, at:at + w], pN[:, n, 0:w]).then_inc(nat_out, 1)
                    act.wait_ge(conv_done, t + 1)
                    act.wait_ge(y_stored, 16 * t)
                    act.activation(sy[:], cy[:], ACT.Silu).then_inc(silu_done, 1)

                act.wait_ge(eps_ready, 1)
                norm(0, 0, 0)

                def step(t, u, r):
                    act.wait_ge(qkv_done, 3 * t)
                    norm(t + 1, 1 - u, r + u)
                    out(t, u, r)

                tiles(act, TP, step)
                out(TP, 0, TP // 2)

            @block.vector
            def _(dve):
                def norm(t, u, r):
                    dve.wait_ge(rs_ready, t + 1)
                    dve.reciprocal(ss[:, u:u + 1], ss[:, u:u + 1])
                    dve.drain()
                    dve.wait_ge(u_turned, t)
                    dve.scalar_tensor_tensor(un[:], xb[:, u, :], ss[:, u:u + 1], g_bc[:],
                                             ALU.mult, ALU.mult).then_inc(u_ready, 1)

                def conv(t, taps, view, width):
                    dve.wait_ge(silu_done, t)
                    for j in range(4):
                        for k in range(CC):
                            if j == 0:
                                i = dve.tensor_scalar(view(k), taps(k, 0), cw[:, k, 0:1], None, ALU.mult)
                            else:
                                i = dve.scalar_tensor_tensor(view(k), taps(k, j), cw[:, k, j:j + 1], view(k),
                                                             ALU.mult, ALU.add)
                        if j < 3:
                            dve.drain()
                    i.then_inc(conv_done, 1)

                def step(t, u, r):
                    norm(t + 1, 1 - u, r + u)
                    dve.tensor_copy(qx[:, :, 0:3], qx[:, :, P:P + 3])
                    dve.drain()
                    for g in range(3):
                        dve.wait_ge(qkv_done, 3 * t + g + 1)
                        dve.tensor_copy(qx[:, 4 * g:4 * g + 4, 3:P + 3], pQ[:, g]).then_inc(qkv_out, 1)
                    dve.drain()
                    conv(t, lambda k, j: qx[:, k, j:j + P], lambda k: cy[:, k, :], P)

                dve.memset(eps[:], EPS).then_inc(eps_ready, 1)
                dve.memset(qx[:, :, P:P + 3], 0.0)
                dve.wait_ge(consts_in, 48)
                norm(0, 0, 0)
                tiles(dve, TP, step)
                dve.wait_ge(state_in, 16)
                dve.tensor_copy(qs[:, :, :, 0:3], sc[:])
                for g in range(3):
                    dve.wait_ge(qkv_done, 3 * TP + g + 1)
                    dve.tensor_copy(qs[:, 4 * g:4 * g + 4, :, 3:ST + 3],
                                    pQ[:, g, :, 0:SR].rearrange("p c (b t) -> p c b t", b=SB)).then_inc(qkv_out, 1)
                dve.wait_ge(silu_done, TP)
                dve.memset(cy[:, :, SR:P], 0.0)
                dve.drain()
                dve.tensor_copy(sc[:], qs[:, :, :, ST:ST + 3]).then_inc(tails_ready, 1)
                conv(TP, lambda k, j: qs[:, k, :, j:j + ST],
                     lambda k: cy[:, k, 0:SR].rearrange("p (b t) -> p b t", b=SB), SR)

            @block.tensor
            def _(pe):
                def turn(t, u, r):
                    pe.wait_ge(u_ready, t + 1)
                    pe.wait_ge(uT_ready, 2 * t)
                    for k in range(KD):
                        i = pe.transpose(pT[:, k, :], un[:, k * P:(k + 1) * P], ident[:])
                    i.then_inc(u_turned, 1)

                def products(t, u, r):
                    pe.wait_ge(uT_ready, 2 * t + 2)
                    pe.wait_ge(nat_out, 3 * t)
                    for n, (at, w) in enumerate(cols):
                        for k in range(KD):
                            i = pe.matmul(pN[:, n, 0:w], uT[:, u, k, :], wn[:, k, at:at + w],
                                          start=(k == 0), stop=(k == KD - 1))
                        i.then_inc(nat_done, 1)
                    pe.wait_ge(qkv_out, 3 * t)
                    for g in range(3):
                        for m in range(4):
                            ch = (4 * g + m) * P
                            for k in range(KD):
                                i = pe.matmul(pQ[:, g, m, :], wq[:, k, ch:ch + P], uT[:, u, k, :],
                                              start=(k == 0), stop=(k == KD - 1))
                        i.then_inc(qkv_done, 1)

                pe.wait_ge(consts_in, 48)
                turn(0, 0, 0)
                pe.wait_ge(w_in[0], 16)
                pe.wait_ge(w_in[1], 16)

                def step(t, u, r):
                    turn(t + 1, 1 - u, r)
                    products(t, u, r)

                tiles(pe, TP, step)
                products(TP, 0, TP // 2)


def phase_gdn(nc, d):
    with ExitStack() as st, Semaphores(nc) as s:
        c = Ctx(nc, st)
        W4 = [P, H, P]
        ident = c.sb("p2_ident", [P, P])
        tri2 = c.sb("p2_tri", [P, 2, P])
        same2 = c.sb("p2_same", [P, 2, P])
        levels = c.sb("p2_levels", [P, LV, P])
        norm_bc = c.sb("p2_norm", [P, P])
        rows_b = c.sb("p2_rows_b", [P, SB])
        dt_bc = c.sb("p2_dt", [P, H])
        ea_bc = c.sb("p2_ea", [P, H])
        eps = c.sb("p2_eps", [P, 1])
        y = c.sb("p2_y", [P, 2, CC, P])
        zb = c.sb("p2_z", [P, 2, ZW + 2 * H])
        sq = c.sb("p2_sq", [P, 2, H, P])
        rn = c.sb("p2_rn", [P, 2 * H])
        qn = c.sb("p2_qn", W4)
        kn = c.sb("p2_kn", W4)
        vb = c.sb("p2_vb", W4)
        beta = c.sb("p2_beta", [P, H])
        g = c.sb("p2_g", [P, H])
        t0 = c.sb("p2_t0", [P, H])
        t1 = c.sb("p2_t1", [P, H])
        gb = c.sb("p2_gb", W4)
        bb = c.sb("p2_bb", W4)
        gc = c.sb("p2_gc", [P, 2 * H])
        eg = c.sb("p2_eg", [P, H])
        ek = c.sb("p2_ek", [P, H])
        bg = c.sb("p2_bg", [P, H])
        egrow = c.sb("p2_egrow", W4)
        dec = c.sb("p2_dec", W4)
        qT = c.sb("p2_qT", W4)
        kT = c.sb("p2_kT", W4)
        kbT = c.sb("p2_kbT", W4)
        qgT = c.sb("p2_qgT", W4)
        kbg = c.sb("p2_kbg", W4)
        kd = c.sb("p2_kd", W4)
        LT = c.sb("p2_LT", W4)
        QKT = c.sb("p2_QKT", W4)
        CT = c.sb("p2_CT", [P, 2, H, P])
        Wm = c.sb("p2_W", W4)
        T = c.sb("p2_T", W4)
        TT = c.sb("p2_TT", W4)
        nwT = c.sb("p2_nwT", W4)
        vn = c.sb("p2_vn", W4)
        S = c.sb("p2_S", W4)
        o1 = c.sb("p2_o1", W4)
        ez = c.sb("p2_ez", W4)
        oT = c.sb("p2_oT", W4)
        Ss = c.sb("p2_Ss", [P, SB, H, P])
        kdb = c.sb("p2_kdb", W4)
        vnT = c.sb("p2_vnT", W4)
        bank = [c.ps(f"p2_bank{n}", W4) for n in range(8)]

        consts_in = s.sem("p2_consts_in")
        state_in = s.sem("p2_state_in")
        tile_in = [s.sem(f"p2_tile_in{u}") for u in range(2)]
        pe_step = s.sem("p2_pe_step")
        dve_step = s.sem("p2_dve_step")
        act_step = s.sem("p2_act_step")
        pool_step = s.sem("p2_pool_step")
        s_turned_in = s.sem("p2_s_turned_in")
        s_turned_out = s.sem("p2_s_turned_out")
        s_state_pe = s.sem("p2_s_state_pe")
        s_state_dve = s.sem("p2_s_state_dve")
        s_state_kd = s.sem("p2_s_state_kd")
        out_stored = s.sem("p2_out_stored")
        state_stored = s.sem("p2_state_stored")

        PE = {n: i + 1 for i, n in enumerate(
            ["qkT_raw", "vraw", "rows", "turned", "grams"]
            + [x for l in range(LV) for x in (f"w{l}", f"t{l}")]
            + ["wT", "v_new", "out", "state", "oT"])}
        DV = {n: i + 1 for i, n in enumerate(
            ["gates", "qk_sums", "normed", "vb", "decay_in", "kbT", "grams"]
            + [x for l in range(LV) for x in (f"w{l}", f"t{l}")]
            + ["w_neg", "v_new", "state", "o_sums", "o_normed", "oT"])}
        AC = {n: i + 1 for i, n in enumerate(
            ["exps", "squares", "roots", "egrow", "decay", "o_squares", "o_root"])}
        PO = {n: i + 1 for i, n in enumerate(["kbg"] + [f"c{l}" for l in range(LV)] + ["gate"])}
        kinds = {"pe": (pe_step, PE), "dve": (dve_step, DV), "act": (act_step, AC), "pool": (pool_step, PO)}

        def at(eng, t, who, name):
            sem, names = kinds[who]
            eng.wait_ge(sem, len(names) * t + names[name])

        with nc.Block() as block:

            @block.sync
            def _(sp):
                def load(t, u):
                    sp.dma_start(y[:, u], d["yT"][t]).then_inc(tile_in[u], 16)
                    sp.dma_start(zb[:, u, 0:ZW], d["nat"][t, :, 0:ZW]).then_inc(tile_in[u], 16)
                    sp.dma_start(zb[:, u, ZW:ZW + 2 * H],
                                 d["nat"][t, :, ZW + LW + RO:NW]).then_inc(tile_in[u], 16)

                load(0, 0)
                load(1, 1)
                for dst, src in ((ident, d["ident"]), (tri2, d["tri"]), (same2, d["same"]), (levels, d["levels"]),
                                 (rows_b, d["batch_rows"]), (norm_bc, d["gdn_norm"].partition_broadcast(P)),
                                 (dt_bc, d["dt_bias"].partition_broadcast(P)),
                                 (ea_bc, d["a_log"].partition_broadcast(P))):
                    sp.dma_start(dst[:], src).then_inc(consts_in, 16)
                sp.dma_start(Ss[:], d["state"]).then_inc(state_in, 16)

                def step(t, u, r):
                    at(sp, t, "dve", "oT")
                    sp.dma_start(d["oT"][t, :, 0:H], oT[:]).then_inc(out_stored, 16)
                    load(t + 2, u)

                tiles(sp, TP - 2, step)
                step(TP - 2, 0, 0)
                at(sp, TP - 1, "dve", "oT")
                sp.dma_start(d["oT"][TP - 1, :, 0:H], oT[:]).then_inc(out_stored, 16)
                sp.dma_start(d["gdn_p"], S[:]).then_inc(state_stored, 16)
                at(sp, TP, "dve", "oT")
                sp.dma_start(d["oT"][TP, :, 0:H], oT[:]).then_inc(out_stored, 16)
                sp.dma_start(d["gdn_s"], Ss[:]).then_inc(state_stored, 16)
                sp.wait_ge(out_stored, 16 * NT)
                sp.wait_ge(state_stored, 32)

            @block.scalar
            def _(act):
                def step(t, u, r, sample=False):
                    act.wait_ge(tile_in[u], 48 * r + 48)
                    act.wait_ge(dve_step, len(DV) * t)
                    act.activation(ez[:].rearrange("p h n -> p (h n)"), zb[:, u, 0:ZW], ACT.Exp, scale=-1.0)
                    act.activation(t0[:], zb[:, u, ZW:ZW + H], ACT.Exp, scale=-1.0)
                    at(act, t, "dve", "gates")
                    act.activation(t1[:], t1[:], ACT.Exp)
                    act.drain()
                    act.activation(t1[:], t1[:], ACT.Ln, bias=1.0).then_inc(act_step, 1)
                    at(act, t, "pe", "qkT_raw")
                    for a in range(2):
                        i = act.activation(sq[:, a], bank[a][:], ACT.Square)
                    i.then_inc(act_step, 1)
                    at(act, t, "dve", "qk_sums")
                    act.activation(rn[:], rn[:], ACT.Sqrt, bias=eps[:]).then_inc(act_step, 1)
                    at(act, t, "pe", "rows")
                    act.activation(egrow[:], bank[3][:], ACT.Exp).then_inc(act_step, 1)
                    at(act, t, "dve", "decay_in")
                    act.activation(eg[:], gc[:, 0:H], ACT.Exp)
                    act.activation(ek[:], ek[:], ACT.Exp)
                    act.activation(dec[:], dec[:], ACT.Exp).then_inc(act_step, 1)
                    at(act, t, "pe", "out")
                    act.activation(sq[:, 0], bank[6][:], ACT.Square).then_inc(act_step, 1)
                    at(act, t, "dve", "o_sums")
                    act.activation(rn[:, 0:H], rn[:, 0:H], ACT.Sqrt, bias=eps[:], scale=1.0 / P).then_inc(act_step, 1)

                act.wait_ge(consts_in, 16 * 9)
                act.activation(ea_bc[:], ea_bc[:], ACT.Exp)
                act.drain()
                tiles(act, TP, step)
                step(TP, 0, TP // 2, True)

            @block.vector
            def _(dve):
                def step(t, u, r, sample=False):
                    m = 1 if sample else 0
                    nl = 3 if sample else LV
                    dve.wait_ge(tile_in[u], 48 * r + 48)
                    dve.tensor_tensor(g[:], zb[:, u, ZW + H:ZW + 2 * H], dt_bc[:], ALU.add)
                    dve.drain()
                    dve.tensor_scalar(t1[:], g[:], -1.0, None, ALU.mult)
                    dve.drain()
                    dve.tensor_tensor(t1[:], t1[:], g[:], ALU.min).then_inc(dve_step, 1)
                    dve.tensor_scalar(g[:], g[:], 0.0, None, ALU.max)
                    dve.drain()
                    at(dve, t, "act", "exps")
                    dve.tensor_tensor(g[:], g[:], t1[:], ALU.add)
                    dve.tensor_scalar(t0[:], t0[:], 1.0, None, ALU.add)
                    dve.tensor_scalar(ez[:], ez[:], 1.0, None, ALU.add)
                    dve.drain()
                    dve.scalar_tensor_tensor(g[:], g[:], -1.0, ea_bc[:], ALU.mult, ALU.mult)
                    dve.reciprocal(beta[:], t0[:])
                    at(dve, t, "act", "squares")
                    dve.tensor_reduce(rn[:], sq[:].rearrange("p a h n -> p (a h) n"), AX_X, ALU.add).then_inc(dve_step, 1)
                    dve.drain()
                    dve.tensor_copy(gb[:], bc(g[:].unsqueeze(2), W4))
                    dve.tensor_copy(bb[:], bc(beta[:].unsqueeze(2), W4))
                    at(dve, t, "act", "roots")
                    dve.reciprocal(rn[:], rn[:])
                    dve.drain()
                    dve.tensor_scalar(rn[:, 0:H], rn[:, 0:H], float(DK) ** -0.5, None, ALU.mult)
                    dve.drain()
                    dve.tensor_tensor(qn[:], bank[0][:], bc(rn[:, 0:H].unsqueeze(2), W4), ALU.mult)
                    dve.tensor_tensor(kn[:], bank[1][:], bc(rn[:, H:2 * H].unsqueeze(2), W4), ALU.mult).then_inc(dve_step, 1)
                    at(dve, t, "pe", "vraw")
                    dve.tensor_tensor(vb[:], bank[2][:], bc(beta[:].unsqueeze(2), W4), ALU.mult)
                    dve.reciprocal(ez[:], ez[:]).then_inc(dve_step, 1)
                    at(dve, t, "pe", "rows")
                    dve.tensor_copy(gc[:], bank[5][:, 0, 0:2 * H])
                    dve.drain()
                    dve.tensor_tensor(ek[:], gc[:, H:2 * H], gc[:, 0:H], ALU.subtract)
                    at(dve, t, "act", "egrow")
                    for h in range(H):
                        i = dve.tensor_scalar(dec[:, h], bank[3][:, h], gc[:, h:h + 1], 0.0, ALU.subtract, ALU.min)
                    i.then_inc(dve_step, 1)
                    at(dve, t, "pe", "turned")
                    dve.tensor_copy(qT[:], bank[6][:])
                    dve.tensor_copy(kT[:], bank[7][:])
                    dve.drain()
                    dve.tensor_tensor(kbT[:], kT[:], bank[4][:], ALU.mult)
                    dve.tensor_tensor(qgT[:], qT[:], egrow[:], ALU.mult).then_inc(dve_step, 1)
                    at(dve, t, "act", "decay")
                    dve.tensor_tensor(dec[:], dec[:], bc(tri2[:, m:m + 1], W4), ALU.mult)
                    dve.tensor_copy(T[:], bc(ident[:].unsqueeze(1), W4))
                    dve.tensor_copy(TT[:], bc(ident[:].unsqueeze(1), W4))
                    dve.drain()
                    at(dve, t, "pe", "grams")
                    dve.tensor_tensor(LT[:], bank[0][:], dec[:], ALU.mult)
                    dve.tensor_tensor(QKT[:], bank[1][:], dec[:], ALU.mult).then_inc(dve_step, 1)
                    for l in range(nl):
                        at(dve, t, "pe", f"w{l}")
                        dve.tensor_copy(Wm[:], bank[2][:]).then_inc(dve_step, 1)
                        at(dve, t, "pe", f"t{l}")
                        dve.tensor_tensor(T[:], T[:], bank[3][:], ALU.subtract)
                        dve.tensor_tensor(TT[:], TT[:], bank[4][:], ALU.subtract).then_inc(dve_step, 1)
                    if sample:
                        dve.drain()
                        dve.sem_inc(dve_step, 2 * (LV - nl))
                    at(dve, t, "pe", "wT")
                    dve.tensor_scalar(nwT[:], bank[5][:], -1.0, None, ALU.mult).then_inc(dve_step, 1)
                    if sample:
                        for n, b in ((0, 7), (1, 6)):
                            dve.wait_ge(s_turned_in, n + 1)
                            dve.tensor_copy(vnT[:], bank[b][:]).then_inc(s_turned_out, 1)
                            if n == 0:
                                at(dve, t, "pe", "v_new")
                                dve.tensor_copy(vn[:], bank[7][:]).then_inc(dve_step, 1)
                        for b in range(SB):
                            last = ST * (b + 1) - 1
                            dve.wait_ge(s_state_pe, b + 1)
                            for h in range(H):
                                i = dve.scalar_tensor_tensor(Ss[:, b, h], Ss[:, b, h], egrow[:, h, last:last + 1],
                                                             bank[b % 2][:, h], ALU.mult, ALU.add)
                            i.then_inc(s_state_dve, 1)
                        dve.drain()
                        dve.sem_inc(dve_step, 1)
                    else:
                        at(dve, t, "pe", "v_new")
                        dve.tensor_copy(vn[:], bank[7][:]).then_inc(dve_step, 1)
                        at(dve, t, "pe", "state")
                        for h in range(H):
                            i = dve.scalar_tensor_tensor(S[:, h], S[:, h], egrow[:, h, P - 1:P], bank[0][:, h],
                                                         ALU.mult, ALU.add)
                        i.then_inc(dve_step, 1)
                    at(dve, t, "act", "o_squares")
                    dve.tensor_reduce(rn[:, 0:H], sq[:, 0], AX_X, ALU.add).then_inc(dve_step, 1)
                    at(dve, t, "act", "o_root")
                    dve.reciprocal(rn[:, 0:H], rn[:, 0:H])
                    dve.drain()
                    dve.tensor_tensor(o1[:], bank[6][:], bc(rn[:, 0:H].unsqueeze(2), W4), ALU.mult)
                    dve.drain()
                    at(dve, t, "pool", "gate")
                    dve.tensor_tensor(o1[:], o1[:], ez[:], ALU.mult).then_inc(dve_step, 1)
                    at(dve, t, "pe", "oT")
                    dve.wait_ge(out_stored, 16 * t)
                    dve.tensor_copy(oT[:], bank[1][:]).then_inc(dve_step, 1)

                dve.memset(eps[:], EPS)
                dve.memset(S[:], 0.0)
                dve.drain()
                dve.sem_inc(consts_in, 16)
                dve.wait_ge(consts_in, 16 * 9)
                dve.wait_ge(state_in, 16)
                tiles(dve, TP, step)
                step(TP, 0, TP // 2, True)

            @block.gpsimd
            def _(pool):
                def step(t, u, r, sample=False):
                    m = 1 if sample else 0
                    nl = 3 if sample else LV
                    at(pool, t, "act", "decay")
                    at(pool, t, "dve", "vb")
                    pool.tensor_tensor(bg[:], beta[:], eg[:], ALU.mult)
                    pool.drain()
                    pool.tensor_tensor(kbg[:], kn[:], bc(bg[:].unsqueeze(2), W4), ALU.mult)
                    pool.tensor_tensor(kd[:], kn[:], bc(ek[:].unsqueeze(2), W4), ALU.mult).then_inc(pool_step, 1)
                    at(pool, t, "dve", "grams")
                    for l in range(nl):
                        if l >= 2:
                            at(pool, t, "pe", f"w{l - 2}")
                        pool.tensor_tensor(CT[:, l % 2], LT[:], bc(levels[:, l:l + 1], W4), ALU.mult).then_inc(pool_step, 1)
                    if sample:
                        pool.drain()
                        pool.sem_inc(pool_step, LV - nl)
                        for b in range(SB):
                            if b:
                                pool.wait_ge(s_state_pe, b)
                            else:
                                pool.drain()
                            pool.tensor_scalar(kdb[:], kd[:], rows_b[:, b:b + 1], None, ALU.mult).then_inc(s_state_kd, 1)
                    pool.tensor_tensor(ez[:], ez[:], bc(norm_bc[:].unsqueeze(1), W4), ALU.mult)
                    pool.drain()
                    pool.tensor_tensor(ez[:].rearrange("p h n -> p (h n)"), ez[:].rearrange("p h n -> p (h n)"),
                                       zb[:, u, 0:ZW], ALU.mult).then_inc(pool_step, 1)

                pool.wait_ge(consts_in, 16 * 9)
                tiles(pool, TP, step)
                step(TP, 0, TP // 2, True)

            @block.tensor
            def _(pe):
                def heads(dst, lhs, rhs, **k):
                    for h in range(H):
                        i = pe.matmul(dst(h), lhs(h), rhs(h), **({"start": True, "stop": True} | k))
                    return i

                def step(t, u, r, sample=False):
                    m = 1 if sample else 0
                    nl = 3 if sample else LV
                    one = ident[:]
                    pe.wait_ge(tile_in[u], 48 * r + 48)
                    pe.wait_ge(dve_step, len(DV) * t)
                    for a in range(3):
                        for h in range(H):
                            i = pe.transpose(bank[a][:, h], y[:, u, H * a + h], one)
                        if a:
                            i.then_inc(pe_step, 1)
                    at(pe, t, "dve", "normed")
                    heads(lambda h: bank[3][:, h], lambda h: gb[:, h], lambda h: tri2[:, m])
                    heads(lambda h: bank[4][:, h], lambda h: bb[:, h], lambda h: one)
                    pe.matmul(bank[5][:, 0, 0:H], tri2[:, m], g[:], start=True, stop=True)
                    pe.matmul(bank[5][:, 0, H:2 * H], same2[:, m], g[:], start=True, stop=True).then_inc(pe_step, 1)
                    for b, src in ((6, qn), (7, kn)):
                        for h in range(H):
                            i = pe.transpose(bank[b][:, h], src[:, h], one)
                    i.then_inc(pe_step, 1)
                    at(pe, t, "dve", "kbT")
                    heads(lambda h: bank[0][:, h], lambda h: kT[:, h], lambda h: kbT[:, h])
                    heads(lambda h: bank[1][:, h], lambda h: kT[:, h], lambda h: qT[:, h]).then_inc(pe_step, 1)
                    for l in range(nl):
                        at(pe, t, "dve", f"t{l - 1}" if l else "grams")
                        at(pe, t, "pool", f"c{l}")
                        heads(lambda h: bank[2][:, h], lambda h: CT[:, l % 2, h], lambda h: T[:, h]).then_inc(pe_step, 1)
                        at(pe, t, "dve", f"w{l}")
                        heads(lambda h: bank[3][:, h], lambda h: TT[:, h], lambda h: Wm[:, h])
                        heads(lambda h: bank[4][:, h], lambda h: Wm[:, h], lambda h: TT[:, h]).then_inc(pe_step, 1)
                    if sample:
                        pe.drain()
                        pe.sem_inc(pe_step, 2 * (LV - nl))
                    at(pe, t, "pool", "kbg")
                    at(pe, t, "dve", f"t{LV - 1}")
                    heads(lambda h: bank[5][:, h], lambda h: kbg[:, h], lambda h: TT[:, h]).then_inc(pe_step, 1)
                    at(pe, t, "dve", "w_neg")
                    if sample:
                        def turned(n, b, lhs, rhs, by_batch):
                            for h in range(H):
                                pe.matmul(bank[b][:, h], lhs(h), rhs(h), start=True, stop=False, skip_group_check=True)
                                for k in range(SB):
                                    cols = slice(ST * k, ST * k + ST)
                                    i = pe.matmul(bank[b][:, h, cols], Ss[:, k, h], by_batch[:, h, cols],
                                                  start=False, stop=(k == SB - 1), skip_group_check=True)
                            i.then_inc(s_turned_in, 1)
                            pe.wait_ge(s_turned_out, n + 1)
                            for h in range(H):
                                i = pe.transpose(bank[b][:, h], vnT[:, h], one)
                            i.then_inc(pe_step, 1)

                        turned(0, 7, lambda h: vb[:, h], lambda h: TT[:, h], nwT)
                        at(pe, t, "dve", "v_new")
                        turned(1, 6, lambda h: vn[:, h], lambda h: QKT[:, h], qgT)
                        for b in range(SB):
                            pe.wait_ge(s_state_kd, b + 1)
                            if b >= 2:
                                pe.wait_ge(s_state_dve, b - 1)
                            heads(lambda h: bank[b % 2][:, h], lambda h: kdb[:, h], lambda h: vn[:, h]).then_inc(s_state_pe, 1)
                        pe.drain()
                        pe.sem_inc(pe_step, 1)
                    else:
                        for h in range(H):
                            pe.matmul(bank[7][:, h], TT[:, h], vb[:, h], start=True, stop=False)
                            i = pe.matmul(bank[7][:, h], nwT[:, h], S[:, h], start=False, stop=True)
                        i.then_inc(pe_step, 1)
                        at(pe, t, "dve", "v_new")
                        for h in range(H):
                            pe.matmul(bank[6][:, h], qgT[:, h], S[:, h], start=True, stop=False)
                            i = pe.matmul(bank[6][:, h], QKT[:, h], vn[:, h], start=False, stop=True)
                        i.then_inc(pe_step, 1)
                        heads(lambda h: bank[0][:, h], lambda h: kd[:, h], lambda h: vn[:, h]).then_inc(pe_step, 1)
                    at(pe, t, "dve", "o_normed")
                    for h in range(H):
                        i = pe.transpose(bank[1][:, h], o1[:, h], one)
                    i.then_inc(pe_step, 1)

                pe.wait_ge(consts_in, 16 * 9)
                tiles(pe, TP, step)
                step(TP, 0, TP // 2, True)


def phase_latents(nc, d, m):
    with ExitStack() as st, Semaphores(nc) as s:
        c = Ctx(nc, st)
        KT, KR, V, QT, QR, ident = m["KT"], m["KR"], m["V"], m["QT"], m["QR"], m["ident"]
        w_uq = c.sb("p3_w_uq", [P, 2, H * (DK + RO)])
        w_uk = c.sb("p3_w_uk", [P, H, R])
        gq = c.sb("p3_gq", [P, R])
        gkv = c.sb("p3_gkv", [P, R])
        eps = c.sb("p3_eps", [P, 1])
        cs = c.sb("p3_cs", [P, 2, 2, RO // 2])
        lt = c.sb("p3_lt", [P, 2, LW + RO])
        sq = c.sb("p3_sq", [P, 2, R])
        rn = c.sb("p3_rn", [P, 2])
        cq = c.sb("p3_cq", [P, R])
        ckv = c.sb("p3_ckv", [P, R])
        kr = c.sb("p3_kr", [P, 2, RO // 2])
        tk = c.sb("p3_tk", [P, 2, RO // 2])
        cqT = c.sb("p3_cqT", [P, 2, P])
        qnT = c.sb("p3_qnT", [P, H, P])
        qr = c.sb("p3_qr", [P, H, 2, RO // 2])
        tq = c.sb("p3_tq", [P, H, 2, RO // 2])
        bank = [c.ps(f"p3_bank{n}", [P, 4, P]) for n in range(7)]

        consts_in = s.sem("p3_consts_in")
        tile_in = [s.sem(f"p3_tile_in{u}") for u in range(2)]
        rooted = s.sem("p3_rooted")
        normed = s.sem("p3_normed")
        turned = s.sem("p3_turned")
        copied = s.sem("p3_copied")
        q_done = s.sem("p3_q_done")
        qnT_ready = s.sem("p3_qnT_ready")
        qr_ready = s.sem("p3_qr_ready")
        lat_done = s.sem("p3_lat_done")
        lat_out = s.sem("p3_lat_out")
        stored = s.sem("p3_stored")
        half = RO // 2
        w_rope = w_uq[:].rearrange("p k (h n) -> p k h n", h=H)[:, :, :, DK:DK + RO]

        with nc.Block() as block:

            @block.sync
            def _(sp):
                def load(t, u):
                    sp.dma_start(lt[:, u], d["nat"][t, :, ZW:ZW + LW + RO]).then_inc(tile_in[u], 16)
                    sp.dma_start(cs[:, u, 0], d["cos"][t]).then_inc(tile_in[u], 16)
                    sp.dma_start(cs[:, u, 1], d["sin"][t]).then_inc(tile_in[u], 16)

                load(0, 0)
                load(1, 1)
                for dst, src in ((ident, d["ident"]), (w_uq, d["w_uq"]), (w_uk, d["w_uk"]),
                                 (gq, d["g_q"].partition_broadcast(P)), (gkv, d["g_kv"].partition_broadcast(P))):
                    sp.dma_start(dst[:], src).then_inc(consts_in, 16)

                def step(t, u, r, more=True):
                    sp.wait_ge(normed, t + 1)
                    sp.dma_start(d["ckv"][t], ckv[:]).then_inc(stored, 16)
                    sp.dma_start(d["krope"][t], kr[:].rearrange("p a n -> p (a n)")).then_inc(stored, 16)
                    if more:
                        sp.wait_ge(qr_ready, t + 1)
                        load(t + 2, u)

                tiles(sp, TP - 2, step)
                step(TP - 2, 0, 0)
                step(TP - 1, 1, 0, False)
                step(TP, 0, 0, False)
                sp.wait_ge(stored, 32 * NT)

            @block.scalar
            def _(act):
                def step(t, u, r):
                    act.wait_ge(tile_in[u], 48 * r + 48)
                    act.wait_ge(normed, t)
                    for a in range(2):
                        act.activation(sq[:, a], lt[:, u, R * a:R * a + R], ACT.Square, accum_out=rn[:, a:a + 1])
                    act.drain()
                    act.activation(rn[:], rn[:], ACT.Sqrt, bias=eps[:], scale=1.0 / R).then_inc(rooted, 1)
                    act.wait_ge(turned, t + 1)
                    act.copy(cqT[:], bank[0][:, 0:2])
                    act.copy(KT[:, :, bass.ds(t * P, P)], bank[0][:, 2:4])
                    act.copy(KR[:, bass.ds(t * P, P)], bank[1][0:RO, 0]).then_inc(copied, 1)
                    act.wait_ge(q_done, t + 1)
                    act.copy(qnT[:], bank[2][:]).then_inc(qnT_ready, 1)
                    act.wait_ge(lat_done, t + 1)
                    for a in range(2):
                        act.copy(QT[:, a, :, bass.ds(t * P, P)], bank[4 + a][:])
                    act.copy(QR[:, :, bass.ds(t * P, P)], bank[6][0:RO]).then_inc(lat_out, 1)

                act.wait_ge(consts_in, 16 * 6)
                tiles(act, TP, step)
                step(TP, 0, TP // 2)

            @block.vector
            def _(dve):
                def step(t, u, r):
                    cos, sin = cs[:, u, 0:1], cs[:, u, 1:2]

                    def rope(out, tmp, x, wide):
                        dve.tensor_tensor(out, x, wide(cos, 2), ALU.mult)
                        dve.tensor_tensor(tmp[0], x[..., 1:2, :], wide(sin, 1), ALU.mult)
                        dve.tensor_tensor(tmp[1], x[..., 0:1, :], wide(sin, 1), ALU.mult)
                        dve.drain()
                        dve.tensor_tensor(out[..., 0:1, :], out[..., 0:1, :], tmp[0], ALU.subtract)
                        return dve.tensor_tensor(out[..., 1:2, :], out[..., 1:2, :], tmp[1], ALU.add)

                    dve.wait_ge(rooted, t + 1)
                    dve.reciprocal(rn[:], rn[:])
                    dve.drain()
                    dve.wait_ge(turned, t)
                    dve.wait_ge(stored, 32 * t)
                    dve.scalar_tensor_tensor(cq[:], lt[:, u, 0:R], rn[:, 0:1], gq[:], ALU.mult, ALU.mult)
                    dve.scalar_tensor_tensor(ckv[:], lt[:, u, R:2 * R], rn[:, 1:2], gkv[:], ALU.mult, ALU.mult)
                    rope(kr[:], (tk[:, 0:1], tk[:, 1:2]), lt[:, u, LW:LW + RO].rearrange("p (a n) -> p a n", a=2),
                         lambda a, k: bc(a, [P, k, half])).then_inc(normed, 1)
                    dve.drain()
                    dve.tensor_copy(V[:, t, :], ckv[:])
                    dve.wait_ge(q_done, t + 1)
                    x = bank[3][:, 0:2].rearrange("p a n -> p (a n)").rearrange("p (h a n) -> p h a n", h=H, a=2)
                    rope(qr[:], (tq[:, :, 0:1], tq[:, :, 1:2]), x,
                         lambda a, k: bc(a.unsqueeze(1), [P, H, k, half])).then_inc(qr_ready, 1)

                dve.memset(eps[:], EPS)
                dve.drain()
                dve.sem_inc(consts_in, 16)
                dve.wait_ge(consts_in, 16 * 6)
                tiles(dve, TP, step)
                step(TP, 0, TP // 2)

            @block.tensor
            def _(pe):
                def step(t, u, r):
                    pe.wait_ge(normed, t + 1)
                    pe.wait_ge(lat_out, t)
                    for a in range(2):
                        pe.transpose(bank[0][:, a], cq[:, a * P:(a + 1) * P], ident[:])
                    for a in range(2):
                        pe.transpose(bank[0][:, 2 + a], ckv[:, a * P:(a + 1) * P], ident[:])
                    pe.transpose(bank[1][0:RO, 0], kr[:].rearrange("p a n -> p (a n)"), ident[:]).then_inc(turned, 1)
                    pe.wait_ge(copied, t + 1)
                    for h in range(H):
                        for k in range(2):
                            pe.matmul(bank[2][:, h], w_uq[:, k, h * (DK + RO):h * (DK + RO) + DK], cqT[:, k],
                                      start=(k == 0), stop=(k == 1))
                    for k in range(2):
                        i = pe.matmul(bank[3][:, 0:2].rearrange("p a n -> p (a n)").rearrange("p (h n) -> p h n", h=H),
                                      cqT[:, k], w_rope[:, k], start=(k == 0), stop=(k == 1))
                    i.then_inc(q_done, 1)
                    pe.wait_ge(qnT_ready, t + 1)
                    pe.wait_ge(qr_ready, t + 1)
                    for a in range(2):
                        for h in range(H):
                            pe.matmul(bank[4 + a][:, h], w_uk[:, h, a * P:(a + 1) * P], qnT[:, h], start=True, stop=True)
                    for h in range(H):
                        i = pe.transpose(bank[6][0:RO, h], qr[:, h].rearrange("p a n -> p (a n)"), ident[:])
                    i.then_inc(lat_done, 1)

                pe.wait_ge(consts_in, 16 * 6)
                tiles(pe, TP, step)
                step(TP, 0, TP // 2)


def phase_prompt_attention(nc, d, m):
    with ExitStack() as st, Semaphores(nc) as s:
        c = Ctx(nc, st)
        KT, KR, V, QT, QR, ident = m["KT"], m["KR"], m["V"], m["QT"], m["QR"], m["ident"]
        w_uv = m["w_uv"]
        causal = c.sb("p4_causal", [P, P])
        mx = c.sb("p4_mx", [P, 2])
        rs = c.sb("p4_rs", [P, 2])
        pb = c.sb("p4_pb", [P, 2, TP * P])
        dg = c.sb("p4_dg", [P, 2, P])
        pts = c.sb("p4_pts", [P, 2, TP, P])
        ols = c.sb("p4_ols", [P, 2, 2, P])
        om = c.sb("p4_om", [P, 2, H, P])
        psS = c.ps("p4_psS", [P, 2, TP * P])
        psT = c.ps("p4_psT", [P, TP, P])
        psL = c.ps("p4_psL", [P, 4, P])
        psO = c.ps("p4_psO", [P, 4, P])

        consts_in = s.sem("p4_consts_in")
        scored = s.sem("p4_scored")
        max_ready = s.sem("p4_max_ready")
        p_ready = s.sem("p4_p_ready")
        diag_ready = s.sem("p4_diag_ready")
        turned = s.sem("p4_turned")
        pt_low = s.sem("p4_pt_low")
        pt_high = s.sem("p4_pt_high")
        lat_done = s.sem("p4_lat_done")
        lat_out = s.sem("p4_lat_out")
        o_done = s.sem("p4_o_done")
        o_out = s.sem("p4_o_out")
        stored = [s.sem(f"p4_stored{u}") for u in range(2)]
        N = TP * H

        def high(n):
            return sum(1 for k in range(n + 1) if k // H >= 4)

        def each(m_, *parts):
            for lag, f in parts:
                if 0 <= m_ - lag < N:
                    f(m_ - lag)

        with nc.Block() as block:

            @block.sync
            def _(sp):
                sp.dma_start(causal[:], d["causal"]).then_inc(consts_in, 16)
                sp.dma_start(w_uv[:], d["w_uv"]).then_inc(consts_in, 16)
                for t in range(TP):
                    sp.wait_ge(o_out, H * (t + 1))
                    sp.dma_start(d["oT"][t, :, H:2 * H], om[:, t % 2]).then_inc(stored[t % 2], 16)
                for u in range(2):
                    sp.wait_ge(stored[u], 16 * TP // 2)

            @block.tensor
            def _(pe):
                def scores(n):
                    t, h = n // H, n % H
                    if n >= 2:
                        pe.wait_ge(p_ready, n - 1)
                    q = slice(t * P, (t + 1) * P)
                    for k in range(0, (t + 1) * P, 512):
                        w = min(512, (t + 1) * P - k)
                        out = psS[:, n % 2, k:k + w]
                        pe.matmul(out, QT[:, 0, h, q], KT[:, 0, k:k + w], start=True, stop=False)
                        pe.matmul(out, QT[:, 1, h, q], KT[:, 1, k:k + w], start=False, stop=False)
                        i = pe.matmul(out, QR[:, h, q], KR[:, k:k + w], start=False, stop=True)
                    i.then_inc(scored, 1)

                def turn(n):
                    pe.wait_ge(diag_ready, n + 1)
                    if n >= 1:
                        pe.wait_ge(pt_low, n)
                        if high(n - 1):
                            pe.wait_ge(pt_high, high(n - 1))
                    for b in range(n // H + 1):
                        i = pe.matmul(psT[:, b], pb[:, n % 2, b * P:(b + 1) * P], dg[:, n % 2], start=True, stop=True)
                    i.then_inc(turned, 1)

                def latent(n):
                    pe.wait_ge(pt_low, n + 1)
                    if high(n):
                        pe.wait_ge(pt_high, high(n))
                    if n >= 1:
                        pe.wait_ge(lat_out, n)
                    for a in range(2):
                        for b in range(n // H + 1):
                            i = pe.matmul(psL[:, a], V[:, b, a * P:(a + 1) * P], pts[:, n % 2, b],
                                          start=(b == 0), stop=(b == n // H))
                    i.then_inc(lat_done, 1)

                def out(n):
                    h = n % H
                    pe.wait_ge(lat_out, n + 1)
                    if n >= 1:
                        pe.wait_ge(o_out, n)
                    for a in range(2):
                        i = pe.matmul(psO[:, 0], w_uv[:, a, h * DK:(h + 1) * DK], ols[:, n % 2, a],
                                      start=(a == 0), stop=(a == 1))
                    i.then_inc(o_done, 1)

                pe.wait_ge(consts_in, 32)
                for k in range(N + 3):
                    each(k, (0, scores), (1, turn), (2, latent), (3, out))

            @block.vector
            def _(dve):
                def diag(n):
                    dve.wait_ge(p_ready, n + 1)
                    dve.reciprocal(rs[:, n % 2:n % 2 + 1], rs[:, n % 2:n % 2 + 1])
                    dve.drain()
                    if n >= 2:
                        dve.wait_ge(turned, n - 1)
                    dve.tensor_scalar(dg[:, n % 2], ident[:], rs[:, n % 2:n % 2 + 1], None, ALU.mult).then_inc(diag_ready, 1)

                def row_max(n):
                    t, u = n // H, n % 2
                    dve.wait_ge(scored, n + 1)
                    last = psS[:, u, t * P:(t + 1) * P]
                    dve.tensor_tensor(last, last, causal[:], ALU.add)
                    dve.drain()
                    dve.tensor_reduce(mx[:, u:u + 1], psS[:, u, 0:(t + 1) * P], AX_X, ALU.max)
                    dve.drain()
                    dve.tensor_scalar(mx[:, u:u + 1], mx[:, u:u + 1], -MLA_SCALE, None, ALU.mult).then_inc(max_ready, 1)

                def low(n):
                    w = min(4, n // H + 1)
                    dve.wait_ge(turned, n + 1)
                    if n >= 2:
                        dve.wait_ge(lat_done, n - 1)
                    dve.tensor_copy(pts[:, n % 2, 0:w], psT[:, 0:w]).then_inc(pt_low, 1)

                def lat(n):
                    dve.wait_ge(lat_done, n + 1)
                    if n >= 2:
                        dve.wait_ge(o_done, n - 1)
                    dve.tensor_copy(ols[:, n % 2], psL[:, 0:2]).then_inc(lat_out, 1)

                dve.wait_ge(consts_in, 32)
                for k in range(N + 3):
                    each(k, (1, diag), (0, row_max), (1, low), (2, lat))

            @block.scalar
            def _(act):
                def exp(n):
                    t, u = n // H, n % 2
                    act.wait_ge(max_ready, n + 1)
                    if n >= 2:
                        act.wait_ge(turned, n - 1)
                    act.activation(pb[:, u, 0:(t + 1) * P], psS[:, u, 0:(t + 1) * P], ACT.Exp, bias=mx[:, u:u + 1],
                                   scale=MLA_SCALE, accum_out=rs[:, u:u + 1]).then_inc(p_ready, 1)

                def high_blocks(n):
                    t = n // H
                    if t < 4:
                        return
                    act.wait_ge(turned, n + 1)
                    act.wait_ge(lat_done, n - 1)
                    act.copy(pts[:, n % 2, 4:t + 1], psT[:, 4:t + 1]).then_inc(pt_high, 1)

                def out(n):
                    t, h = n // H, n % H
                    act.wait_ge(o_done, n + 1)
                    if t >= 2 and h == 0:
                        act.wait_ge(stored[t % 2], 16 * (t // 2))
                    act.copy(om[:, t % 2, h], psO[:, 0]).then_inc(o_out, 1)

                for k in range(N + 3):
                    each(k, (0, exp), (1, high_blocks), (3, out))


def mla_tensors(c):
    return {
        "KT": c.sb("mla_KT", [P, 2, NT * P]), "KR": c.sb("mla_KR", [RO, NT * P]), "V": c.sb("mla_V", [P, NT, R]),
        "QT": c.sb("mla_QT", [P, 2, H, NT * P]), "QR": c.sb("mla_QR", [RO, H, NT * P]),
        "ident": c.sb("mla_ident", [P, P]), "w_uv": c.sb("mla_w_uv", [P, 2, H * DK]),
    }


def phase_sample_attention(nc, d, m):
    G, J, PC = 2, 4, 4
    NC = NPAGE // PC
    CK = PC * PAGE
    HT = H * ST
    with ExitStack() as st, Semaphores(nc) as s:
        c = Ctx(nc, st)
        KT, KR, V, QT, QR, ident, w_uv = (m[n] for n in ("KT", "KR", "V", "QT", "QR", "ident", "w_uv"))
        n_pool = d["cache"].shape[0]
        KW = R + PAGE // 2
        pages = c.sb("p5_pages", [1, G * NC * J * PC], I32)
        mask = c.sb("p5_mask", [P, G, SR])
        ring = c.sb("p5_ring", [P, 2, J * PC * KW])
        kt = [ring[:, u].rearrange("p (j q w) -> p j q w", j=J, q=PC) for u in range(2)]
        vt = [ring[:, u, 0:J * PC * R].rearrange("p (j q w) -> p j q w", j=J, q=PC) for u in range(2)]
        S = c.sb("p5_S", [P, NC * CK + SR])
        qg = c.sb("p5_qg", [P, G, 2, J, HT])
        qr = c.sb("p5_qr", [P, G, 2, J, HT])
        mxc = c.sb("p5_mxc", [P, NC + 1])
        nm = c.sb("p5_nm", [P, 1])
        sums = c.sb("p5_sums", [P, NC + 1])
        den = c.sb("p5_den", [P, 1])
        pb = c.sb("p5_pb", [P, 2, CK])
        pts = c.sb("p5_pts", [P, 2, PC, P])
        acc = c.sb("p5_acc", [P, R])
        ols = c.sb("p5_ols", [P, 2, P])
        om = c.sb("p5_om", [P, H, P])
        psS = c.ps("p5_psS", [P, 2, 512])
        psT = c.ps("p5_psT", [P, 2, PC, P])
        psV = c.ps("p5_psV", [P, 2, 512])
        psO = c.ps("p5_psO", [P, H, P])

        consts_in = s.sem("p5_consts_in")
        pages_in = s.sem("p5_pages_in")
        q_ready = s.sem("p5_q_ready")
        chunk_in = [s.sem(f"p5_chunk_in{u}") for u in range(2)]
        chunk_used = s.sem("p5_chunk_used")
        scored = s.sem("p5_scored")
        kept = s.sem("p5_kept")
        max_ready = s.sem("p5_max_ready")
        p_ready = s.sem("p5_p_ready")
        turned = s.sem("p5_turned")
        pt_ready = s.sem("p5_pt_ready")
        pv_done = s.sem("p5_pv_done")
        added = s.sem("p5_added")
        acc_ready = s.sem("p5_acc_ready")
        acc_turned = s.sem("p5_acc_turned")
        ols_ready = s.sem("p5_ols_ready")
        o_done = s.sem("p5_o_done")
        o_out = s.sem("p5_o_out")
        stored = s.sem("p5_stored")
        KS = NC + 1

        def chunks(eng, n, body, base=0):
            with eng.Fori(0, n // 2) as r:
                for u in range(2):
                    body(r * 2 + (u + base), u, r + base // 2)

        with nc.Block() as block:

            @block.sync
            def _(sp):
                sp.dma_start(pages[:], d["pages"]).then_inc(pages_in, 16)
                sp.dma_start(mask[:], d["new_mask"]).then_inc(consts_in, 16)
                sp.wait_ge(pages_in, 16)

                def load(g, second, c_, u, seq):
                    for j in range(J):
                        for q in range(PC):
                            page = sp.value_load(pages[0:1, bass.ds((c_ + NC * g) * (J * PC) + (j * PC + q), 1)],
                                                 min_val=0, max_val=n_pool - 1)
                            if second:
                                sp.dma_start(vt[u][:, j, q], d["cache"][page]).then_inc(chunk_in[u], 16)
                            else:
                                sp.dma_start(kt[u][:, j, q], d["cacheT"][page]).then_inc(chunk_in[u], 16)

                for g in range(G):
                    for second in range(2):
                        base = 0
                        if g == 0 and second == 0:
                            load(0, 0, 0, 0, 0)
                            load(0, 0, 1, 1, 1)
                            base = 2

                        def step(c_, u, r):
                            sp.wait_ge(chunk_used, c_ + (NC * (2 * g + second) - 1))
                            load(g, second, c_, u, None)

                        chunks(sp, NC - base, step, base)
                sp.wait_ge(o_out, G)
                sp.dma_start(d["oT"][TP, :, H:2 * H], om[:]).then_inc(stored, 16)
                sp.wait_ge(stored, 16)

            @block.tensor
            def _(pe):
                pe.wait_ge(q_ready, 1)
                for g in range(G):
                    def score(c_, u, r):
                        pe.wait_ge(chunk_in[u], (r + (NC * g + 1)) * (16 * J * PC))
                        pe.wait_ge(kept, c_ + KS * g)
                        for a in range(2):
                            for j in range(J):
                                out = psS[HT * j:HT * (j + 1), u].rearrange("p (q w) -> p q w", q=PC)
                                pe.matmul(out, qg[:, g, a, j], kt[u][:, j, :, a * P:(a + 1) * P],
                                          start=(a == 0), stop=False, skip_group_check=True)
                        for a in range(2):
                            for j in range(J):
                                out = psS[HT * j:HT * (j + 1), u].rearrange("p (q w) -> p q w", q=PC)
                                half = slice(a * PAGE // 2, (a + 1) * PAGE // 2)
                                i = pe.matmul(out[:, :, half], qr[:, g, a, j], kt[u][:, j, :, R:KW],
                                              start=False, stop=True, skip_group_check=True)
                        i.then_inc(scored, 1)
                        pe.drain()
                        pe.sem_inc(chunk_used, 1)

                    chunks(pe, NC, score)
                    pe.wait_ge(kept, NC + KS * g)
                    new = slice(TP * P, TP * P + SR)
                    for j in range(J):
                        out = psS[HT * j:HT * (j + 1), 0, 0:SR]
                        pe.matmul(out, qg[:, g, 0, j], KT[:, 0, new], start=True, stop=False, skip_group_check=True)
                        pe.matmul(out, qg[:, g, 1, j], KT[:, 1, new], start=False, stop=False, skip_group_check=True)
                        i = pe.matmul(out, qr[0:RO, g, 0, j], KR[:, new], start=False, stop=True, skip_group_check=True)
                    i.then_inc(scored, 1)

                    def values(c_, u, r):
                        pe.wait_ge(p_ready, c_ + (KS * g + 1))
                        pe.wait_ge(pt_ready, c_ + KS * g)
                        for q in range(PC):
                            i = pe.transpose(psT[:, u, q], pb[:, u, q * P:(q + 1) * P], ident[:])
                        i.then_inc(turned, 1)
                        pe.wait_ge(pt_ready, c_ + (KS * g + 1))
                        pe.wait_ge(chunk_in[u], (r + (NC * g + NC // 2 + 1)) * (16 * J * PC))
                        pe.wait_ge(added, c_ + KS * g)
                        for q in range(PC):
                            for j in range(J):
                                i = pe.matmul(psV[HT * j:HT * (j + 1), u, 0:R], pts[:, u, q, HT * j:HT * (j + 1)],
                                              vt[u][:, j, q], start=(q == 0), stop=(q == PC - 1), skip_group_check=True)
                        i.then_inc(pv_done, 1)
                        pe.drain()
                        pe.sem_inc(chunk_used, 1)

                    chunks(pe, NC, values)
                    n = NC + KS * g
                    pe.wait_ge(p_ready, n + 1)
                    pe.wait_ge(pt_ready, n)
                    pe.transpose(psT[0:SR, 0, 0], pb[:, 0, 0:SR], ident[:]).then_inc(turned, 1)
                    pe.wait_ge(pt_ready, n + 1)
                    pe.wait_ge(added, n)
                    for j in range(J):
                        i = pe.matmul(psV[HT * j:HT * (j + 1), 0, 0:R], pts[0:SR, 0, 0, HT * j:HT * (j + 1)],
                                      V[0:SR, TP], start=True, stop=True, skip_group_check=True)
                    i.then_inc(pv_done, 1)
                    pe.wait_ge(acc_ready, g + 1)
                    for a in range(2):
                        i = pe.transpose(psT[:, 1, a], acc[:, a * P:(a + 1) * P], ident[:])
                    i.then_inc(acc_turned, 1)
                    pe.wait_ge(ols_ready, g + 1)
                    for h in range(H):
                        for a in range(2):
                            i = pe.matmul(psO[:, h, 0:J * ST].rearrange("p (j t) -> p j t", j=J),
                                          w_uv[:, a, h * DK:(h + 1) * DK],
                                          ols[:, a].rearrange("p (j h t) -> p j h t", j=J, h=H)[:, :, h],
                                          start=(a == 0), stop=(a == 1))
                    i.then_inc(o_done, 1)

            @block.vector
            def _(dve):
                dve.memset(qr[:], 0.0)
                dve.memset(om[:], 0.0)
                dve.drain()
                for g in range(G):
                    for j in range(J):
                        at = TP * P + ST * (J * g + j)
                        for a in range(2):
                            dve.tensor_copy(qg[:, g, a, j].rearrange("p (h t) -> p h t", h=H), QT[:, a, :, at:at + ST])
                            i = dve.tensor_copy(qr[RO * a:RO * (a + 1), g, a, j].rearrange("p (h t) -> p h t", h=H),
                                                QR[:, :, at:at + ST])
                i.then_inc(q_ready, 1)
                dve.wait_ge(consts_in, 16)
                for g in range(G):
                    def keep(c_, u, r):
                        dve.wait_ge(scored, c_ + (KS * g + 1))
                        dve.tensor_scalar(S[:, bass.ds(c_ * CK, CK)], psS[:, u], 1.0, NEG, ALU.mult, ALU.max,
                                          accum_out=mxc[:, bass.ds(c_, 1)]).then_inc(kept, 1)

                    if g:
                        dve.wait_ge(p_ready, KS * g)
                    chunks(dve, NC, keep)
                    dve.wait_ge(scored, NC + KS * g + 1)
                    tail = S[:, NC * CK:NC * CK + SR]
                    dve.tensor_tensor(tail, psS[:, 0, 0:SR], mask[:, g], ALU.add)
                    dve.drain()
                    dve.tensor_reduce(mxc[:, NC:NC + 1], tail, AX_X, ALU.max).then_inc(kept, 1)
                    dve.drain()
                    dve.tensor_reduce(nm[:], mxc[:], AX_X, ALU.max)
                    dve.drain()
                    dve.tensor_scalar(nm[:], nm[:], -MLA_SCALE, None, ALU.mult).then_inc(max_ready, 1)
                    if g:
                        dve.wait_ge(acc_turned, g)
                    dve.memset(acc[:], 0.0)

                    def add(c_, u, r):
                        dve.wait_ge(turned, c_ + (KS * g + 1))
                        dve.tensor_copy(pts[:, u], psT[:, u]).then_inc(pt_ready, 1)
                        dve.wait_ge(pv_done, c_ + (KS * g + 1))
                        dve.tensor_tensor(acc[:], acc[:], psV[:, u, 0:R], ALU.add).then_inc(added, 1)

                    chunks(dve, NC, add)
                    n = NC + KS * g
                    dve.wait_ge(turned, n + 1)
                    dve.tensor_copy(pts[0:SR, 0, 0], psT[0:SR, 0, 0]).then_inc(pt_ready, 1)
                    dve.tensor_reduce(den[:], sums[:], AX_X, ALU.add)
                    dve.drain()
                    dve.reciprocal(den[:], den[:])
                    dve.wait_ge(pv_done, n + 1)
                    dve.tensor_tensor(acc[:], acc[:], psV[:, 0, 0:R], ALU.add).then_inc(added, 1)
                    dve.drain()
                    dve.tensor_scalar(acc[:], acc[:], den[:], None, ALU.mult).then_inc(acc_ready, 1)
                    dve.wait_ge(acc_turned, g + 1)
                    dve.tensor_copy(ols[:], psT[:, 1, 0:2]).then_inc(ols_ready, 1)
                    dve.wait_ge(o_done, g + 1)
                    dve.tensor_copy(om[:, :, J * ST * g:J * ST * (g + 1)], psO[:, :, 0:J * ST]).then_inc(o_out, 1)

            @block.scalar
            def _(act):
                for g in range(G):
                    act.wait_ge(max_ready, g + 1)

                    def exp(c_, u, r):
                        act.wait_ge(turned, c_ + KS * g)
                        act.activation(pb[:, u], S[:, bass.ds(c_ * CK, CK)], ACT.Exp, bias=nm[:], scale=MLA_SCALE,
                                       accum_out=sums[:, bass.ds(c_, 1)]).then_inc(p_ready, 1)

                    chunks(act, NC, exp)
                    act.wait_ge(turned, NC + KS * g)
                    act.activation(pb[:, 0, 0:SR], S[:, NC * CK:NC * CK + SR], ACT.Exp, bias=nm[:], scale=MLA_SCALE,
                                   accum_out=sums[:, NC:NC + 1]).then_inc(p_ready, 1)


def route_tensors(c):
    return {"dest8": c.sb("route_dest8", [P, NT, TOPK], I32), "w8": c.sb("route_w8", [P, NT, TOPK])}


def phase_mix_and_route(nc, d, m):
    with ExitStack() as st, Semaphores(nc) as s:
        c = Ctx(nc, st)
        dest8, w8 = m["dest8"], m["w8"]
        w_out = c.sb("p6_w_out", [P, KD, D])
        w_r = c.sb("p6_w_r", [P, KD, E])
        w_sh = c.sb("p6_w_sh", [P, KD, 2 * DE])
        w_dn = c.sb("p6_w_dn", [P, 2, D])
        ident = c.sb("p6_ident", [P, P])
        g_bc = c.sb("p6_g", [P, D])
        bias = c.sb("p6_bias", [P, E])
        before = c.sb("p6_before", [P, P])
        ones = c.sb("p6_ones", [P, P])
        token = c.sb("p6_token", [P, NT], I32)
        e_base = c.sb("p6_e_base", [P, 2, E])
        eps = c.sb("p6_eps", [P, 1])
        oT = c.sb("p6_oT", [P, 2, KD, P])
        x = c.sb("p6_x", [P, 2, D])
        hh = c.sb("p6_h", [P, D])
        sq = c.sb("p6_sq", [P, D])
        ss = c.sb("p6_ss", [P, 1])
        n2 = c.sb("p6_n2", [P, D])
        nT = c.sb("p6_nT", [P, KD, P])
        sg = c.sb("p6_sg", [P, DE])
        hs = c.sb("p6_hs", [P, DE])
        hT = c.sb("p6_hT", [P, 2, P])
        acc = c.sb("p6_acc", [P, D])
        scores = c.sb("p6_scores", [P, E])
        biased = c.sb("p6_biased", [P, E])
        g8 = c.sb("p6_g8", [P, NG, 8])
        gs = c.sb("p6_gs", [P, NG])
        m8 = c.sb("p6_m8", [P, 8])
        gr = c.sb("p6_gr", [P, NG])
        t8 = c.sb("p6_t8", [P, 8])
        rep = c.sb("p6_rep", [P, E])
        sel = c.sb("p6_sel", [P, E])
        seen = c.sb("p6_seen", [P, E])
        wd = c.sb("p6_wd", [P, E])
        ws = c.sb("p6_ws", [P, 1])
        dv = c.sb("p6_dv", [P, E])
        dv8 = c.sb("p6_dv8", [P, 2, 8])
        pf = c.sb("p6_pf", [P, 8])
        big = c.sb("p6_big", [P, 8])
        junk = c.sb("p6_junk", [P, 2, 8, E])
        d8f = c.sb("p6_d8f", [P, 8])
        d8 = c.sb("p6_d8", [P, 2, 8], I32)
        rk = c.sb("p6_rk", [P, E])
        near = c.sb("p6_near", [P, E])
        wn = c.sb("p6_wn", [P, E])
        dn8 = c.sb("p6_dn8", [P, 8])
        entry = c.sb("p6_entry", [P, 2, TOPK, 2], I32)
        zeros = c.sb("p6_zeros", [P, D])
        none = c.sb("p6_none", [P, E * SLOTS // P, 2], I32)
        cnt = c.sb("p6_cnt", [P, E], I32)
        psH = c.ps("p6_psH", [P, D])
        psT = c.ps("p6_psT", [P, KD, P])
        psG = c.ps("p6_psG", [P, 2 * DE])
        psR = c.ps("p6_psR", [P, 512])
        psD = c.ps("p6_psD", [P, D])
        FAR = 1e30

        consts_in = s.sem("p6_consts_in")
        tile_in = [s.sem(f"p6_tile_in{u}") for u in range(2)]
        none_stored = s.sem("p6_none_stored")
        h_done = s.sem("p6_h_done")
        h_ready = s.sem("p6_h_ready")
        rooted = s.sem("p6_rooted")
        n_ready = s.sem("p6_n_ready")
        n_turned = s.sem("p6_n_turned")
        nT_ready = s.sem("p6_nT_ready")
        routed = s.sem("p6_routed")
        gated = s.sem("p6_gated")
        scores_ready = s.sem("p6_scores_ready")
        silu_ready = s.sem("p6_silu_ready")
        hs_ready = s.sem("p6_hs_ready")
        hs_turned = s.sem("p6_hs_turned")
        hT_ready = s.sem("p6_hT_ready")
        shared_done = s.sem("p6_shared_done")
        acc_ready = s.sem("p6_acc_ready")
        sel_ready = s.sem("p6_sel_ready")
        ranked = s.sem("p6_ranked")
        slots_ready = s.sem("p6_slots_ready")
        n_stored = s.sem("p6_n_stored")
        acc_stored = s.sem("p6_acc_stored")
        table_stored = [s.sem(f"p6_table_stored{u}") for u in range(2)]
        count_ready = s.sem("p6_count_ready")
        count_stored = s.sem("p6_count_stored")
        NCONST = 10

        with nc.Block() as block:

            @block.sync
            def _(sp):
                def load(t, u):
                    sp.dma_start(oT[:, u], d["oT"][t]).then_inc(tile_in[u], 16)
                    sp.dma_start(x[:, u], d["x"][t]).then_inc(tile_in[u], 16)

                for dst, src in ((none, d["no_token"]), (ident, d["ident"]), (w_out, d["w_out"]), (w_r, d["w_router"]),
                                 (g_bc, d["g_ffn"].partition_broadcast(P)), (bias, d["router_bias"].partition_broadcast(P)),
                                 (before, d["before"]), (token, d["token"]), (e_base, d["e_base"])):
                    sp.dma_start(dst[:], src).then_inc(consts_in, 16)
                load(0, 0)
                load(1, 1)
                sp.dma_start(w_sh[:], d["w_sh"]).then_inc(consts_in, 16)
                sp.dma_start(w_dn[:], d["w_sh_down"]).then_inc(consts_in, 16)

                def step(t, u, r, more=True):
                    sp.wait_ge(h_ready, t + 1)
                    if more:
                        load(t + 2, u)
                    sp.wait_ge(n_ready, t + 1)
                    sp.dma_start(d["n2"][t], n2[:]).then_inc(n_stored, 16)
                    sp.wait_ge(acc_ready, t + 1)
                    sp.dma_start(d["acc"][t], acc[:]).then_inc(acc_stored, 16)

                tiles(sp, TP - 2, step)
                step(TP - 2, 0, 0)
                step(TP - 1, 1, 0, False)
                step(TP, 0, 0, False)
                for a in range(2):
                    sp.dma_start(d["n2"][NT + a], zeros[:]).then_inc(n_stored, 16)
                    sp.dma_start(d["acc"][NT + a], zeros[:]).then_inc(acc_stored, 16)
                sp.wait_ge(count_ready, 1)
                sp.dma_start(d["count"], cnt[0:1, :]).then_inc(count_stored, 16)
                sp.wait_ge(n_stored, 16 * (NT + 2))
                sp.wait_ge(acc_stored, 16 * (NT + 2))
                sp.wait_ge(count_stored, 16)

            @block.tensor
            def _(pe):
                def mix(t, u, r):
                    pe.wait_ge(tile_in[u], 32 * r + 32)
                    pe.wait_ge(h_ready, t)
                    for a in range(2):
                        for k in range(KD):
                            i = pe.matmul(psH[:, 512 * a:512 * a + 512], oT[:, u, k], w_out[:, k, 512 * a:512 * a + 512],
                                          start=(k == 0), stop=(k == KD - 1))
                    i.then_inc(h_done, 1)

                def rest(t, u, r, sample=False):
                    pe.wait_ge(n_ready, t + 1)
                    pe.wait_ge(nT_ready, t)
                    for k in range(KD):
                        i = pe.transpose(psT[:, k], n2[:, k * P:(k + 1) * P], ident[:])
                    i.then_inc(n_turned, 1)
                    pe.wait_ge(nT_ready, t + 1)
                    pe.wait_ge(slots_ready, t)
                    for k in range(KD):
                        i = pe.matmul(psR[:, 0:E], nT[:, k], w_r[:, k], start=(k == 0), stop=(k == KD - 1))
                    i.then_inc(routed, 1)
                    pe.wait_ge(hs_ready, t)
                    for k in range(KD):
                        i = pe.matmul(psG[:], nT[:, k], w_sh[:, k], start=(k == 0), stop=(k == KD - 1))
                    i.then_inc(gated, 1)
                    pe.wait_ge(hs_ready, t + 1)
                    for k in range(2):
                        i = pe.transpose(psT[:, k], hs[:, k * P:(k + 1) * P], ident[:])
                    i.then_inc(hs_turned, 1)
                    pe.wait_ge(hT_ready, t + 1)
                    pe.wait_ge(acc_ready, t)
                    for a in range(2):
                        for k in range(2):
                            i = pe.matmul(psD[:, 512 * a:512 * a + 512], hT[:, k], w_dn[:, k, 512 * a:512 * a + 512],
                                          start=(k == 0), stop=(k == 1))
                    i.then_inc(shared_done, 1)
                    n = SR if sample else P
                    pe.wait_ge(sel_ready, t + 1)
                    pe.matmul(psR[0:n, E:2 * E], before[0:n, 0:n], sel[0:n], start=True, stop=True)
                    pe.matmul(psR[:, 2 * E:3 * E], ones[0:n], sel[0:n], start=True, stop=True).then_inc(ranked, 1)

                pe.wait_ge(consts_in, 16 * (NCONST + 2))
                mix(0, 0, 0)

                def step(t, u, r):
                    mix(t + 1, 1 - u, r + u)
                    rest(t, u, r)

                tiles(pe, TP, step)
                rest(TP, 0, TP // 2, True)

            @block.scalar
            def _(act):
                def step(t, u, r):
                    act.wait_ge(h_ready, t + 1)
                    act.activation(sq[:], hh[:], ACT.Square, accum_out=ss[:])
                    act.drain()
                    act.activation(ss[:], ss[:], ACT.Sqrt, bias=eps[:], scale=1.0 / D).then_inc(rooted, 1)
                    act.wait_ge(n_turned, t + 1)
                    act.copy(nT[:, 0:4], psT[:, 0:4])
                    act.copy(nT[:, 4:8], psT[:, 4:8]).then_inc(nT_ready, 1)
                    act.wait_ge(routed, t + 1)
                    act.activation(scores[:], psR[:, 0:E], ACT.Sigmoid).then_inc(scores_ready, 1)
                    act.wait_ge(gated, t + 1)
                    act.activation(sg[:], psG[:, 0:DE], ACT.Silu).then_inc(silu_ready, 1)
                    act.wait_ge(hs_turned, t + 1)
                    act.copy(hT[:], psT[:, 0:2]).then_inc(hT_ready, 1)

                act.wait_ge(consts_in, 16 * (NCONST + 2))
                tiles(act, TP, step)
                step(TP, 0, TP // 2)

            @block.vector
            def _(dve):
                def step(t, u, r, sample=False):
                    n = SR if sample else P
                    dve.wait_ge(h_done, t + 1)
                    dve.tensor_tensor(hh[:], x[:, u], psH[:], ALU.add).then_inc(h_ready, 1)
                    dve.wait_ge(rooted, t + 1)
                    dve.reciprocal(ss[:], ss[:])
                    dve.drain()
                    dve.wait_ge(n_stored, 16 * t)
                    dve.scalar_tensor_tensor(n2[:], hh[:], ss[:], g_bc[:], ALU.mult, ALU.mult).then_inc(n_ready, 1)
                    dve.wait_ge(scores_ready, t + 1)
                    dve.tensor_tensor(biased[:], scores[:], bias[:], ALU.add)
                    dve.drain()
                    for g in range(NG):
                        dve.max(g8[:, g], biased[:, g * GW:(g + 1) * GW])
                    dve.drain()
                    dve.tensor_tensor(gs[:].unsqueeze(2), g8[:, :, 0:1], g8[:, :, 1:2], ALU.add)
                    dve.drain()
                    dve.max(m8[:], gs[:])
                    dve.drain()
                    dve.memset(m8[:, TOPG:8], FAR)
                    dve.drain()
                    dve.match_replace(gr[:], m8[:], gs[:], -FAR)
                    dve.drain()
                    dve.tensor_scalar(gr[:], gr[:], -FAR, -1.0, ALU.is_equal, ALU.add)
                    dve.drain()
                    dve.scalar_tensor_tensor(biased[:].rearrange("p (g w) -> p g w", g=NG), bc(gr[:].unsqueeze(2), [P, NG, GW]),
                                             FAR, biased[:].rearrange("p (g w) -> p g w", g=NG), ALU.mult, ALU.add)
                    dve.drain()
                    dve.max(t8[:], biased[:])
                    dve.drain()
                    dve.match_replace(rep[:], t8[:], biased[:], 2 * FAR)
                    dve.drain()
                    dve.tensor_scalar(sel[:], rep[:], 2 * FAR, None, ALU.is_equal).then_inc(sel_ready, 1)
                    dve.drain()
                    dve.tensor_tensor_reduce(wd[:], sel[:], scores[:], 1.0, 0.0, ALU.mult, ALU.add, ws[:])
                    dve.drain()
                    dve.tensor_scalar(ws[:], ws[:], 1e-20, None, ALU.add)
                    dve.drain()
                    dve.reciprocal(ws[:], ws[:])
                    dve.drain()
                    dve.tensor_scalar(wd[:], wd[:], ws[:], 2.5, ALU.mult, ALU.mult)
                    dve.wait_ge(gated, t + 1)
                    dve.wait_ge(silu_ready, t + 1)
                    dve.tensor_tensor(hs[:], sg[:], psG[:, DE:2 * DE], ALU.mult).then_inc(hs_ready, 1)
                    dve.wait_ge(shared_done, t + 1)
                    dve.wait_ge(acc_stored, 16 * t)
                    dve.tensor_tensor(acc[:], hh[:], psD[:], ALU.add).then_inc(acc_ready, 1)
                    dve.wait_ge(ranked, t + 1)
                    dve.wait_ge(table_stored[u], 128 * r)
                    dve.tensor_tensor(rk[0:n], seen[0:n], psR[0:n, E:2 * E], ALU.add)
                    dve.drain()
                    dve.tensor_tensor(seen[:], seen[:], psR[:, 2 * E:3 * E], ALU.add)
                    dve.tensor_tensor(dv[0:n], e_base[0:n, 0], rk[0:n], ALU.subtract)
                    dve.scalar_tensor_tensor(near[0:n], rk[0:n], float(CAP), sel[0:n], ALU.is_lt, ALU.mult)
                    dve.drain()
                    dve.tensor_tensor(rk[0:n], e_base[0:n, 1], rk[0:n], ALU.subtract)
                    dve.drain()
                    dve.tensor_tensor(dv[0:n], dv[0:n], sel[0:n], ALU.mult)
                    dve.tensor_tensor(rk[0:n], rk[0:n], near[0:n], ALU.mult)
                    dve.tensor_tensor(wn[0:n], wd[0:n], near[0:n], ALU.mult)
                    dve.drain()
                    dve.max(dv8[0:n, u], dv[0:n])
                    dve.max(dn8[0:n], rk[0:n])
                    dve.drain()
                    for k in range(TOPK):
                        dve.scalar_tensor_tensor(junk[0:n, 0, k], dv[0:n], dv8[0:n, u, k:k + 1], wd[0:n], ALU.is_equal,
                                                 ALU.mult, accum_out=entry[0:n, u, k, 1:2].bitcast(F32))
                        dve.scalar_tensor_tensor(junk[0:n, 1, k], rk[0:n], dn8[0:n, k:k + 1], wn[0:n], ALU.is_equal,
                                                 ALU.mult, accum_out=w8[0:n, t, k:k + 1])
                    dve.tensor_scalar(d8f[0:n], dn8[0:n], -1.0, BIG, ALU.mult, ALU.add)
                    dve.tensor_copy(entry[0:n, u, :, 0:1], bc(token[0:n, bass.ds(t, 1)].unsqueeze(1), [n, TOPK, 1]))
                    dve.drain()
                    dve.tensor_scalar(dest8[0:n, t], d8f[0:n], float(E * CAP - 1), None, ALU.min).then_inc(slots_ready, 1)

                dve.memset(seen[:], 0.0)
                dve.memset(big[:], BIG)
                dve.memset(zeros[:], 0.0)
                dve.memset(ones[:], 1.0)
                dve.memset(eps[:], EPS)
                dve.memset(dest8[:], 0)
                dve.memset(w8[:], 0.0)
                dve.drain()
                dve.sem_inc(consts_in, 16)
                dve.wait_ge(consts_in, 16 * (NCONST + 2))
                tiles(dve, TP, step)
                step(TP, 0, TP // 2, True)
                dve.drain()
                dve.tensor_copy(cnt[:], seen[:]).then_inc(count_ready, 1)

            @block.gpsimd
            def _(pool):
                pool.wait_ge(consts_in, 16 * (NCONST + 2))
                pool.dma_start(d["table"].rearrange("(p n) two -> p n two", p=P), none[:]).then_inc(none_stored, 16)
                pool.wait_ge(none_stored, 16)

                def step(t, u, r, sample=False):
                    n = SR if sample else P
                    pool.wait_ge(slots_ready, t + 1)
                    pool.tensor_tensor(pf[0:n], big[0:n], dv8[0:n, u], ALU.subtract)
                    pool.drain()
                    pool.tensor_copy(d8[0:n, u], pf[0:n])
                    pool.drain()
                    for k in range(TOPK):
                        pool.indirect_dma_start(d["table"], bass.IndirectOffsetOnAxis(ap=d8[0:n, u, k:k + 1], axis=0),
                                                entry[0:n, u, k], None).then_inc(table_stored[u], 16)

                tiles(pool, TP, step)
                step(TP, 0, TP // 2, True)
                pool.wait_ge(table_stored[0], 128 * (TP // 2 + 1))
                pool.wait_ge(table_stored[1], 128 * (TP // 2))


def phase_experts(nc, d):
    B = CAP - P
    HC = DE // P
    MORE = SLOTS // CAP - 1
    with ExitStack() as st, Semaphores(nc) as s:
        c = Ctx(nc, st)
        ident = c.sb("p8_ident", [P, P])
        wg = c.sb("p8_wg", [P, 2, KD, DE])
        wu = c.sb("p8_wu", [P, 2, KD, DE])
        wd = c.sb("p8_wd", [P, 2, HC, D])
        idx = c.sb("p8_idx", [P, 2, 2, 2], I32)
        rows = c.sb("p8_rows", [P, 2, 2], I32)
        zero = c.sb("p8_zero", [P, 1], I32)
        cnt = c.sb("p8_cnt", [1, E], I32)
        xg = c.sb("p8_xg", [P, 2, 2, D])
        xT = c.sb("p8_xT", [P, 2, KD, CAP])
        sg = c.sb("p8_sg", [P, HC, CAP])
        hT = c.sb("p8_hT", [P, HC, CAP])
        y = c.sb("p8_y", [P, 2, 2, D])
        pT = c.ps("p8_pT", [P, KD, P])
        pTb = pT[:].rearrange("p k n -> p (k n)")[:, 0:KD * B].rearrange("p (k n) -> p k n", k=KD)
        pG = c.ps("p8_pG", [P, HC, 256])
        pU = c.ps("p8_pU", [P, HC, 256])
        pY = c.ps("p8_pY", [P, 2, D])
        pYb = pY[:, 1, 0:KD * B].rearrange("p (k n) -> p k n", k=KD)

        consts_in = s.sem("p8_consts_in")
        idx_in = [s.sem(f"p8_idx_in{u}") for u in range(2)]
        idx_read = s.sem("p8_idx_read")
        w_in = [s.sem(f"p8_w_in{u}") for u in range(2)]
        x_in = [s.sem(f"p8_x_in{u}") for u in range(2)]
        turned_a = s.sem("p8_turned_a")
        turned_b = s.sem("p8_turned_b")
        xa_act = s.sem("p8_xa_act")
        xa_dve = s.sem("p8_xa_dve")
        xb_dve = s.sem("p8_xb_dve")
        gate_done = s.sem("p8_gate_done")
        up_done = s.sem("p8_up_done")
        silu_done = s.sem("p8_silu_done")
        h_ready = s.sem("p8_h_ready")
        ya_done = s.sem("p8_ya_done")
        yb_done = s.sem("p8_yb_done")
        ya_out = s.sem("p8_ya_out")
        yb_out = s.sem("p8_yb_out")
        y_stored = [s.sem(f"p8_y_stored{u}") for u in range(2)]
        f_load = s.sem("p8f_load")
        f_in = s.sem("p8f_in")
        f_rows = s.sem("p8f_rows")
        f_x_in = s.sem("p8f_x_in")
        f_turned = s.sem("p8f_turned")
        f_x_out = s.sem("p8f_x_out")
        f_gated = s.sem("p8f_gated")
        f_silu = s.sem("p8f_silu")
        f_h = s.sem("p8f_h")
        f_y = s.sem("p8f_y")
        f_ya_out = s.sem("p8f_ya_out")
        f_yb_out = s.sem("p8f_yb_out")
        f_done = s.sem("p8f_done")

        def load_idx(sp, e, u, first, sem):
            for a, (at, n) in enumerate(((0, P), (P, B))):
                sp.dma_start(idx[0:n, u, a], d["table"][bass.ds(e * SLOTS + (first + at), n)]).then_inc(sem, 16)

        def load_w(sp, e, u, sem):
            sp.dma_start(wg[:, u], d["w_gate"][e].rearrange("k p n -> p k n")).then_inc(sem, 16)
            sp.dma_start(wu[:, u], d["w_up"][e].rearrange("k p n -> p k n")).then_inc(sem, 16)
            sp.dma_start(wd[:, u], d["w_down"][e].rearrange("k p n -> p k n")).then_inc(sem, 16)

        def store_y(sp, e, u, sem):
            for a, (at, n) in enumerate(((0, P), (P, B))):
                sp.dma_start(d["ys"][bass.ds(e * CAP + at, n)], y[0:n, u, a]).then_inc(sem, 16)

        def gather(pool, u, sem):
            pool.tensor_tensor(rows[:, u, 0:1], idx[:, u, 0, 0:1], zero[:], ALU.add)
            i = pool.tensor_tensor(rows[0:B, u, 1:2], idx[0:B, u, 1, 0:1], zero[0:B], ALU.add)
            pool.drain()
            for a, n in enumerate((P, B)):
                pool.indirect_dma_start(xg[0:n, u, a], None, d["n2"].rearrange("t p n -> (t p) n"),
                                        bass.IndirectOffsetOnAxis(ap=rows[0:n, u, a:a + 1], axis=0)).then_inc(sem, 16)
            return i

        def turn_a(pe, u):
            for k in range(KD):
                i = pe.transpose(pT[:, k], xg[:, u, 0, k * P:(k + 1) * P], ident[:])
            return i

        def turn_b(pe, u, out=pTb):
            for k in range(KD):
                i = pe.transpose(out[:, k], xg[0:B, u, 1, k * P:(k + 1) * P], ident[0:B, 0:B])
            return i

        def hidden(pe, u, ps, w):
            for m in range(HC):
                for k in range(KD):
                    i = pe.matmul(ps[:, m, 0:CAP], w[:, u, k, m * P:(m + 1) * P], xT[:, u, k],
                                  start=(k == 0), stop=(k == KD - 1))
            return i

        def down(pe, u, a):
            at, n = ((0, P), (P, B))[a]
            for half in range(2):
                cols = slice(512 * half, 512 * half + 512)
                for k in range(HC):
                    i = pe.matmul(pY[0:n, a, cols], hT[:, k, at:at + n], wd[:, u, k, cols],
                                  start=(k == 0), stop=(k == HC - 1))
            return i

        def experts(eng, body, last):
            tiles(eng, E - 2, body)
            last(E - 2, 0, E // 2 - 1)
            last(E - 1, 1, E // 2 - 1)

        with nc.Block() as block:

            @block.sync
            def _(sp):
                sp.dma_start(ident[:], d["ident"]).then_inc(consts_in, 16)
                for e in range(2):
                    load_idx(sp, e, e, 0, idx_in[e])
                    load_w(sp, e, e, w_in[e])

                def step(e, u, r, more=True):
                    if more:
                        sp.wait_ge(idx_read, e + 1)
                        load_idx(sp, e + 2, u, 0, idx_in[u])
                    sp.wait_ge(ya_out, e + 1)
                    sp.wait_ge(yb_out, e + 1)
                    if more:
                        load_w(sp, e + 2, u, w_in[u])
                    store_y(sp, e, u, y_stored[u])

                experts(sp, step, lambda e, u, r: step(e, u, r, False))
                for u in range(2):
                    sp.wait_ge(y_stored[u], 32 * (E // 2))

            @block.gpsimd
            def _(pool):
                pool.memset(zero[:], 0)
                pool.drain()
                for e in range(2):
                    pool.wait_ge(idx_in[e], 32)
                    gather(pool, e, x_in[e]).then_inc(idx_read, 1)

                def step(e, u, r):
                    pool.wait_ge(turned_b, e + 1)
                    pool.wait_ge(idx_in[u], 32 * r + 64)
                    gather(pool, u, x_in[u]).then_inc(idx_read, 1)

                tiles(pool, E - 2, step)

            @block.tensor
            def _(pe):
                def turns(e, u, r):
                    pe.wait_ge(x_in[u], 32 * r + 32)
                    pe.wait_ge(xb_dve, e)
                    turn_a(pe, u).then_inc(turned_a, 1)

                def pT_free(e):
                    pe.wait_ge(xa_act, e + 1)
                    pe.wait_ge(xa_dve, e + 1)

                def products(e, u, r, more=True):
                    pe.wait_ge(w_in[u], 48 * r + 48)
                    pe.wait_ge(xb_dve, e + 1)
                    pe.wait_ge(h_ready, e)
                    hidden(pe, u, pG, wg).then_inc(gate_done, 1)
                    if more:
                        pT_free(e + 1)
                    hidden(pe, u, pU, wu).then_inc(up_done, 1)
                    if more:
                        turn_b(pe, 1 - u).then_inc(turned_b, 1)
                    pe.wait_ge(h_ready, e + 1)
                    pe.wait_ge(ya_out, e)
                    down(pe, u, 0).then_inc(ya_done, 1)
                    pe.wait_ge(yb_out, e)
                    down(pe, u, 1).then_inc(yb_done, 1)

                pe.wait_ge(consts_in, 16)
                turns(0, 0, 0)
                pT_free(0)
                turn_b(pe, 0).then_inc(turned_b, 1)

                def step(e, u, r):
                    turns(e + 1, 1 - u, r + u)
                    products(e, u, r)

                tiles(pe, E - 2, step)
                step(E - 2, 0, E // 2 - 1)
                products(E - 1, 1, E // 2 - 1, False)

            @block.scalar
            def _(act):
                def xa(e, u):
                    act.wait_ge(turned_a, e + 1)
                    act.copy(xT[:, u, 4:8, 0:P], pT[:, 4:8]).then_inc(xa_act, 1)

                def step(e, u, r, more=True):
                    if more:
                        act.wait_ge(up_done, e)
                        xa(e + 1, 1 - u)
                    act.wait_ge(gate_done, e + 1)
                    act.wait_ge(h_ready, e)
                    act.activation(sg[:], pG[:, :, 0:CAP], ACT.Silu).then_inc(silu_done, 1)
                    act.wait_ge(ya_done, e + 1)
                    act.wait_ge(y_stored[u], 32 * r)
                    act.copy(y[:, u, 0], pY[:, 0]).then_inc(ya_out, 1)

                xa(0, 0)
                tiles(act, E - 2, step)
                step(E - 2, 0, E // 2 - 1)
                step(E - 1, 1, E // 2 - 1, False)

            @block.vector
            def _(dve):
                def xa(e, u):
                    dve.wait_ge(turned_a, e + 1)
                    dve.tensor_copy(xT[:, u, 0:4, 0:P], pT[:, 0:4]).then_inc(xa_dve, 1)

                def xb(e, u):
                    dve.wait_ge(turned_b, e + 1)
                    dve.tensor_copy(xT[:, u, :, P:CAP], pTb).then_inc(xb_dve, 1)

                def step(e, u, r, more=True):
                    if more:
                        dve.wait_ge(up_done, e)
                        xa(e + 1, 1 - u)
                    dve.wait_ge(silu_done, e + 1)
                    dve.wait_ge(up_done, e + 1)
                    dve.wait_ge(yb_done, e)
                    dve.tensor_tensor(hT[:], sg[:], pU[:, :, 0:CAP], ALU.mult).then_inc(h_ready, 1)
                    if more:
                        xb(e + 1, 1 - u)
                    dve.wait_ge(yb_done, e + 1)
                    dve.wait_ge(y_stored[u], 32 * r)
                    dve.tensor_copy(y[0:B, u, 1], pY[0:B, 1]).then_inc(yb_out, 1)

                xa(0, 0)
                xb(0, 0)
                tiles(dve, E - 2, step)
                step(E - 2, 0, E // 2 - 1)
                step(E - 1, 1, E // 2 - 1, False)

        with nc.Block() as block:
            def further(eng, body, skip):
                with eng.Fori(0, E) as e:
                    have = eng.value_load(cnt[0:1, bass.ds(e, 1)], min_val=0, max_val=NT * P)
                    with eng.If(have > CAP):
                        with eng.Fori(1, MORE + 1) as b:
                            with eng.If(have > b * CAP):
                                body(e, b, e * MORE + b - 1)
                            with eng.Else():
                                skip(1)
                    with eng.Else():
                        skip(MORE)

            @block.sync
            def _(sp):
                sp.dma_start(cnt[:], d["count"]).then_inc(consts_in, 16)
                sp.wait_ge(consts_in, 32)

                def body(e, b, n):
                    sp.wait_ge(f_done, n)
                    load_idx(sp, e, 0, b * CAP, f_load)
                    load_w(sp, e, 0, f_load)
                    sp.wait_ge(f_load, 80)
                    sp.sem_clear(f_load)
                    sp.sem_inc(f_in, 1)

                def skip(k):
                    sp.sem_inc(f_in, k)

                further(sp, body, skip)

            @block.gpsimd
            def _(pool):
                def body(e, b, n):
                    pool.wait_ge(f_in, n + 1)
                    gather(pool, 0, f_rows)
                    pool.wait_ge(f_rows, 32)
                    pool.sem_inc(f_x_in, 1)
                    pool.wait_ge(f_ya_out, n + 1)
                    pool.wait_ge(f_yb_out, n + 1)
                    pool.tensor_tensor(rows[:, 1, 0:1], zero[:], zero[:], ALU.add)
                    for a, m in enumerate((P, B)):
                        pool.indirect_dma_start(d["acc"].rearrange("t p n -> (t p) n"),
                                                bass.IndirectOffsetOnAxis(ap=rows[0:m, 0, a:a + 1], axis=0),
                                                y[0:m, 0, a], None, compute_op=ALU.add).then_inc(f_rows, 16)
                    pool.wait_ge(f_rows, 64)
                    pool.dma_reset(range(f_rows.num, f_rows.num + 1))
                    pool.sem_clear(f_rows)
                    pool.sem_inc(f_done, 1)

                def skip(k):
                    pool.sem_inc(f_x_in, k)
                    pool.sem_inc(f_done, k)

                pool.wait_ge(consts_in, 32)
                further(pool, body, skip)

            @block.tensor
            def _(pe):
                def body(e, b, n):
                    pe.wait_ge(f_x_in, n + 1)
                    turn_a(pe, 0)
                    turn_b(pe, 0, pYb).then_inc(f_turned, 1)
                    pe.wait_ge(f_x_out, n + 1)
                    hidden(pe, 0, pG, wg)
                    hidden(pe, 0, pU, wu).then_inc(f_gated, 1)
                    pe.wait_ge(f_h, n + 1)
                    down(pe, 0, 0)
                    down(pe, 0, 1).then_inc(f_y, 1)

                def skip(k):
                    pe.drain()
                    pe.sem_inc(f_turned, k)
                    pe.sem_inc(f_gated, k)
                    pe.sem_inc(f_y, k)

                pe.wait_ge(consts_in, 32)
                further(pe, body, skip)

            @block.scalar
            def _(act):
                def body(e, b, n):
                    act.wait_ge(f_gated, n + 1)
                    act.activation(sg[:], pG[:, :, 0:CAP], ACT.Silu).then_inc(f_silu, 1)
                    act.wait_ge(f_y, n + 1)
                    act.wait_ge(f_done, n)
                    act.mul(y[:, 0, 0], pY[:, 0], idx[:, 0, 0, 1:2].bitcast(F32)).then_inc(f_ya_out, 1)

                def skip(k):
                    act.drain()
                    act.sem_inc(f_silu, k)
                    act.sem_inc(f_ya_out, k)

                act.wait_ge(consts_in, 32)
                further(act, body, skip)

            @block.vector
            def _(dve):
                def body(e, b, n):
                    dve.wait_ge(f_turned, n + 1)
                    dve.tensor_copy(xT[:, 0, :, 0:P], pT[:])
                    dve.tensor_copy(xT[:, 0, :, P:CAP], pYb).then_inc(f_x_out, 1)
                    dve.wait_ge(f_silu, n + 1)
                    dve.tensor_tensor(hT[:], sg[:], pU[:, :, 0:CAP], ALU.mult).then_inc(f_h, 1)
                    dve.wait_ge(f_y, n + 1)
                    dve.wait_ge(f_done, n)
                    dve.tensor_scalar(y[0:B, 0, 1], pY[0:B, 1], idx[0:B, 0, 1, 1:2].bitcast(F32), None,
                                      ALU.mult).then_inc(f_yb_out, 1)

                def skip(k):
                    dve.drain()
                    dve.sem_inc(f_x_out, k)
                    dve.sem_inc(f_h, k)
                    dve.sem_inc(f_yb_out, k)

                dve.wait_ge(consts_in, 32)
                further(dve, body, skip)


def phase_combine(nc, d, m):
    with ExitStack() as st, Semaphores(nc) as s:
        c = Ctx(nc, st)
        dest8, w8 = m["dest8"], m["w8"]
        ident = c.sb("p9_ident", [P, P])
        wpg = c.sb("p9_wpg", [P, KD, D])
        wpp = c.sb("p9_wpp", [P, 2, D])
        g1 = c.sb("p9_g1", [P, D])
        g2 = c.sb("p9_g2", [P, D])
        eps = c.sb("p9_eps", [P, 1])
        zero = c.sb("p9_zero", [P, TOPK], I32)
        still = c.sb("p9_still", [P, TOPK], I32)
        slot = c.sb("p9_slot", [P, 2, TOPK], I32)
        yg = c.sb("p9_yg", [P, 2, TOPK, D])
        hh = c.sb("p9_h", [P, 2, D])
        pt = c.sb("p9_p", [P, 2, R])
        sq = c.sb("p9_sq", [P, D])
        ss = c.sb("p9_ss", [P, 2])
        n3 = c.sb("p9_n3", [P, D])
        nT = c.sb("p9_nT", [P, KD + 2, P])
        gate = c.sb("p9_gate", [P, D])
        yo = c.sb("p9_y", [P, D])
        psT = c.ps("p9_psT", [P, 12, P])
        psG = c.ps("p9_psG", [P, D])
        psP = c.ps("p9_psP", [P, D])

        consts_in = s.sem("p9_consts_in")
        tile_in = [s.sem(f"p9_tile_in{u}") for u in range(2)]
        rows_in = [s.sem(f"p9_rows_in{u}") for u in range(2)]
        summed = s.sem("p9_summed")
        rooted = s.sem("p9_rooted")
        n_ready = s.sem("p9_n_ready")
        turned = s.sem("p9_turned")
        nT_ready = s.sem("p9_nT_ready")
        gated = s.sem("p9_gated")
        projected = s.sem("p9_projected")
        gate_ready = s.sem("p9_gate_ready")
        h_ready = s.sem("p9_h_ready")
        y_ready = s.sem("p9_y_ready")
        y_stored = s.sem("p9_y_stored")

        with nc.Block() as block:

            @block.sync
            def _(sp):
                def load(t, u):
                    sp.dma_start(hh[:, u], d["acc"][t]).then_inc(tile_in[u], 16)
                    sp.dma_start(pt[:, u], d["p"][t]).then_inc(tile_in[u], 16)

                load(0, 0)
                load(1, 1)
                for dst, src in ((ident, d["ident"]), (wpg, d["w_ple_gate"]), (wpp, d["w_ple_proj"]),
                                 (g1, d["g_ple"].partition_broadcast(P)), (g2, d["g_final"].partition_broadcast(P))):
                    sp.dma_start(dst[:], src).then_inc(consts_in, 16)

                def step(t, u, r, more=True):
                    sp.wait_ge(y_ready, t + 1)
                    if more:
                        load(t + 2, u)
                    sp.dma_start(d["y"][t], yo[:]).then_inc(y_stored, 16)

                tiles(sp, TP - 2, step)
                step(TP - 2, 0, 0)
                step(TP - 1, 1, 0, False)
                step(TP, 0, 0, False)
                sp.wait_ge(y_stored, 16 * NT)

            @block.gpsimd
            def _(pool):
                def gather(t, u):
                    pool.tensor_tensor(still[:], zero[:], zero[:], ALU.add)
                    pool.tensor_tensor(slot[:, u], dest8[:, t], zero[:], ALU.add)
                    pool.drain()
                    for k in range(TOPK):
                        pool.indirect_dma_start(yg[:, u, k], None, d["ys"],
                                                bass.IndirectOffsetOnAxis(ap=slot[:, u, k:k + 1], axis=0)).then_inc(rows_in[u], 16)

                pool.memset(zero[:], 0)
                pool.drain()
                gather(0, 0)
                gather(1, 1)

                def step(t, u, r):
                    pool.wait_ge(summed, t + 1)
                    gather(t + 2, u)

                tiles(pool, TP - 2, step)
                step(TP - 2, 0, 0)

            @block.tensor
            def _(pe):
                def step(t, u, r):
                    pe.wait_ge(n_ready, t + 1)
                    pe.wait_ge(tile_in[u], 32 * r + 32)
                    pe.wait_ge(nT_ready, t)
                    for k in range(KD):
                        pe.transpose(psT[:, k], n3[:, k * P:(k + 1) * P], ident[:])
                    for k in range(2):
                        i = pe.transpose(psT[:, KD + k], pt[:, u, k * P:(k + 1) * P], ident[:])
                    i.then_inc(turned, 1)
                    pe.wait_ge(nT_ready, t + 1)
                    pe.wait_ge(h_ready, t)
                    for a in range(2):
                        cols = slice(512 * a, 512 * a + 512)
                        for k in range(KD):
                            i = pe.matmul(psG[:, cols], nT[:, k], wpg[:, k, cols], start=(k == 0), stop=(k == KD - 1))
                    i.then_inc(gated, 1)
                    for a in range(2):
                        cols = slice(512 * a, 512 * a + 512)
                        for k in range(2):
                            i = pe.matmul(psP[:, cols], nT[:, KD + k], wpp[:, k, cols], start=(k == 0), stop=(k == 1))
                    i.then_inc(projected, 1)

                pe.wait_ge(consts_in, 96)
                tiles(pe, TP, step)
                step(TP, 0, TP // 2)

            @block.scalar
            def _(act):
                def root(a):
                    act.drain()
                    act.activation(ss[:, a:a + 1], ss[:, a:a + 1], ACT.Sqrt, bias=eps[:], scale=1.0 / D).then_inc(rooted, 1)

                def step(t, u, r):
                    act.wait_ge(summed, t + 1)
                    act.activation(sq[:], hh[:, u], ACT.Square, accum_out=ss[:, 0:1])
                    root(0)
                    act.wait_ge(turned, t + 1)
                    for a in range(3):
                        w = min(4, KD + 2 - 4 * a)
                        i = act.copy(nT[:, 4 * a:4 * a + w], psT[:, 4 * a:4 * a + w])
                    i.then_inc(nT_ready, 1)
                    act.wait_ge(gated, t + 1)
                    act.activation(gate[:], psG[:], ACT.Sigmoid).then_inc(gate_ready, 1)
                    act.wait_ge(h_ready, t + 1)
                    act.activation(sq[:], hh[:, u], ACT.Square, accum_out=ss[:, 1:2])
                    root(1)

                act.wait_ge(consts_in, 96)
                tiles(act, TP, step)
                step(TP, 0, TP // 2)

            @block.vector
            def _(dve):
                def step(t, u, r):
                    dve.wait_ge(tile_in[u], 32 * r + 32)
                    dve.wait_ge(rows_in[u], 16 * TOPK * r + 16 * TOPK)
                    for k in range(TOPK):
                        i = dve.scalar_tensor_tensor(hh[:, u], yg[:, u, k], w8[:, t, k:k + 1], hh[:, u], ALU.mult, ALU.add)
                        if k < TOPK - 1:
                            dve.drain()
                    i.then_inc(summed, 1)
                    dve.wait_ge(rooted, 2 * t + 1)
                    dve.reciprocal(ss[:, 0:1], ss[:, 0:1])
                    dve.drain()
                    dve.scalar_tensor_tensor(n3[:], hh[:, u], ss[:, 0:1], g1[:], ALU.mult, ALU.mult).then_inc(n_ready, 1)
                    dve.wait_ge(gate_ready, t + 1)
                    dve.wait_ge(projected, t + 1)
                    dve.tensor_tensor(gate[:], gate[:], psP[:], ALU.mult)
                    dve.drain()
                    dve.tensor_tensor(hh[:, u], hh[:, u], gate[:], ALU.add).then_inc(h_ready, 1)
                    dve.wait_ge(rooted, 2 * t + 2)
                    dve.reciprocal(ss[:, 1:2], ss[:, 1:2])
                    dve.drain()
                    dve.wait_ge(y_stored, 16 * t)
                    dve.scalar_tensor_tensor(yo[:], hh[:, u], ss[:, 1:2], g2[:], ALU.mult, ALU.mult).then_inc(y_ready, 1)

                dve.memset(eps[:], EPS)
                dve.drain()
                dve.sem_inc(consts_in, 16)
                dve.wait_ge(consts_in, 96)
                tiles(dve, TP, step)
                step(TP, 0, TP // 2)


def constants():
    i = np.arange(P)
    tri = (i[:, None] <= i[None, :]).astype(np.float32)
    same_b = (i[:, None] // ST == i[None, :] // ST) & (i[:, None] < SR) & (i[None, :] < SR)
    tri_s = tri * same_b
    levels = np.zeros((P, LV, P), np.float32)
    for n in range(LV):
        s = 1 << n
        levels[:, n, :] = (i[:, None] // (2 * s) == i[None, :] // (2 * s)) & (i[:, None] // s % 2 == 0) & (i[None, :] // s % 2 == 1)
    half = RO // 2
    inv = 10000.0 ** (-np.arange(half, dtype=np.float32) / np.float32(half)).astype(np.float32)
    pos = np.zeros((NT, P), np.float32)
    pos[:TP] = np.arange(TP * P).reshape(TP, P)
    pos[TP, :SR] = np.tile(NPAGE * PAGE + np.arange(ST), SB)
    ang = (pos[:, :, None] * inv.astype(np.float32)).astype(np.float32)
    rows = np.arange(P)
    new = np.full((2, P, SR), NEG, np.float32)
    for g in range(2):
        b, t = 4 * g + rows // 32, rows % 8
        key = np.arange(SR)
        new[g][(key[None, :] // ST == b[:, None]) & (key[None, :] % ST <= t[:, None])] = 0.0
    return {
        "ident": np.eye(P, dtype=np.float32),
        "tri": np.ascontiguousarray(np.stack([tri, tri_s], 1)),
        "same": np.ascontiguousarray(np.stack([np.ones((P, P), np.float32), same_b.astype(np.float32)], 1)),
        "levels": levels,
        "batch_rows": (i[:, None] // ST == np.arange(SB)[None, :]).astype(np.float32),
        "causal": np.where(i[:, None] >= i[None, :], 0.0, NEG).astype(np.float32),
        "new_mask": np.ascontiguousarray(new.transpose(1, 0, 2)),
        "cos": np.cos(ang).astype(np.float32),
        "sin": np.sin(ang).astype(np.float32),
        "before": (i[:, None] < i[None, :]).astype(np.float32),
        "token": np.ascontiguousarray((np.arange(NT)[None, :] * P + i[:, None]).astype(np.int32)),
        "e_base": np.ascontiguousarray(np.broadcast_to(
            BIG - np.stack([SLOTS * np.arange(E), CAP * np.arange(E)]).astype(np.float32), (P, 2, E))),
        "no_token": np.ascontiguousarray(np.stack(
            [NT * P + np.arange(E * SLOTS) % CAP, np.zeros(E * SLOTS)], 1).astype(np.int32).reshape(P, -1, 2)),
    }


BIG = float(1 << 17)

_INS = ['x_prompt', 'x_sample', 'p_prompt', 'p_sample', 'cache_ckv', 'cache_krope', 'state_gdn', 'state_conv',
        'page_table', 'g_mix', 'w_in', 'gdn_conv_w', 'gdn_a_log', 'gdn_dt_bias', 'gdn_norm', 'mla_g_q', 'mla_w_uq',
        'mla_g_kv', 'mla_w_uk', 'mla_w_uv', 'w_out', 'g_ffn', 'w_router', 'router_bias', 'w_exp_gate', 'w_exp_up',
        'w_exp_down', 'w_sh_gate', 'w_sh_up', 'w_sh_down', 'g_ple', 'w_ple_gate', 'w_ple_proj', 'g_final']


def rows_in(w):
    return np.ascontiguousarray(w.reshape(-1, P, w.shape[-1]).transpose(1, 0, 2))


def tile_rows(a, b):
    w = a.shape[-1]
    z = np.zeros((NT * P - TP * P - SR, w), a.dtype)
    return np.concatenate([a.reshape(-1, w), b.reshape(-1, w), z]).reshape(NT, P, w)


def layout(v):
    w = v['w_in'][0]
    at = np.cumsum([0, 3 * ZW, ZW, H, H, R, R, RO])
    qkv, z, b, a, cq, ckv, kr = (w[:, at[n]:at[n + 1]] for n in range(7))
    ck = v['cache_ckv'][0]
    ins = {
        "x": tile_rows(v['x_prompt'], v['x_sample']),
        "p": tile_rows(v['p_prompt'], v['p_sample']),
        "w_nat": rows_in(np.concatenate([z, cq, ckv, kr, b, a], 1)),
        "w_qkv": rows_in(qkv),
        "conv_w": np.ascontiguousarray(v['gdn_conv_w'][0].reshape(4, CC, P).transpose(2, 1, 0)),
        "state_conv": np.ascontiguousarray(v['state_conv'][0].reshape(SB, 3, CC, P).transpose(3, 2, 0, 1)),
        "state": np.ascontiguousarray(v['state_gdn'][0].transpose(2, 0, 1, 3)),
        "g_mix": v['g_mix'][0], "g_ffn": v['g_ffn'][0], "g_ple": v['g_ple'][0], "g_final": v['g_final'],
        "a_log": v['gdn_a_log'][0], "dt_bias": v['gdn_dt_bias'][0], "gdn_norm": v['gdn_norm'][0],
        "g_q": v['mla_g_q'][0], "g_kv": v['mla_g_kv'][0],
        "w_uq": rows_in(v['mla_w_uq'][0]),
        "w_uk": np.ascontiguousarray(v['mla_w_uk'][0].transpose(2, 1, 0)),
        "w_uv": rows_in(v['mla_w_uv'][0].reshape(R, H * DK)),
        "w_out": rows_in(v['w_out'][0]),
        "w_router": rows_in(v['w_router'][0]), "router_bias": v['router_bias'][0],
        "w_sh": rows_in(np.concatenate([v['w_sh_gate'][0], v['w_sh_up'][0]], 1)),
        "w_sh_down": rows_in(v['w_sh_down'][0]),
        "w_ple_gate": rows_in(v['w_ple_gate'][0]), "w_ple_proj": rows_in(v['w_ple_proj'][0]),
        "w_gate": v['w_exp_gate'][0].reshape(E, KD, P, DE), "w_up": v['w_exp_up'][0].reshape(E, KD, P, DE),
        "w_down": v['w_exp_down'][0].reshape(E, 2, P, D),
        "cache": ck,
        "cacheT": np.concatenate([ck.reshape(-1, PAGE, 2, P).transpose(0, 3, 2, 1).reshape(-1, P, R),
                                  v['cache_krope'][0].reshape(-1, 2, PAGE // 2, RO).transpose(0, 1, 3, 2).reshape(-1, P, PAGE // 2)], 2),
        "pages": v['page_table'].reshape(2, 4, NPAGE // 4, 4).transpose(0, 2, 1, 3).reshape(1, -1),
    }
    return {n: np.ascontiguousarray(x) for n, x in ins.items()} | constants()


def outputs():
    return {"y": (NT, P, D), "ckv": (NT, P, R), "krope": (NT, P, RO), "gdn_p": (P, H, P), "gdn_s": (P, SB, H, P),
            "conv_p": (P, CC, 3), "conv_s": (P, CC, SB, 3)}


def scratch():
    return {"nat": (NT, P, NW), "yT": (NT, P, CC, P), "oT": (NT, P, KD, P), "n2": (NT + 2, P, D), "acc": (NT + 2, P, D),
            "table": [(E * SLOTS, 2), I32], "count": [(1, E), I32], "ys": (E * CAP, D)}


def program(nc, arrays):
    d = {n: nc.dram_tensor(f"in_{n}", a.shape, mybir.dt.from_np(a.dtype), kind="ExternalInput").ap() for n, a in arrays.items()}
    d |= {n: nc.dram_tensor(f"out_{n}", s, F32, kind="ExternalOutput").ap() for n, s in outputs().items()}
    for n, s in scratch().items():
        s, dt = s if isinstance(s, list) else (s, F32)
        d[n] = nc.dram_tensor(f"scratch_{n}", s, dt).ap()
    phase_project(nc, d)
    phase_gdn(nc, d)
    with ExitStack() as st:
        m = mla_tensors(Ctx(nc, st))
        phase_latents(nc, d, m)
        phase_prompt_attention(nc, d, m)
        phase_sample_attention(nc, d, m)
    with ExitStack() as st:
        m = route_tensors(Ctx(nc, st))
        phase_mix_and_route(nc, d, m)
        phase_experts(nc, d)
        phase_combine(nc, d, m)


def kernel(**inputs):
    import concourse.bacc as bacc
    from concourse.bass_utils import run_bass_kernel_spmd

    arrays = layout({n: np.asarray(inputs[n]) for n in _INS})
    nc = bacc.Bacc("TRN2", target_bir_lowering=False, num_devices=1)
    program(nc, arrays)
    r = run_bass_kernel_spmd(nc, [{f"in_{n}": a for n, a in arrays.items()}], core_ids=[0]).results[0]
    o = {n: r[f"out_{n}"] for n in outputs()}

    def split(a):
        w = a.shape[-1]
        a = a.reshape(NT * P, w)
        return a[:TP * P].reshape(1, TP * P, w), a[TP * P:TP * P + SR].reshape(SB, ST, w)

    y_p, y_s = split(o["y"])
    ckv_p, ckv_s = split(o["ckv"])
    kr_p, kr_s = split(o["krope"])
    return (y_p, y_s, ckv_p[None], kr_p[None],
            np.ascontiguousarray(o["gdn_p"].transpose(1, 0, 2))[None, None],
            np.ascontiguousarray(o["conv_p"].transpose(2, 1, 0)).reshape(1, 1, 3, CC * P),
            ckv_s[None], kr_s[None],
            np.ascontiguousarray(o["gdn_s"].transpose(1, 2, 0, 3))[None],
            np.ascontiguousarray(o["conv_s"].transpose(2, 3, 1, 0)).reshape(1, SB, 3, CC * P))
```

```python
from contextlib import ExitStack

import numpy as np
import concourse.bass as bass
from concourse import mybir

F32 = mybir.dt.float32
I32 = mybir.dt.int32
ALU = mybir.AluOpType
ACT = mybir.ActivationFunctionType
AX_X = mybir.AxisListType.X

P = 128
D = 1024
KD = D // P
TP = 8
NT = TP + 1
SB, ST = 8, 8
SR = SB * ST
H = 4
DK = 128
CC = 3 * H
R = 256
RO = 64
ZW, LW, TW = H * DK, 2 * R, RO + 2 * H
NW = ZW + LW + TW
PAGE = 128
NPAGE = 64
EPS = 1e-6
MLA_SCALE = float(DK + RO) ** -0.5
NEG = -1e30
E = 64
TOPK = 8
NG = 8
GW = E // NG
TOPG = 4
DE = 256
CAP = 192
SLOTS = 6 * CAP
LV = 7


class Ctx:

    def __init__(self, nc, stack):
        self.nc, self.stack = nc, stack

    def sb(self, name, shape, dt=F32):
        return self.stack.enter_context(self.nc.sbuf_tensor(name, shape, dt))

    def ps(self, name, shape, dt=F32):
        return self.stack.enter_context(self.nc.psum_tensor(name, shape, dt))


class Semaphores:

    def __init__(self, nc):
        self.nc, self.stack, self.taken = nc, ExitStack(), []

    def sem(self, name):
        self.taken.append(self.stack.enter_context(self.nc.semaphore(name)))
        return self.taken[-1]

    def __enter__(self):
        return self

    def __exit__(self, *error):
        if error[0] is None:
            nums = sorted(t.num for t in self.taken)
            runs = [[nums[0], nums[0] + 1]]
            for n in nums[1:]:
                if n == runs[-1][1]:
                    runs[-1][1] = n + 1
                else:
                    runs.append([n, n + 1])
            with self.nc.Block() as block:

                @block.gpsimd
                def _(pool):
                    for a, b in runs:
                        pool.dma_reset(range(a, b))
                        pool.sem_clear(range(a, b))

        self.stack.close()


def tiles(eng, n, body, first=0):
    assert n % 2 == 0 and first == 0
    with eng.Fori(0, n // 2) as r:
        for u in range(2):
            body(r * 2 + u, u, r)


def bc(ap, shape):
    return ap.to_broadcast(shape)



def phase_project(nc, d):
    with ExitStack() as st, Semaphores(nc) as s:
        c = Ctx(nc, st)
        wn = c.sb("p1_wn", [P, KD, NW])
        wq = c.sb("p1_wq", [P, KD, CC * P])
        ident = c.sb("p1_ident", [P, P])
        g_bc = c.sb("p1_g", [P, D])
        cw = c.sb("p1_cw", [P, CC, 4])
        xb = c.sb("p1_x", [P, 2, D])
        sq = c.sb("p1_sq", [P, D])
        ss = c.sb("p1_ss", [P, 2])
        eps = c.sb("p1_eps", [P, 1])
        un = c.sb("p1_un", [P, 2, D])
        uT = c.sb("p1_uT", [P, 2, KD, P])
        nat = c.sb("p1_nat", [P, NW])
        qx = c.sb("p1_qx", [P, CC, P + 3])
        qs = c.sb("p1_qs", [P, CC, SB, ST + 3])
        sc = c.sb("p1_sc", [P, CC, SB, 3])
        cy = c.sb("p1_cy", [P, CC, P])
        sy = c.sb("p1_sy", [P, CC, P])
        pT = c.ps("p1_pT", [P, KD, P])
        pN = c.ps("p1_pN", [P, 3, 512])
        pQ = c.ps("p1_pQ", [P, 3, 4, P])

        consts_in = s.sem("p1_consts_in")
        w_in = [s.sem(f"p1_w_in{n}") for n in range(2)]
        state_in = s.sem("p1_state_in")
        x_in = [s.sem(f"p1_x_in{u}") for u in range(2)]
        eps_ready = s.sem("p1_eps_ready")
        rs_ready = s.sem("p1_rs_ready")
        u_ready = s.sem("p1_u_ready")
        u_turned = s.sem("p1_u_turned")
        uT_ready = s.sem("p1_uT_ready")
        nat_done = s.sem("p1_nat_done")
        nat_out = s.sem("p1_nat_out")
        nat_stored = s.sem("p1_nat_stored")
        qkv_done = s.sem("p1_qkv_done")
        qkv_out = s.sem("p1_qkv_out")
        conv_done = s.sem("p1_conv_done")
        silu_done = s.sem("p1_silu_done")
        y_stored = s.sem("p1_y_stored")
        tails_ready = s.sem("p1_tails_ready")
        tails_stored = s.sem("p1_tails_stored")
        cols = [(0, ZW), (ZW, LW), (ZW + LW, TW)]

        with nc.Block() as block:

            @block.sync
            def _(sp):
                def load(t, u):
                    sp.dma_start(xb[:, u, :], d["x"][t]).then_inc(x_in[u], 16)

                load(0, 0)
                load(1, 1)
                sp.dma_start(ident[:], d["ident"]).then_inc(consts_in, 16)
                sp.dma_start(g_bc[:], d["g_mix"].partition_broadcast(P)).then_inc(consts_in, 16)
                sp.dma_start(cw[:], d["conv_w"]).then_inc(consts_in, 16)
                sp.dma_start(wn[:], d["w_nat"]).then_inc(w_in[0], 16)
                sp.dma_start(wq[:], d["w_qkv"]).then_inc(w_in[1], 16)
                sp.dma_start(sc[:], d["state_conv"]).then_inc(state_in, 16)

                def reload(t, u):
                    sp.wait_ge(u_ready, t + 1)
                    load(t + 2, u)

                def store(t, u, r):
                    sp.wait_ge(nat_out, 3 * t + 3)
                    sp.dma_start(d["nat"][t], nat[:]).then_inc(nat_stored, 16)
                    sp.wait_ge(silu_done, t + 1)
                    sp.dma_start(d["yT"][t], sy[:]).then_inc(y_stored, 16)

                def step(t, u, r):
                    reload(t + 1, 1 - u)
                    store(t, u, r)

                reload(0, 0)
                tiles(sp, TP - 2, step)
                store(TP - 2, 0, 0)
                store(TP - 1, 1, 0)
                sp.dma_start(d["conv_p"], qx[:, :, P:P + 3]).then_inc(tails_stored, 16)
                sp.wait_ge(tails_ready, 1)
                sp.dma_start(d["conv_s"], sc[:]).then_inc(tails_stored, 16)
                store(TP, 0, 0)
                sp.wait_ge(nat_stored, 16 * NT)
                sp.wait_ge(y_stored, 16 * NT)
                sp.wait_ge(tails_stored, 32)

            @block.scalar
            def _(act):
                def norm(t, u, r):
                    act.wait_ge(x_in[u], 16 * r + 16)
                    act.activation(sq[:], xb[:, u, :], ACT.Square, accum_out=ss[:, u:u + 1])
                    act.drain()
                    act.activation(ss[:, u:u + 1], ss[:, u:u + 1], ACT.Sqrt, bias=eps[:], scale=1.0 / D).then_inc(rs_ready, 1)

                def turned(t, u):
                    act.wait_ge(u_turned, t + 1)
                    for a in range(2):
                        act.copy(uT[:, u, 4 * a:4 * a + 4, :], pT[:, 4 * a:4 * a + 4, :]).then_inc(uT_ready, 1)

                def out(t, u, r):
                    act.wait_ge(nat_stored, 16 * t)
                    for n, (at, w) in enumerate(cols):
                        act.wait_ge(nat_done, 3 * t + n + 1)
                        act.copy(nat[:, at:at + w], pN[:, n, 0:w]).then_inc(nat_out, 1)
                    act.wait_ge(conv_done, t + 1)
                    act.wait_ge(y_stored, 16 * t)
                    act.activation(sy[:], cy[:], ACT.Silu).then_inc(silu_done, 1)

                act.wait_ge(eps_ready, 1)
                norm(0, 0, 0)
                norm(1, 1, 0)
                turned(0, 0)

                def step(t, u, r, ahead=True):
                    if ahead:
                        norm(t + 2, u, r + 1)
                    act.wait_ge(qkv_done, 3 * t)
                    turned(t + 1, 1 - u)
                    out(t, u, r)

                tiles(act, TP - 2, step)
                step(TP - 2, 0, TP // 2 - 1)
                step(TP - 1, 1, TP // 2 - 1, False)
                out(TP, 0, TP // 2)

            @block.vector
            def _(dve):
                def norm(t, u, r):
                    dve.wait_ge(rs_ready, t + 1)
                    dve.reciprocal(ss[:, u:u + 1], ss[:, u:u + 1])
                    dve.drain()
                    if not (isinstance(t, int) and t < 2):
                        dve.wait_ge(u_turned, t - 1)
                    dve.scalar_tensor_tensor(un[:, u], xb[:, u, :], ss[:, u:u + 1], g_bc[:],
                                             ALU.mult, ALU.mult).then_inc(u_ready, 1)

                def conv(t, taps, view, width):
                    dve.wait_ge(silu_done, t)
                    for j in range(4):
                        for k in range(CC):
                            if j == 0:
                                i = dve.tensor_scalar(view(k), taps(k, 0), cw[:, k, 0:1], None, ALU.mult)
                            else:
                                i = dve.scalar_tensor_tensor(view(k), taps(k, j), cw[:, k, j:j + 1], view(k),
                                                             ALU.mult, ALU.add)
                        if j < 3:
                            dve.drain()
                    i.then_inc(conv_done, 1)

                def step(t, u, r, ahead=True):
                    if ahead:
                        norm(t + 2, u, r + 1)
                    dve.tensor_copy(qx[:, :, 0:3], qx[:, :, P:P + 3])
                    dve.drain()
                    for g in range(3):
                        dve.wait_ge(qkv_done, 3 * t + g + 1)
                        dve.tensor_copy(qx[:, 4 * g:4 * g + 4, 3:P + 3], pQ[:, g]).then_inc(qkv_out, 1)
                    dve.drain()
                    conv(t, lambda k, j: qx[:, k, j:j + P], lambda k: cy[:, k, :], P)

                dve.memset(eps[:], EPS).then_inc(eps_ready, 1)
                dve.memset(qx[:, :, P:P + 3], 0.0)
                dve.wait_ge(consts_in, 48)
                norm(0, 0, 0)
                norm(1, 1, 0)
                tiles(dve, TP - 2, step)
                step(TP - 2, 0, TP // 2 - 1)
                step(TP - 1, 1, TP // 2 - 1, False)
                dve.wait_ge(state_in, 16)
                dve.tensor_copy(qs[:, :, :, 0:3], sc[:])
                for g in range(3):
                    dve.wait_ge(qkv_done, 3 * TP + g + 1)
                    dve.tensor_copy(qs[:, 4 * g:4 * g + 4, :, 3:ST + 3],
                                    pQ[:, g, :, 0:SR].rearrange("p c (b t) -> p c b t", b=SB)).then_inc(qkv_out, 1)
                dve.wait_ge(silu_done, TP)
                dve.memset(cy[:, :, SR:P], 0.0)
                dve.drain()
                dve.tensor_copy(sc[:], qs[:, :, :, ST:ST + 3]).then_inc(tails_ready, 1)
                conv(TP, lambda k, j: qs[:, k, :, j:j + ST],
                     lambda k: cy[:, k, 0:SR].rearrange("p (b t) -> p b t", b=SB), SR)

            @block.tensor
            def _(pe):
                def turn(t, u, r):
                    pe.wait_ge(u_ready, t + 1)
                    pe.wait_ge(uT_ready, 2 * t)
                    for k in range(KD):
                        i = pe.transpose(pT[:, k, :], un[:, u, k * P:(k + 1) * P], ident[:])
                    i.then_inc(u_turned, 1)

                def products(t, u, r):
                    pe.wait_ge(uT_ready, 2 * t + 2)
                    pe.wait_ge(nat_out, 3 * t)
                    for n, (at, w) in enumerate(cols):
                        for k in range(KD):
                            i = pe.matmul(pN[:, n, 0:w], uT[:, u, k, :], wn[:, k, at:at + w],
                                          start=(k == 0), stop=(k == KD - 1))
                        i.then_inc(nat_done, 1)
                    pe.wait_ge(w_in[1], 16)
                    pe.wait_ge(qkv_out, 3 * t)
                    for g in range(3):
                        for m in range(4):
                            ch = (4 * g + m) * P
                            for k in range(KD):
                                i = pe.matmul(pQ[:, g, m, :], wq[:, k, ch:ch + P], uT[:, u, k, :],
                                              start=(k == 0), stop=(k == KD - 1))
                        i.then_inc(qkv_done, 1)

                pe.wait_ge(consts_in, 48)
                turn(0, 0, 0)
                pe.wait_ge(w_in[0], 16)

                def step(t, u, r):
                    turn(t + 1, 1 - u, r)
                    products(t, u, r)

                tiles(pe, TP, step)
                products(TP, 0, TP // 2)


def phase_gdn(nc, d):
    with ExitStack() as st, Semaphores(nc) as s:
        c = Ctx(nc, st)
        W4 = [P, H, P]
        HH = H // 2
        ident = c.sb("p2_ident", [P, P])
        tri2 = c.sb("p2_tri", [P, 2, P])
        same2 = c.sb("p2_same", [P, 2, P])
        levels = c.sb("p2_levels", [P, LV, P])
        norm_bc = c.sb("p2_norm", [P, P])
        rows_b = c.sb("p2_rows_b", [P, SB])
        dt_bc = c.sb("p2_dt", [P, H])
        ea_bc = c.sb("p2_ea", [P, H])
        eps = c.sb("p2_eps", [P, 1])
        y = c.sb("p2_y", [P, 2, CC, P])
        zb = c.sb("p2_z", [P, 2, ZW + 2 * H])
        sq = c.sb("p2_sq", [P, 2, H, P])
        rn = c.sb("p2_rn", [P, 2 * H])
        qn = c.sb("p2_qn", W4)
        kn = c.sb("p2_kn", W4)
        kb = c.sb("p2_kb", W4)
        beta = c.sb("p2_beta", [P, H])
        g = c.sb("p2_g", [P, H])
        t0 = c.sb("p2_t0", [P, H])
        t1 = c.sb("p2_t1", [P, H])
        gb = c.sb("p2_gb", W4)
        gc = c.sb("p2_gc", [P, 2 * H])
        eg = c.sb("p2_eg", [P, H])
        ek = c.sb("p2_ek", [P, H])
        bg = c.sb("p2_bg", [P, H])
        dec = c.sb("p2_dec", W4)
        qT = c.sb("p2_qT", W4)
        kT = c.sb("p2_kT", W4)
        kbT = c.sb("p2_kbT", W4)
        vb = c.sb("p2_vb", [P, 2, H, P])
        egrow = c.sb("p2_egrow", [P, 2, H, P])
        qgT = c.sb("p2_qgT", [P, 2, H, P])
        kbg = c.sb("p2_kbg", [P, 2, H, P])
        kd = c.sb("p2_kd", [P, 2, H, P])
        QKT = c.sb("p2_QKT", [P, 2, H, P])
        ez = c.sb("p2_ez", [P, 2, H, P])
        LT = c.sb("p2_LT", W4)
        CT = c.sb("p2_CT", [P, 2, H, P])
        Wm = c.sb("p2_W", W4)
        X = c.sb("p2_X", [P, 2, 2, HH, P])
        nwT = c.sb("p2_nwT", W4)
        vn = c.sb("p2_vn", W4)
        S = c.sb("p2_S", W4)
        Ss = c.sb("p2_Ss", [P, SB, H, P])
        kdb = c.sb("p2_kdb", W4)
        vnT = c.sb("p2_vnT", W4)
        o = c.sb("p2_o", W4)
        sqo = c.sb("p2_sqo", W4)
        rno = c.sb("p2_rno", [P, H])
        o1 = c.sb("p2_o1", W4)
        oT = c.sb("p2_oT", W4)
        bank = [c.ps(f"p2_bank{n}", W4) for n in range(8)]

        def T(h):
            return X[:, h // HH, 0, h % HH]

        def TT(h):
            return X[:, h // HH, 1, h % HH]

        consts_in = s.sem("p2_consts_in")
        state_in = s.sem("p2_state_in")
        tile_in = [s.sem(f"p2_tile_in{u}") for u in range(2)]
        out_stored = s.sem("p2_out_stored")
        state_stored = s.sem("p2_state_stored")
        pe_raw_qk = s.sem("p2_pe_raw_qk")
        pe_raw_v = s.sem("p2_pe_raw_v")
        pe_sums = s.sem("p2_pe_sums")
        pe_rows = s.sem("p2_pe_rows")
        pe_turned = s.sem("p2_pe_turned")
        pe_grams = s.sem("p2_pe_grams")
        pe_wT = s.sem("p2_pe_wT")
        pe_v_new = s.sem("p2_pe_v_new")
        pe_out = s.sem("p2_pe_out")
        pe_state = s.sem("p2_pe_state")
        pe_oT = s.sem("p2_pe_oT")
        dve_gates = s.sem("p2_dve_gates")
        dve_g = s.sem("p2_dve_g")
        dve_qk_sums = s.sem("p2_dve_qk_sums")
        dve_gc = s.sem("p2_dve_gc")
        dve_normed = s.sem("p2_dve_normed")
        dve_vb = s.sem("p2_dve_vb")
        dve_dec_in = s.sem("p2_dve_dec_in")
        dve_qkT = s.sem("p2_dve_qkT")
        dve_ez = s.sem("p2_dve_ez")
        dve_LT = s.sem("p2_dve_LT")
        dve_QKT = s.sem("p2_dve_QKT")
        dve_nwT = s.sem("p2_dve_nwT")
        dve_vn = s.sem("p2_dve_vn")
        dve_S = s.sem("p2_dve_S")
        dve_o_sums = s.sem("p2_dve_o_sums")
        dve_o_normed = s.sem("p2_dve_o_normed")
        dve_oT = s.sem("p2_dve_oT")
        act_softplus = s.sem("p2_act_softplus")
        act_squares = s.sem("p2_act_squares")
        act_roots = s.sem("p2_act_roots")
        act_egrow = s.sem("p2_act_egrow")
        act_decay = s.sem("p2_act_decay")
        act_kbT = s.sem("p2_act_kbT")
        act_ez = s.sem("p2_act_ez")
        act_o = s.sem("p2_act_o")
        act_o_squares = s.sem("p2_act_o_squares")
        act_o_root = s.sem("p2_act_o_root")
        pool_kb = s.sem("p2_pool_kb")
        pool_kd = s.sem("p2_pool_kd")
        pool_gate = s.sem("p2_pool_gate")
        w_done = [s.sem(f"p2_w_done{a}") for a in range(2)]
        X_ready = [s.sem(f"p2_X_ready{a}") for a in range(2)]
        C_ready = s.sem("p2_C_ready")
        x_done = [s.sem(f"p2_x_done{a}") for a in range(2)]
        W_ready = [s.sem(f"p2_W_ready{a}") for a in range(2)]
        s_turned_in = s.sem("p2_s_turned_in")
        s_turned_out = s.sem("p2_s_turned_out")
        s_state_pe = s.sem("p2_s_state_pe")
        s_state_dve = s.sem("p2_s_state_dve")
        s_state_kd = s.sem("p2_s_state_kd")

        def steps(eng, step):
            step(False, True, 0, 0, 0)
            with eng.Fori(0, TP // 2 - 1) as r:
                for a in range(2):
                    step(True, True, r * 2 + (a + 1), 1 - a, r + a)
            step(True, True, TP - 1, 1, TP // 2 - 1)
            step(True, False, TP, 0, TP // 2)

        def is_sample(t):
            return isinstance(t, int) and t == TP

        def count(t):
            return 3 if is_sample(t) else LV

        with nc.Block() as block:

            @block.sync
            def _(sp):
                def load(t, u):
                    sp.dma_start(y[:, u], d["yT"][t]).then_inc(tile_in[u], 16)
                    sp.dma_start(zb[:, u, 0:ZW], d["nat"][t, :, 0:ZW]).then_inc(tile_in[u], 16)
                    sp.dma_start(zb[:, u, ZW:ZW + 2 * H],
                                 d["nat"][t, :, ZW + LW + RO:NW]).then_inc(tile_in[u], 16)

                load(0, 0)
                for dst, src in ((ident, d["ident"]), (tri2, d["tri"]), (same2, d["same"]), (levels, d["levels"]),
                                 (rows_b, d["batch_rows"]), (norm_bc, d["gdn_norm"].partition_broadcast(P)),
                                 (dt_bc, d["dt_bias"].partition_broadcast(P)),
                                 (ea_bc, d["a_log"].partition_broadcast(P))):
                    sp.dma_start(dst[:], src).then_inc(consts_in, 16)
                load(1, 1)
                sp.dma_start(Ss[:], d["state"]).then_inc(state_in, 16)

                def store(t):
                    sp.wait_ge(dve_oT, t + 1)
                    sp.dma_start(d["oT"][t, :, 0:H], oT[:]).then_inc(out_stored, 16)

                def step(p, n, t, u, q):
                    if not (isinstance(t, int) and t > TP - 2):
                        sp.wait_ge(pool_gate, t + 1)
                        sp.wait_ge(dve_qk_sums, t + 1)
                        load(t + 2, u)
                    if p:
                        store(t - 1)

                steps(sp, step)
                sp.dma_start(d["gdn_p"], S[:]).then_inc(state_stored, 16)
                store(TP)
                sp.dma_start(d["gdn_s"], Ss[:]).then_inc(state_stored, 16)
                sp.wait_ge(out_stored, 16 * NT)
                sp.wait_ge(state_stored, 32)

            @block.scalar
            def _(act):
                def gates(t, u, q):
                    act.wait_ge(tile_in[u], 48 * q + 48)
                    act.wait_ge(dve_gates, t + 1)
                    act.activation(t0[:], zb[:, u, ZW:ZW + H], ACT.Exp, scale=-1.0)
                    act.activation(t1[:], t1[:], ACT.Exp)
                    act.drain()
                    act.activation(t1[:], t1[:], ACT.Ln, bias=1.0).then_inc(act_softplus, 1)

                def squares(t):
                    act.wait_ge(pe_raw_qk, t + 1)
                    for a in range(2):
                        i = act.activation(sq[:, a], bank[4 + a][:], ACT.Square)
                    i.then_inc(act_squares, 1)

                def roots(t):
                    act.wait_ge(dve_qk_sums, t + 1)
                    act.activation(rn[:], rn[:], ACT.Sqrt, bias=eps[:]).then_inc(act_roots, 1)

                def growth(t, u):
                    act.wait_ge(pe_rows, t + 1)
                    act.activation(egrow[:, u], bank[7][:], ACT.Exp).then_inc(act_egrow, 1)

                def decay(t):
                    act.wait_ge(dve_dec_in, t + 1)
                    act.activation(eg[:], gc[:, 0:H], ACT.Exp)
                    act.activation(ek[:], ek[:], ACT.Exp)
                    act.activation(dec[:], dec[:], ACT.Exp).then_inc(act_decay, 1)
                    act.wait_ge(pe_turned, t + 1)
                    act.copy(kbT[:], bank[6][:]).then_inc(act_kbT, 1)

                def exp_z(t, u, before):
                    if before:
                        act.wait_ge(dve_o_normed, t - 1)
                    act.activation(ez[:, u].rearrange("p h n -> p (h n)"), zb[:, u, 0:ZW], ACT.Exp,
                                   scale=-1.0).then_inc(act_ez, 1)

                def level(t, l):
                    for a in range(2):
                        act.wait_ge(w_done[a], LV * t + (l + 1))
                        act.copy(Wm[:, HH * a:HH * a + HH], bank[a][:, 0:HH]).then_inc(W_ready[a], 1)

                def square_o(t):
                    act.activation(sqo[:], o[:], ACT.Square).then_inc(act_o_squares, 1)

                def root_o(t):
                    act.wait_ge(dve_o_sums, t + 1)
                    act.activation(rno[:], rno[:], ACT.Sqrt, bias=eps[:], scale=1.0 / P).then_inc(act_o_root, 1)

                def step(p, n, t, u, q):
                    nxt = (t + 1, 1 - u, q + u)
                    if p:
                        act.drain()
                        square_o(t - 1)
                    if n:
                        gates(*nxt)
                    if p:
                        root_o(t - 1)
                    if n:
                        squares(nxt[0])
                    for l in range(1, count(t)):
                        level(t, l)
                        if n and l == 2:
                            roots(nxt[0])
                        if n and l == 3:
                            growth(nxt[0], nxt[1])
                        if n and l == 4:
                            decay(nxt[0])
                        if n and l == 5:
                            exp_z(nxt[0], nxt[1], p)
                    act.wait_ge(pe_out, t + 1)
                    act.copy(o[:], bank[2][:]).then_inc(act_o, 1)

                act.wait_ge(consts_in, 16 * 9)
                act.activation(ea_bc[:], ea_bc[:], ACT.Exp)
                act.drain()
                gates(0, 0, 0)
                squares(0)
                roots(0)
                growth(0, 0)
                decay(0)
                exp_z(0, 0, False)
                steps(act, step)
                act.drain()
                square_o(TP)
                root_o(TP)

            @block.vector
            def _(dve):
                def gates_in(t, u, q):
                    dve.wait_ge(tile_in[u], 48 * q + 48)
                    dve.tensor_tensor(g[:], zb[:, u, ZW + H:ZW + 2 * H], dt_bc[:], ALU.add)
                    dve.drain()
                    dve.tensor_scalar(t1[:], g[:], -1.0, None, ALU.mult)
                    dve.drain()
                    dve.tensor_tensor(t1[:], t1[:], g[:], ALU.min).then_inc(dve_gates, 1)
                    dve.tensor_scalar(g[:], g[:], 0.0, None, ALU.max)

                def gates_out(t):
                    dve.drain()
                    dve.wait_ge(act_softplus, t + 1)
                    dve.tensor_tensor(g[:], g[:], t1[:], ALU.add)
                    dve.tensor_scalar(t0[:], t0[:], 1.0, None, ALU.add)
                    dve.drain()
                    dve.scalar_tensor_tensor(g[:], g[:], -1.0, ea_bc[:], ALU.mult, ALU.mult)
                    dve.reciprocal(beta[:], t0[:])
                    dve.drain()
                    dve.tensor_copy(gb[:], bc(g[:].unsqueeze(2), W4)).then_inc(dve_g, 1)

                def sums(t):
                    dve.wait_ge(act_squares, t + 1)
                    dve.tensor_reduce(rn[:], sq[:].rearrange("p a h n -> p (a h) n"), AX_X, ALU.add).then_inc(dve_qk_sums, 1)
                    dve.wait_ge(pe_sums, t + 1)
                    dve.tensor_copy(gc[:], bank[7][:, 0, 0:2 * H])
                    dve.drain()
                    dve.tensor_tensor(ek[:], gc[:, H:2 * H], gc[:, 0:H], ALU.subtract).then_inc(dve_gc, 1)

                def normed(t, u, before):
                    dve.wait_ge(act_roots, t + 1)
                    dve.reciprocal(rn[:], rn[:])
                    dve.drain()
                    dve.tensor_scalar(rn[:, 0:H], rn[:, 0:H], float(DK) ** -0.5, None, ALU.mult)
                    dve.drain()
                    if before:
                        dve.wait_ge(pool_kd, t)
                    dve.tensor_tensor(kn[:], bank[5][:], bc(rn[:, H:2 * H].unsqueeze(2), W4), ALU.mult)
                    dve.tensor_tensor(qn[:], bank[4][:], bc(rn[:, 0:H].unsqueeze(2), W4), ALU.mult).then_inc(dve_normed, 1)
                    dve.wait_ge(pe_raw_v, t + 1)
                    dve.tensor_tensor(vb[:, u], bank[6][:], bc(beta[:].unsqueeze(2), W4), ALU.mult).then_inc(dve_vb, 1)

                def decay_in(t):
                    dve.wait_ge(act_egrow, t + 1)
                    for h in range(H):
                        i = dve.tensor_scalar(dec[:, h], bank[7][:, h], gc[:, h:h + 1], 0.0, ALU.subtract, ALU.min)
                    i.then_inc(dve_dec_in, 1)

                def turned(t, u):
                    dve.wait_ge(pe_turned, t + 1)
                    dve.tensor_copy(kT[:], bank[5][:])
                    dve.tensor_copy(qT[:], bank[4][:]).then_inc(dve_qkT, 1)
                    dve.drain()
                    dve.tensor_tensor(qgT[:, u], qT[:], egrow[:, u], ALU.mult)

                def decay_out(t, u):
                    m = 1 if is_sample(t) else 0
                    dve.wait_ge(act_decay, t + 1)
                    dve.tensor_tensor(dec[:], dec[:], bc(tri2[:, m:m + 1], W4), ALU.mult)
                    dve.wait_ge(act_ez, t + 1)
                    dve.tensor_scalar(ez[:, u], ez[:, u], 1.0, None, ALU.add)
                    dve.drain()
                    dve.reciprocal(ez[:, u], ez[:, u]).then_inc(dve_ez, 1)

                def make_LT(t, before):
                    if before:
                        dve.wait_ge(C_ready, LV * t)
                    dve.wait_ge(pe_grams, t + 1)
                    dve.tensor_tensor(LT[:], bank[4][:], dec[:], ALU.mult).then_inc(dve_LT, 1)

                def make_QKT(t, u):
                    dve.tensor_tensor(QKT[:, u], bank[5][:], dec[:], ALU.mult).then_inc(dve_QKT, 1)

                def level(t, l):
                    dve.drain()
                    for a in range(2):
                        if l == 0:
                            dve.wait_ge(w_done[a], LV * t + 1)
                            one = bc(ident[:].unsqueeze(1), [P, HH, P])
                            dve.tensor_tensor(X[:, a, 0], one, bank[a][:, 0:HH], ALU.subtract)
                            i = dve.tensor_tensor(X[:, a, 1], one, CT[:, 0, HH * a:HH * a + HH], ALU.subtract)
                        else:
                            dve.wait_ge(x_done[a], (LV - 1) * t + l)
                            i = dve.tensor_tensor(X[:, a].rearrange("p b h n -> p (b h) n"), X[:, a].rearrange("p b h n -> p (b h) n"),
                                                  bank[2 + a][:], ALU.subtract)
                        i.then_inc(X_ready[a], 1)

                def tail_sums(t):
                    dve.wait_ge(act_o_squares, t + 1)
                    dve.tensor_reduce(rno[:], sqo[:], AX_X, ALU.add).then_inc(dve_o_sums, 1)

                def tail_norm(t, u):
                    dve.wait_ge(act_o_root, t + 1)
                    dve.reciprocal(rno[:], rno[:])
                    dve.drain()
                    dve.tensor_tensor(o1[:], o[:], bc(rno[:].unsqueeze(2), W4), ALU.mult)
                    dve.drain()
                    dve.tensor_tensor(o1[:], o1[:], ez[:, u], ALU.mult).then_inc(dve_o_normed, 1)

                def tail_out(t, before):
                    dve.wait_ge(pe_oT, t + 1)
                    if before:
                        dve.wait_ge(out_stored, 16 * t)
                    dve.tensor_copy(oT[:], bank[7][:]).then_inc(dve_oT, 1)

                def sample_core(t, u):
                    for n, b in ((0, 1), (1, 2)):
                        dve.wait_ge(s_turned_in, n + 1)
                        dve.tensor_copy(vnT[:], bank[b][:]).then_inc(s_turned_out, 1)
                        if n == 0:
                            dve.wait_ge(pe_v_new, t + 1)
                            dve.tensor_copy(vn[:], bank[1][:]).then_inc(dve_vn, 1)
                    for b in range(SB):
                        last = ST * (b + 1) - 1
                        dve.wait_ge(s_state_pe, b + 1)
                        for h in range(H):
                            i = dve.scalar_tensor_tensor(Ss[:, b, h], Ss[:, b, h], egrow[:, u, h, last:last + 1],
                                                         bank[(0, 3)[b % 2]][:, h], ALU.mult, ALU.add)
                        i.then_inc(s_state_dve, 1)

                def step(p, n, t, u, q):
                    nxt, nu = t + 1, 1 - u
                    if n:
                        gates_in(nxt, nu, q + u)
                    if p:
                        tail_sums(t - 1)
                    level(t, 0)
                    if n:
                        gates_out(nxt)
                    if p:
                        tail_norm(t - 1, nu)
                    level(t, 1)
                    if n:
                        sums(nxt)
                    level(t, 2)
                    if n:
                        normed(nxt, nu, True)
                        level(t, 3)
                        decay_in(nxt)
                        level(t, 4)
                        turned(nxt, nu)
                        level(t, 5)
                    if p:
                        tail_out(t - 1, not (isinstance(t, int) and t == 1))
                    if n:
                        decay_out(nxt, nu)
                        level(t, 6)
                    dve.wait_ge(pe_wT, t + 1)
                    dve.tensor_scalar(nwT[:], bank[0][:], -1.0, None, ALU.mult).then_inc(dve_nwT, 1)
                    if n:
                        make_LT(nxt, True)
                        dve.wait_ge(pe_v_new, t + 1)
                        dve.tensor_copy(vn[:], bank[1][:]).then_inc(dve_vn, 1)
                        make_QKT(nxt, nu)
                        dve.wait_ge(pe_state, t + 1)
                        for h in range(H):
                            i = dve.scalar_tensor_tensor(S[:, h], S[:, h], egrow[:, u, h, P - 1:P], bank[3][:, h],
                                                         ALU.mult, ALU.add)
                        i.then_inc(dve_S, 1)
                    else:
                        sample_core(t, u)

                dve.memset(eps[:], EPS)
                dve.memset(S[:], 0.0)
                dve.drain()
                dve.sem_inc(consts_in, 16)
                dve.wait_ge(consts_in, 16 * 9)
                gates_in(0, 0, 0)
                gates_out(0)
                sums(0)
                normed(0, 0, False)
                decay_in(0)
                turned(0, 0)
                decay_out(0, 0)
                make_LT(0, False)
                make_QKT(0, 0)
                dve.wait_ge(state_in, 16)
                steps(dve, step)
                tail_sums(TP)
                tail_norm(TP, 0)
                tail_out(TP, True)

            @block.gpsimd
            def _(pool):
                def blocks(t, l, before=True):
                    if l == 0 and before:
                        pool.wait_ge(w_done[1], LV * t)
                    if l == 2:
                        for a in range(2):
                            pool.wait_ge(X_ready[a], LV * t + 1)
                    if l > 2:
                        pool.wait_ge(w_done[1], LV * t + (l - 1))
                    pool.tensor_tensor(CT[:, l % 2], LT[:], bc(levels[:, l:l + 1], W4), ALU.mult).then_inc(C_ready, 1)

                def scaled_k(t):
                    pool.wait_ge(dve_normed, t + 1)
                    pool.tensor_tensor(kb[:], kn[:], bc(beta[:].unsqueeze(2), W4), ALU.mult).then_inc(pool_kb, 1)

                def rest(t, u):
                    pool.wait_ge(act_decay, t + 1)
                    pool.tensor_tensor(bg[:], beta[:], eg[:], ALU.mult)
                    pool.drain()
                    pool.tensor_tensor(kbg[:, u], kn[:], bc(bg[:].unsqueeze(2), W4), ALU.mult)
                    pool.tensor_tensor(kd[:, u], kn[:], bc(ek[:].unsqueeze(2), W4), ALU.mult).then_inc(pool_kd, 1)
                    pool.wait_ge(dve_ez, t + 1)
                    pool.tensor_tensor(ez[:, u], ez[:, u], bc(norm_bc[:].unsqueeze(1), W4), ALU.mult)
                    pool.drain()
                    flat = ez[:, u].rearrange("p h n -> p (h n)")
                    pool.tensor_tensor(flat, flat, zb[:, u, 0:ZW], ALU.mult).then_inc(pool_gate, 1)

                def step(p, n, t, u, q):
                    for l in range(1, count(t)):
                        blocks(t, l)
                        if n and l == 3:
                            scaled_k(t + 1)
                    if n:
                        rest(t + 1, 1 - u)
                        pool.wait_ge(dve_LT, t + 2)
                        blocks(t + 1, 0)
                    else:
                        for b in range(SB):
                            if b:
                                pool.wait_ge(s_state_pe, b)
                            else:
                                pool.drain()
                            pool.tensor_scalar(kdb[:], kd[:, u], rows_b[:, b:b + 1], None, ALU.mult).then_inc(s_state_kd, 1)

                pool.wait_ge(consts_in, 16 * 9)
                scaled_k(0)
                rest(0, 0)
                pool.wait_ge(dve_LT, 1)
                blocks(0, 0, False)
                steps(pool, step)

            @block.tensor
            def _(pe):
                def heads(dst, lhs, rhs, hs=range(H), **k):
                    for h in hs:
                        i = pe.matmul(dst(h), lhs(h), rhs(h), **({"start": True, "stop": True} | k))
                    return i

                def raw(t, u, q, before):
                    pe.wait_ge(tile_in[u], 48 * q + 48)
                    if before:
                        pe.wait_ge(dve_QKT, t)
                    for a in range(3):
                        for h in range(H):
                            i = pe.transpose(bank[4 + a][:, h], y[:, u, H * a + h], ident[:])
                        if a:
                            i.then_inc(pe_raw_qk if a == 1 else pe_raw_v, 1)

                def sums(t):
                    m = 1 if is_sample(t) else 0
                    pe.wait_ge(dve_g, t + 1)
                    pe.matmul(bank[7][:, 0, 0:H], tri2[:, m], g[:], start=True, stop=True)
                    pe.matmul(bank[7][:, 0, H:2 * H], same2[:, m], g[:], start=True, stop=True).then_inc(pe_sums, 1)

                def rows(t):
                    m = 1 if is_sample(t) else 0
                    pe.wait_ge(dve_gc, t + 1)
                    heads(lambda h: bank[7][:, h], lambda h: gb[:, h], lambda h: tri2[:, m]).then_inc(pe_rows, 1)

                def turned(t):
                    pe.wait_ge(dve_vb, t + 1)
                    pe.wait_ge(pool_kb, t + 1)
                    for b, src in ((4, qn), (5, kn), (6, kb)):
                        for h in range(H):
                            i = pe.transpose(bank[b][:, h], src[:, h], ident[:])
                    i.then_inc(pe_turned, 1)

                def grams(t):
                    pe.wait_ge(dve_qkT, t + 1)
                    pe.wait_ge(act_kbT, t + 1)
                    heads(lambda h: bank[4][:, h], lambda h: kT[:, h], lambda h: kbT[:, h])
                    heads(lambda h: bank[5][:, h], lambda h: kT[:, h], lambda h: qT[:, h]).then_inc(pe_grams, 1)

                def level(t, l, before):
                    for a in range(2):
                        pe.wait_ge(C_ready, LV * t + (l + 1))
                        if l:
                            pe.wait_ge(X_ready[a], LV * t + l)
                        heads(lambda h: bank[a][:, h % HH], lambda h: CT[:, l % 2, h], (lambda h: T(h)) if l else (lambda h: ident[:]),
                              range(HH * a, HH * a + HH)).then_inc(w_done[a], 1)
                    if l:
                        if l == 1 and before:
                            pe.wait_ge(act_o, t)
                            pe.wait_ge(dve_S, t)
                        for a in range(2):
                            pe.wait_ge(W_ready[a], (LV - 1) * t + l)
                            half = range(HH * a, HH * a + HH)
                            heads(lambda h: bank[2 + a][:, h % HH], TT, lambda h: Wm[:, h], half)
                            heads(lambda h: bank[2 + a][:, HH + h % HH], lambda h: Wm[:, h], TT, half).then_inc(x_done[a], 1)

                def tail(t, fronts):
                    pe.wait_ge(dve_o_normed, t + 1)
                    pe.wait_ge(dve_dec_in, fronts)
                    for h in range(H):
                        i = pe.transpose(bank[7][:, h], o1[:, h], ident[:])
                    i.then_inc(pe_oT, 1)

                def core(t, u):
                    pe.wait_ge(dve_nwT, t + 1)
                    for h in range(H):
                        pe.matmul(bank[1][:, h], TT(h), vb[:, u, h], start=True, stop=False)
                        i = pe.matmul(bank[1][:, h], nwT[:, h], S[:, h], start=False, stop=True)
                    i.then_inc(pe_v_new, 1)
                    pe.wait_ge(dve_vn, t + 1)
                    pe.wait_ge(dve_QKT, t + 1)
                    for h in range(H):
                        pe.matmul(bank[2][:, h], qgT[:, u, h], S[:, h], start=True, stop=False)
                        i = pe.matmul(bank[2][:, h], QKT[:, u, h], vn[:, h], start=False, stop=True)
                    i.then_inc(pe_out, 1)
                    heads(lambda h: bank[3][:, h], lambda h: kd[:, u, h], lambda h: vn[:, h]).then_inc(pe_state, 1)

                def sample_core(t, u):
                    def by_batch(n, b, lhs, rhs, cols_of, done):
                        for h in range(H):
                            pe.matmul(bank[b][:, h], lhs(h), rhs(h), start=True, stop=False, skip_group_check=True)
                            for k in range(SB):
                                cols = slice(ST * k, ST * k + ST)
                                i = pe.matmul(bank[b][:, h, cols], Ss[:, k, h], cols_of(h)[:, cols],
                                              start=False, stop=(k == SB - 1), skip_group_check=True)
                        i.then_inc(s_turned_in, 1)
                        pe.wait_ge(s_turned_out, n + 1)
                        for h in range(H):
                            i = pe.transpose(bank[b][:, h], vnT[:, h], ident[:])
                        i.then_inc(done, 1)

                    pe.wait_ge(dve_nwT, t + 1)
                    by_batch(0, 1, lambda h: vb[:, u, h], TT, lambda h: nwT[:, h], pe_v_new)
                    pe.wait_ge(dve_vn, t + 1)
                    by_batch(1, 2, lambda h: vn[:, h], lambda h: QKT[:, u, h], lambda h: qgT[:, u, h], pe_out)
                    for b in range(SB):
                        pe.wait_ge(s_state_kd, b + 1)
                        if b >= 2:
                            pe.wait_ge(s_state_dve, b - 1)
                        heads(lambda h: bank[(0, 3)[b % 2]][:, h], lambda h: kdb[:, h], lambda h: vn[:, h]).then_inc(s_state_pe, 1)

                def step(p, n, t, u, q):
                    nxt, nu = t + 1, 1 - u
                    level(t, 0, p)
                    if n:
                        raw(nxt, nu, q + u, True)
                    level(t, 1, p)
                    if n:
                        sums(nxt)
                    level(t, 2, p)
                    if n:
                        rows(nxt)
                        level(t, 3, p)
                        turned(nxt)
                        level(t, 4, p)
                    if p:
                        tail(t - 1, t + 2 if n else NT)
                    if n:
                        level(t, 5, p)
                        grams(nxt)
                        level(t, 6, p)
                    if p:
                        pe.wait_ge(dve_oT, t)
                    for a in range(2):
                        pe.wait_ge(X_ready[a], LV * t + count(t))
                    pe.wait_ge(pool_kd, t + 1)
                    heads(lambda h: bank[0][:, h], lambda h: kbg[:, u, h], TT).then_inc(pe_wT, 1)
                    if n:
                        core(t, u)
                    else:
                        sample_core(t, u)

                pe.wait_ge(consts_in, 16 * 9)
                raw(0, 0, 0, False)
                sums(0)
                rows(0)
                turned(0)
                grams(0)
                steps(pe, step)
                tail(TP, NT)


def phase_latents(nc, d, m):
    with ExitStack() as st, Semaphores(nc) as s:
        c = Ctx(nc, st)
        KT, KR, V, QT, QR, ident = m["KT"], m["KR"], m["V"], m["QT"], m["QR"], m["ident"]
        w_uq = c.sb("p3_w_uq", [P, 2, H * (DK + RO)])
        w_uk = c.sb("p3_w_uk", [P, H, R])
        gq = c.sb("p3_gq", [P, R])
        gkv = c.sb("p3_gkv", [P, R])
        eps = c.sb("p3_eps", [P, 1])
        cs = c.sb("p3_cs", [P, 2, 2, RO // 2])
        lt = c.sb("p3_lt", [P, 2, LW + RO])
        sq = c.sb("p3_sq", [P, 2, R])
        rn = c.sb("p3_rn", [P, 2])
        cq = c.sb("p3_cq", [P, R])
        ckv = c.sb("p3_ckv", [P, R])
        kr = c.sb("p3_kr", [P, 2, RO // 2])
        tk = c.sb("p3_tk", [P, 2, RO // 2])
        cqT = c.sb("p3_cqT", [P, 2, P])
        qnT = c.sb("p3_qnT", [P, H, P])
        qr = c.sb("p3_qr", [P, H, 2, RO // 2])
        tq = c.sb("p3_tq", [P, H, 2, RO // 2])
        bank = [c.ps(f"p3_bank{n}", [P, 4, P]) for n in range(7)]

        consts_in = s.sem("p3_consts_in")
        tile_in = [s.sem(f"p3_tile_in{u}") for u in range(2)]
        rooted = s.sem("p3_rooted")
        normed = s.sem("p3_normed")
        turned = s.sem("p3_turned")
        copied = s.sem("p3_copied")
        q_done = s.sem("p3_q_done")
        qnT_ready = s.sem("p3_qnT_ready")
        qr_ready = s.sem("p3_qr_ready")
        lat_done = s.sem("p3_lat_done")
        lat_out = s.sem("p3_lat_out")
        stored = s.sem("p3_stored")
        half = RO // 2
        w_rope = w_uq[:].rearrange("p k (h n) -> p k h n", h=H)[:, :, :, DK:DK + RO]

        with nc.Block() as block:

            @block.sync
            def _(sp):
                def load(t, u):
                    sp.dma_start(lt[:, u], d["nat"][t, :, ZW:ZW + LW + RO]).then_inc(tile_in[u], 16)
                    sp.dma_start(cs[:, u, 0], d["cos"][t]).then_inc(tile_in[u], 16)
                    sp.dma_start(cs[:, u, 1], d["sin"][t]).then_inc(tile_in[u], 16)

                load(0, 0)
                load(1, 1)
                for dst, src in ((ident, d["ident"]), (w_uq, d["w_uq"]), (w_uk, d["w_uk"]),
                                 (gq, d["g_q"].partition_broadcast(P)), (gkv, d["g_kv"].partition_broadcast(P))):
                    sp.dma_start(dst[:], src).then_inc(consts_in, 16)

                def step(t, u, r, more=True):
                    sp.wait_ge(normed, t + 1)
                    sp.dma_start(d["ckv"][t], ckv[:]).then_inc(stored, 16)
                    sp.dma_start(d["krope"][t], kr[:].rearrange("p a n -> p (a n)")).then_inc(stored, 16)
                    if more:
                        sp.wait_ge(qr_ready, t + 1)
                        load(t + 2, u)

                tiles(sp, TP - 2, step)
                step(TP - 2, 0, 0)
                step(TP - 1, 1, 0, False)
                step(TP, 0, 0, False)
                sp.wait_ge(stored, 32 * NT)

            @block.scalar
            def _(act):
                def step(t, u, r):
                    act.wait_ge(tile_in[u], 48 * r + 48)
                    act.wait_ge(normed, t)
                    for a in range(2):
                        act.activation(sq[:, a], lt[:, u, R * a:R * a + R], ACT.Square, accum_out=rn[:, a:a + 1])
                    act.drain()
                    act.activation(rn[:], rn[:], ACT.Sqrt, bias=eps[:], scale=1.0 / R).then_inc(rooted, 1)
                    act.wait_ge(turned, t + 1)
                    act.copy(cqT[:], bank[0][:, 0:2])
                    act.copy(KT[:, :, bass.ds(t * P, P)], bank[0][:, 2:4])
                    act.copy(KR[:, bass.ds(t * P, P)], bank[1][0:RO, 0]).then_inc(copied, 1)
                    act.wait_ge(q_done, t + 1)
                    act.copy(qnT[:], bank[2][:]).then_inc(qnT_ready, 1)
                    act.wait_ge(lat_done, t + 1)
                    for a in range(2):
                        act.copy(QT[:, a, :, bass.ds(t * P, P)], bank[4 + a][:])
                    act.copy(QR[:, :, bass.ds(t * P, P)], bank[6][0:RO]).then_inc(lat_out, 1)

                act.wait_ge(consts_in, 16 * 6)
                tiles(act, TP, step)
                step(TP, 0, TP // 2)

            @block.vector
            def _(dve):
                def step(t, u, r):
                    cos, sin = cs[:, u, 0:1], cs[:, u, 1:2]

                    def rope(out, tmp, x, wide):
                        dve.tensor_tensor(out, x, wide(cos, 2), ALU.mult)
                        dve.tensor_tensor(tmp[0], x[..., 1:2, :], wide(sin, 1), ALU.mult)
                        dve.tensor_tensor(tmp[1], x[..., 0:1, :], wide(sin, 1), ALU.mult)
                        dve.drain()
                        dve.tensor_tensor(out[..., 0:1, :], out[..., 0:1, :], tmp[0], ALU.subtract)
                        return dve.tensor_tensor(out[..., 1:2, :], out[..., 1:2, :], tmp[1], ALU.add)

                    dve.wait_ge(rooted, t + 1)
                    dve.reciprocal(rn[:], rn[:])
                    dve.drain()
                    dve.wait_ge(turned, t)
                    dve.wait_ge(stored, 32 * t)
                    dve.scalar_tensor_tensor(cq[:], lt[:, u, 0:R], rn[:, 0:1], gq[:], ALU.mult, ALU.mult)
                    dve.scalar_tensor_tensor(ckv[:], lt[:, u, R:2 * R], rn[:, 1:2], gkv[:], ALU.mult, ALU.mult)
                    rope(kr[:], (tk[:, 0:1], tk[:, 1:2]), lt[:, u, LW:LW + RO].rearrange("p (a n) -> p a n", a=2),
                         lambda a, k: bc(a, [P, k, half])).then_inc(normed, 1)
                    dve.drain()
                    dve.tensor_copy(V[:, t, :], ckv[:])
                    dve.wait_ge(q_done, t + 1)
                    x = bank[3][:, 0:2].rearrange("p a n -> p (a n)").rearrange("p (h a n) -> p h a n", h=H, a=2)
                    rope(qr[:], (tq[:, :, 0:1], tq[:, :, 1:2]), x,
                         lambda a, k: bc(a.unsqueeze(1), [P, H, k, half])).then_inc(qr_ready, 1)

                dve.memset(eps[:], EPS)
                dve.drain()
                dve.sem_inc(consts_in, 16)
                dve.wait_ge(consts_in, 16 * 6)
                tiles(dve, TP, step)
                step(TP, 0, TP // 2)

            @block.tensor
            def _(pe):
                def step(t, u, r):
                    pe.wait_ge(normed, t + 1)
                    pe.wait_ge(lat_out, t)
                    for a in range(2):
                        pe.transpose(bank[0][:, a], cq[:, a * P:(a + 1) * P], ident[:])
                    for a in range(2):
                        pe.transpose(bank[0][:, 2 + a], ckv[:, a * P:(a + 1) * P], ident[:])
                    pe.transpose(bank[1][0:RO, 0], kr[:].rearrange("p a n -> p (a n)"), ident[:]).then_inc(turned, 1)
                    pe.wait_ge(copied, t + 1)
                    for h in range(H):
                        for k in range(2):
                            pe.matmul(bank[2][:, h], w_uq[:, k, h * (DK + RO):h * (DK + RO) + DK], cqT[:, k],
                                      start=(k == 0), stop=(k == 1))
                    for k in range(2):
                        i = pe.matmul(bank[3][:, 0:2].rearrange("p a n -> p (a n)").rearrange("p (h n) -> p h n", h=H),
                                      cqT[:, k], w_rope[:, k], start=(k == 0), stop=(k == 1))
                    i.then_inc(q_done, 1)
                    pe.wait_ge(qnT_ready, t + 1)
                    pe.wait_ge(qr_ready, t + 1)
                    for a in range(2):
                        for h in range(H):
                            pe.matmul(bank[4 + a][:, h], w_uk[:, h, a * P:(a + 1) * P], qnT[:, h], start=True, stop=True)
                    for h in range(H):
                        i = pe.transpose(bank[6][0:RO, h], qr[:, h].rearrange("p a n -> p (a n)"), ident[:])
                    i.then_inc(lat_done, 1)

                pe.wait_ge(consts_in, 16 * 6)
                tiles(pe, TP, step)
                step(TP, 0, TP // 2)


def phase_prompt_attention(nc, d, m):
    with ExitStack() as st, Semaphores(nc) as s:
        c = Ctx(nc, st)
        KT, KR, V, QT, QR, ident = m["KT"], m["KR"], m["V"], m["QT"], m["QR"], m["ident"]
        w_uv = m["w_uv"]
        causal = c.sb("p4_causal", [P, P])
        mx = c.sb("p4_mx", [P, 2])
        rs = c.sb("p4_rs", [P, 2])
        pb = c.sb("p4_pb", [P, 2, TP * P])
        dg = c.sb("p4_dg", [P, 2, P])
        pts = c.sb("p4_pts", [P, 2, TP, P])
        ols = c.sb("p4_ols", [P, 2, 2, P])
        om = c.sb("p4_om", [P, 2, H, P])
        psS = c.ps("p4_psS", [P, 2, TP * P])
        psT = c.ps("p4_psT", [P, TP, P])
        psL = c.ps("p4_psL", [P, 4, P])
        psO = c.ps("p4_psO", [P, 4, P])

        consts_in = s.sem("p4_consts_in")
        scored = s.sem("p4_scored")
        max_ready = s.sem("p4_max_ready")
        p_ready = s.sem("p4_p_ready")
        diag_ready = s.sem("p4_diag_ready")
        turned = s.sem("p4_turned")
        pt_low = s.sem("p4_pt_low")
        pt_high = s.sem("p4_pt_high")
        lat_done = s.sem("p4_lat_done")
        lat_out = s.sem("p4_lat_out")
        o_done = s.sem("p4_o_done")
        o_out = s.sem("p4_o_out")
        stored = [s.sem(f"p4_stored{u}") for u in range(2)]
        N = TP * H

        def high(n):
            return sum(1 for k in range(n + 1) if k // H >= 4)

        def each(m_, *parts):
            for lag, f in parts:
                if 0 <= m_ - lag < N:
                    f(m_ - lag)

        with nc.Block() as block:

            @block.sync
            def _(sp):
                sp.dma_start(causal[:], d["causal"]).then_inc(consts_in, 16)
                sp.dma_start(w_uv[:], d["w_uv"]).then_inc(consts_in, 16)
                for t in range(TP):
                    sp.wait_ge(o_out, H * (t + 1))
                    sp.dma_start(d["oT"][t, :, H:2 * H], om[:, t % 2]).then_inc(stored[t % 2], 16)
                for u in range(2):
                    sp.wait_ge(stored[u], 16 * TP // 2)

            @block.tensor
            def _(pe):
                def scores(n):
                    t, h = n // H, n % H
                    if n >= 2:
                        pe.wait_ge(p_ready, n - 1)
                    q = slice(t * P, (t + 1) * P)
                    for k in range(0, (t + 1) * P, 512):
                        w = min(512, (t + 1) * P - k)
                        out = psS[:, n % 2, k:k + w]
                        pe.matmul(out, QT[:, 0, h, q], KT[:, 0, k:k + w], start=True, stop=False)
                        pe.matmul(out, QT[:, 1, h, q], KT[:, 1, k:k + w], start=False, stop=False)
                        i = pe.matmul(out, QR[:, h, q], KR[:, k:k + w], start=False, stop=True)
                    i.then_inc(scored, 1)

                def turn(n):
                    pe.wait_ge(diag_ready, n + 1)
                    if n >= 1:
                        pe.wait_ge(pt_low, n)
                        if high(n - 1):
                            pe.wait_ge(pt_high, high(n - 1))
                    for b in range(n // H + 1):
                        i = pe.matmul(psT[:, b], pb[:, n % 2, b * P:(b + 1) * P], dg[:, n % 2], start=True, stop=True)
                    i.then_inc(turned, 1)

                def latent(n):
                    pe.wait_ge(pt_low, n + 1)
                    if high(n):
                        pe.wait_ge(pt_high, high(n))
                    if n >= 1:
                        pe.wait_ge(lat_out, n)
                    for a in range(2):
                        for b in range(n // H + 1):
                            i = pe.matmul(psL[:, a], V[:, b, a * P:(a + 1) * P], pts[:, n % 2, b],
                                          start=(b == 0), stop=(b == n // H))
                    i.then_inc(lat_done, 1)

                def out(n):
                    h = n % H
                    pe.wait_ge(lat_out, n + 1)
                    if n >= 1:
                        pe.wait_ge(o_out, n)
                    for a in range(2):
                        i = pe.matmul(psO[:, 0], w_uv[:, a, h * DK:(h + 1) * DK], ols[:, n % 2, a],
                                      start=(a == 0), stop=(a == 1))
                    i.then_inc(o_done, 1)

                pe.wait_ge(consts_in, 32)
                for k in range(N + 3):
                    each(k, (0, scores), (1, turn), (2, latent), (3, out))

            @block.vector
            def _(dve):
                def diag(n):
                    dve.wait_ge(p_ready, n + 1)
                    dve.reciprocal(rs[:, n % 2:n % 2 + 1], rs[:, n % 2:n % 2 + 1])
                    dve.drain()
                    if n >= 2:
                        dve.wait_ge(turned, n - 1)
                    dve.tensor_scalar(dg[:, n % 2], ident[:], rs[:, n % 2:n % 2 + 1], None, ALU.mult).then_inc(diag_ready, 1)

                def row_max(n):
                    t, u = n // H, n % 2
                    dve.wait_ge(scored, n + 1)
                    last = psS[:, u, t * P:(t + 1) * P]
                    dve.tensor_tensor(last, last, causal[:], ALU.add)
                    dve.drain()
                    dve.tensor_reduce(mx[:, u:u + 1], psS[:, u, 0:(t + 1) * P], AX_X, ALU.max)
                    dve.drain()
                    dve.tensor_scalar(mx[:, u:u + 1], mx[:, u:u + 1], -MLA_SCALE, None, ALU.mult).then_inc(max_ready, 1)

                def low(n):
                    w = min(4, n // H + 1)
                    dve.wait_ge(turned, n + 1)
                    if n >= 2:
                        dve.wait_ge(lat_done, n - 1)
                    dve.tensor_copy(pts[:, n % 2, 0:w], psT[:, 0:w]).then_inc(pt_low, 1)

                def lat(n):
                    dve.wait_ge(lat_done, n + 1)
                    if n >= 2:
                        dve.wait_ge(o_done, n - 1)
                    dve.tensor_copy(ols[:, n % 2], psL[:, 0:2]).then_inc(lat_out, 1)

                dve.wait_ge(consts_in, 32)
                for k in range(N + 3):
                    each(k, (1, diag), (0, row_max), (1, low), (2, lat))

            @block.scalar
            def _(act):
                def exp(n):
                    t, u = n // H, n % 2
                    act.wait_ge(max_ready, n + 1)
                    if n >= 2:
                        act.wait_ge(turned, n - 1)
                    act.activation(pb[:, u, 0:(t + 1) * P], psS[:, u, 0:(t + 1) * P], ACT.Exp, bias=mx[:, u:u + 1],
                                   scale=MLA_SCALE, accum_out=rs[:, u:u + 1]).then_inc(p_ready, 1)

                def high_blocks(n):
                    t = n // H
                    if t < 4:
                        return
                    act.wait_ge(turned, n + 1)
                    act.wait_ge(lat_done, n - 1)
                    act.copy(pts[:, n % 2, 4:t + 1], psT[:, 4:t + 1]).then_inc(pt_high, 1)

                def out(n):
                    t, h = n // H, n % H
                    act.wait_ge(o_done, n + 1)
                    if t >= 2 and h == 0:
                        act.wait_ge(stored[t % 2], 16 * (t // 2))
                    act.copy(om[:, t % 2, h], psO[:, 0]).then_inc(o_out, 1)

                for k in range(N + 3):
                    each(k, (0, exp), (1, high_blocks), (3, out))


def mla_tensors(c):
    return {
        "KT": c.sb("mla_KT", [P, 2, NT * P]), "KR": c.sb("mla_KR", [RO, NT * P]), "V": c.sb("mla_V", [P, NT, R]),
        "QT": c.sb("mla_QT", [P, 2, H, NT * P]), "QR": c.sb("mla_QR", [RO, H, NT * P]),
        "ident": c.sb("mla_ident", [P, P]), "w_uv": c.sb("mla_w_uv", [P, 2, H * DK]),
    }


def phase_sample_attention(nc, d, m):
    G, J, PC = 2, 4, 4
    NC = NPAGE // PC
    CK = PC * PAGE
    HT = H * ST
    with ExitStack() as st, Semaphores(nc) as s:
        c = Ctx(nc, st)
        KT, KR, V, QT, QR, ident, w_uv = (m[n] for n in ("KT", "KR", "V", "QT", "QR", "ident", "w_uv"))
        n_pool = d["cache"].shape[0]
        KW = R + PAGE // 2
        pages = c.sb("p5_pages", [1, G * NC * J * PC], I32)
        mask = c.sb("p5_mask", [P, G, SR])
        ring = c.sb("p5_ring", [P, 2, J * PC * KW])
        kt = [ring[:, u].rearrange("p (j q w) -> p j q w", j=J, q=PC) for u in range(2)]
        vt = [ring[:, u, 0:J * PC * R].rearrange("p (j q w) -> p j q w", j=J, q=PC) for u in range(2)]
        S = c.sb("p5_S", [P, NC * CK + SR])
        qg = c.sb("p5_qg", [P, G, 2, J, HT])
        qr = c.sb("p5_qr", [P, G, 2, J, HT])
        mxc = c.sb("p5_mxc", [P, NC + 1])
        nm = c.sb("p5_nm", [P, 1])
        sums = c.sb("p5_sums", [P, NC + 1])
        den = c.sb("p5_den", [P, 1])
        pb = c.sb("p5_pb", [P, 2, CK])
        pts = c.sb("p5_pts", [P, 2, PC, P])
        acc = c.sb("p5_acc", [P, R])
        ols = c.sb("p5_ols", [P, 2, P])
        om = c.sb("p5_om", [P, H, P])
        psS = c.ps("p5_psS", [P, 2, 512])
        psT = c.ps("p5_psT", [P, 2, PC, P])
        psV = c.ps("p5_psV", [P, 2, 512])
        psO = c.ps("p5_psO", [P, H, P])

        consts_in = s.sem("p5_consts_in")
        pages_in = s.sem("p5_pages_in")
        q_ready = s.sem("p5_q_ready")
        chunk_in = [s.sem(f"p5_chunk_in{u}") for u in range(2)]
        chunk_used = s.sem("p5_chunk_used")
        scored = s.sem("p5_scored")
        kept = s.sem("p5_kept")
        max_ready = s.sem("p5_max_ready")
        p_ready = s.sem("p5_p_ready")
        turned = s.sem("p5_turned")
        pt_ready = s.sem("p5_pt_ready")
        pv_done = s.sem("p5_pv_done")
        added = s.sem("p5_added")
        acc_ready = s.sem("p5_acc_ready")
        acc_turned = s.sem("p5_acc_turned")
        ols_ready = s.sem("p5_ols_ready")
        o_done = s.sem("p5_o_done")
        o_out = s.sem("p5_o_out")
        stored = s.sem("p5_stored")
        KS = NC + 1

        def chunks(eng, n, body, base=0):
            with eng.Fori(0, n // 2) as r:
                for u in range(2):
                    body(r * 2 + (u + base), u, r + base // 2)

        halves = {nc.sync: range(J // 2), nc.scalar: range(J // 2, J)}

        def load(eng, g, second, c_, u):
            for j in halves[eng]:
                ids = [eng.value_load(pages[0:1, bass.ds((c_ + NC * g) * (J * PC) + (j * PC + q), 1)],
                                      min_val=0, max_val=n_pool - 1) for q in range(PC)]
                for q, page in enumerate(ids):
                    if second:
                        eng.dma_start(vt[u][:, j, q], d["cache"][page]).then_inc(chunk_in[u], 16)
                    else:
                        eng.dma_start(kt[u][:, j, q], d["cacheT"][page]).then_inc(chunk_in[u], 16)

        def reload(eng, g, second, c_, u):
            eng.wait_ge(chunk_used, c_ + (NC * (2 * g + second) - 1))
            load(eng, g, second, c_, u)

        with nc.Block() as block:

            @block.sync
            def _(sp):
                sp.dma_start(pages[:], d["pages"]).then_inc(pages_in, 16)
                sp.dma_start(mask[:], d["new_mask"]).then_inc(consts_in, 16)
                sp.wait_ge(pages_in, 16)

                for g in range(G):
                    for second in range(2):
                        base = 0
                        if g == 0 and second == 0:
                            load(sp, g, second, 0, 0)
                            load(sp, g, second, 1, 1)
                            base = 2
                        chunks(sp, NC - base, lambda c_, u, r: reload(sp, g, second, c_, u), base)
                sp.wait_ge(o_out, G)
                sp.dma_start(d["oT"][TP, :, H:2 * H], om[:]).then_inc(stored, 16)
                sp.wait_ge(stored, 16)

            @block.tensor
            def _(pe):
                pe.wait_ge(q_ready, 1)
                for g in range(G):
                    def score(c_, u, r):
                        pe.wait_ge(chunk_in[u], (r + (NC * g + 1)) * (16 * J * PC))
                        pe.wait_ge(kept, c_ + KS * g)
                        for a in range(2):
                            for j in range(J):
                                out = psS[HT * j:HT * (j + 1), u].rearrange("p (q w) -> p q w", q=PC)
                                pe.matmul(out, qg[:, g, a, j], kt[u][:, j, :, a * P:(a + 1) * P],
                                          start=(a == 0), stop=False, skip_group_check=True)
                        for a in range(2):
                            for j in range(J):
                                out = psS[HT * j:HT * (j + 1), u].rearrange("p (q w) -> p q w", q=PC)
                                half = slice(a * PAGE // 2, (a + 1) * PAGE // 2)
                                i = pe.matmul(out[:, :, half], qr[:, g, a, j], kt[u][:, j, :, R:KW],
                                              start=False, stop=True, skip_group_check=True)
                        i.then_inc(scored, 1)
                        pe.drain()
                        pe.sem_inc(chunk_used, 1)

                    chunks(pe, NC, score)
                    pe.wait_ge(kept, NC + KS * g)
                    new = slice(TP * P, TP * P + SR)
                    for j in range(J):
                        out = psS[HT * j:HT * (j + 1), 0, 0:SR]
                        pe.matmul(out, qg[:, g, 0, j], KT[:, 0, new], start=True, stop=False, skip_group_check=True)
                        pe.matmul(out, qg[:, g, 1, j], KT[:, 1, new], start=False, stop=False, skip_group_check=True)
                        i = pe.matmul(out, qr[0:RO, g, 0, j], KR[:, new], start=False, stop=True, skip_group_check=True)
                    i.then_inc(scored, 1)

                    def values(c_, u, r):
                        pe.wait_ge(p_ready, c_ + (KS * g + 1))
                        pe.wait_ge(pt_ready, c_ + KS * g)
                        for q in range(PC):
                            i = pe.transpose(psT[:, u, q], pb[:, u, q * P:(q + 1) * P], ident[:])
                        i.then_inc(turned, 1)
                        pe.wait_ge(pt_ready, c_ + (KS * g + 1))
                        pe.wait_ge(chunk_in[u], (r + (NC * g + NC // 2 + 1)) * (16 * J * PC))
                        pe.wait_ge(added, c_ + KS * g)
                        for q in range(PC):
                            for j in range(J):
                                i = pe.matmul(psV[HT * j:HT * (j + 1), u, 0:R], pts[:, u, q, HT * j:HT * (j + 1)],
                                              vt[u][:, j, q], start=(q == 0), stop=(q == PC - 1), skip_group_check=True)
                        i.then_inc(pv_done, 1)
                        pe.drain()
                        pe.sem_inc(chunk_used, 1)

                    chunks(pe, NC, values)
                    n = NC + KS * g
                    pe.wait_ge(p_ready, n + 1)
                    pe.wait_ge(pt_ready, n)
                    pe.transpose(psT[0:SR, 0, 0], pb[:, 0, 0:SR], ident[:]).then_inc(turned, 1)
                    pe.wait_ge(pt_ready, n + 1)
                    pe.wait_ge(added, n)
                    for j in range(J):
                        i = pe.matmul(psV[HT * j:HT * (j + 1), 0, 0:R], pts[0:SR, 0, 0, HT * j:HT * (j + 1)],
                                      V[0:SR, TP], start=True, stop=True, skip_group_check=True)
                    i.then_inc(pv_done, 1)
                    pe.wait_ge(acc_ready, g + 1)
                    for a in range(2):
                        i = pe.transpose(psT[:, 1, a], acc[:, a * P:(a + 1) * P], ident[:])
                    i.then_inc(acc_turned, 1)
                    pe.wait_ge(ols_ready, g + 1)
                    for h in range(H):
                        for a in range(2):
                            i = pe.matmul(psO[:, h, 0:J * ST].rearrange("p (j t) -> p j t", j=J),
                                          w_uv[:, a, h * DK:(h + 1) * DK],
                                          ols[:, a].rearrange("p (j h t) -> p j h t", j=J, h=H)[:, :, h],
                                          start=(a == 0), stop=(a == 1))
                    i.then_inc(o_done, 1)

            @block.vector
            def _(dve):
                dve.memset(qr[:], 0.0)
                dve.memset(om[:], 0.0)
                dve.drain()
                for g in range(G):
                    for j in range(J):
                        at = TP * P + ST * (J * g + j)
                        for a in range(2):
                            dve.tensor_copy(qg[:, g, a, j].rearrange("p (h t) -> p h t", h=H), QT[:, a, :, at:at + ST])
                            i = dve.tensor_copy(qr[RO * a:RO * (a + 1), g, a, j].rearrange("p (h t) -> p h t", h=H),
                                                QR[:, :, at:at + ST])
                i.then_inc(q_ready, 1)
                dve.wait_ge(consts_in, 16)
                for g in range(G):
                    def keep(c_, u, r):
                        dve.wait_ge(scored, c_ + (KS * g + 1))
                        dve.tensor_scalar(S[:, bass.ds(c_ * CK, CK)], psS[:, u], 1.0, NEG, ALU.mult, ALU.max,
                                          accum_out=mxc[:, bass.ds(c_, 1)]).then_inc(kept, 1)

                    if g:
                        dve.wait_ge(p_ready, KS * g)
                    chunks(dve, NC, keep)
                    dve.wait_ge(scored, NC + KS * g + 1)
                    tail = S[:, NC * CK:NC * CK + SR]
                    dve.tensor_tensor(tail, psS[:, 0, 0:SR], mask[:, g], ALU.add)
                    dve.drain()
                    dve.tensor_reduce(mxc[:, NC:NC + 1], tail, AX_X, ALU.max).then_inc(kept, 1)
                    dve.drain()
                    dve.tensor_reduce(nm[:], mxc[:], AX_X, ALU.max)
                    dve.drain()
                    dve.tensor_scalar(nm[:], nm[:], -MLA_SCALE, None, ALU.mult).then_inc(max_ready, 1)
                    if g:
                        dve.wait_ge(acc_turned, g)
                    dve.memset(acc[:], 0.0)

                    def add(c_, u, r):
                        dve.wait_ge(turned, c_ + (KS * g + 1))
                        dve.tensor_copy(pts[:, u], psT[:, u]).then_inc(pt_ready, 1)
                        dve.wait_ge(pv_done, c_ + (KS * g + 1))
                        dve.tensor_tensor(acc[:], acc[:], psV[:, u, 0:R], ALU.add).then_inc(added, 1)

                    chunks(dve, NC, add)
                    n = NC + KS * g
                    dve.wait_ge(turned, n + 1)
                    dve.tensor_copy(pts[0:SR, 0, 0], psT[0:SR, 0, 0]).then_inc(pt_ready, 1)
                    dve.tensor_reduce(den[:], sums[:], AX_X, ALU.add)
                    dve.drain()
                    dve.reciprocal(den[:], den[:])
                    dve.wait_ge(pv_done, n + 1)
                    dve.tensor_tensor(acc[:], acc[:], psV[:, 0, 0:R], ALU.add).then_inc(added, 1)
                    dve.drain()
                    dve.tensor_scalar(acc[:], acc[:], den[:], None, ALU.mult).then_inc(acc_ready, 1)
                    dve.wait_ge(acc_turned, g + 1)
                    dve.tensor_copy(ols[:], psT[:, 1, 0:2]).then_inc(ols_ready, 1)
                    dve.wait_ge(o_done, g + 1)
                    dve.tensor_copy(om[:, :, J * ST * g:J * ST * (g + 1)], psO[:, :, 0:J * ST]).then_inc(o_out, 1)

            @block.scalar
            def _(act):
                act.wait_ge(pages_in, 16)
                for g in range(G):
                    base = 0
                    if g == 0:
                        load(act, 0, 0, 0, 0)
                        load(act, 0, 0, 1, 1)
                        base = 2
                    chunks(act, NC - base, lambda c_, u, r: reload(act, g, 0, c_, u), base)
                    reload(act, g, 1, 0, 0)
                    reload(act, g, 1, 1, 1)
                    act.wait_ge(max_ready, g + 1)

                    def exp(c_, u):
                        act.wait_ge(turned, c_ + KS * g)
                        act.activation(pb[:, u], S[:, bass.ds(c_ * CK, CK)], ACT.Exp, bias=nm[:], scale=MLA_SCALE,
                                       accum_out=sums[:, bass.ds(c_, 1)]).then_inc(p_ready, 1)

                    def step(c_, u, r):
                        exp(c_ + 1, 1 - u)
                        reload(act, g, 1, c_ + 2, u)

                    exp(0, 0)
                    chunks(act, NC - 2, step)
                    exp(NC - 1, 1)
                    act.wait_ge(turned, NC + KS * g)
                    act.activation(pb[:, 0, 0:SR], S[:, NC * CK:NC * CK + SR], ACT.Exp, bias=nm[:], scale=MLA_SCALE,
                                   accum_out=sums[:, NC:NC + 1]).then_inc(p_ready, 1)


def route_tensors(c):
    return {"dest8": c.sb("route_dest8", [P, NT, TOPK], I32), "w8": c.sb("route_w8", [P, NT, TOPK])}


def phase_mix_and_route(nc, d, m):
    with ExitStack() as st, Semaphores(nc) as s:
        c = Ctx(nc, st)
        dest8, w8 = m["dest8"], m["w8"]
        w_out = c.sb("p6_w_out", [P, KD, D])
        w_r = c.sb("p6_w_r", [P, KD, E])
        w_sh = c.sb("p6_w_sh", [P, KD, 2 * DE])
        w_dn = c.sb("p6_w_dn", [P, 2, D])
        ident = c.sb("p6_ident", [P, P])
        g_bc = c.sb("p6_g", [P, D])
        bias = c.sb("p6_bias", [P, E])
        before = c.sb("p6_before", [P, P])
        ones = c.sb("p6_ones", [P, P])
        token = c.sb("p6_token", [P, NT], I32)
        e_base = c.sb("p6_e_base", [P, 2, E])
        eps = c.sb("p6_eps", [P, 1])
        oT = c.sb("p6_oT", [P, 2, KD, P])
        x = c.sb("p6_x", [P, 2, D])
        hh = c.sb("p6_h", [P, 2, D])
        sq = c.sb("p6_sq", [P, D])
        ss = c.sb("p6_ss", [P, 1])
        n2 = c.sb("p6_n2", [P, 2, D])
        nT = c.sb("p6_nT", [P, KD, P])
        sg = c.sb("p6_sg", [P, DE])
        hs = c.sb("p6_hs", [P, DE])
        hT = c.sb("p6_hT", [P, 2, P])
        acc = c.sb("p6_acc", [P, D])
        scores = c.sb("p6_scores", [P, E])
        biased = c.sb("p6_biased", [P, E])
        g8 = c.sb("p6_g8", [P, NG, 8])
        gs = c.sb("p6_gs", [P, NG])
        m8 = c.sb("p6_m8", [P, 8])
        gr = c.sb("p6_gr", [P, NG])
        t8 = c.sb("p6_t8", [P, 8])
        rep = c.sb("p6_rep", [P, E])
        sel = c.sb("p6_sel", [P, E])
        seen = c.sb("p6_seen", [P, E])
        wd = c.sb("p6_wd", [P, E])
        ws = c.sb("p6_ws", [P, 1])
        dv = c.sb("p6_dv", [P, E])
        dv8 = c.sb("p6_dv8", [P, 2, 8])
        pf = c.sb("p6_pf", [P, 8])
        big = c.sb("p6_big", [P, 8])
        junk = c.sb("p6_junk", [P, 2, 8, E])
        d8f = c.sb("p6_d8f", [P, 8])
        d8 = c.sb("p6_d8", [P, 2, 8], I32)
        rk = c.sb("p6_rk", [P, E])
        near = c.sb("p6_near", [P, E])
        wn = c.sb("p6_wn", [P, E])
        dn8 = c.sb("p6_dn8", [P, 8])
        entry = c.sb("p6_entry", [P, 2, TOPK, 2], I32)
        zeros = c.sb("p6_zeros", [P, D])
        none = c.sb("p6_none", [P, E * SLOTS // P, 2], I32)
        cnt = c.sb("p6_cnt", [P, E], I32)
        psH = c.ps("p6_psH", [P, D])
        psT = c.ps("p6_psT", [P, KD, P])
        psG = c.ps("p6_psG", [P, 2 * DE])
        psR = c.ps("p6_psR", [P, 512])
        psD = c.ps("p6_psD", [P, D])
        FAR = 1e30

        consts_in = s.sem("p6_consts_in")
        tile_in = [s.sem(f"p6_tile_in{u}") for u in range(2)]
        none_stored = s.sem("p6_none_stored")
        h_done = s.sem("p6_h_done")
        h_ready = s.sem("p6_h_ready")
        rooted = s.sem("p6_rooted")
        n_ready = s.sem("p6_n_ready")
        n_turned = s.sem("p6_n_turned")
        nT_ready = s.sem("p6_nT_ready")
        routed = s.sem("p6_routed")
        gated = s.sem("p6_gated")
        scores_ready = s.sem("p6_scores_ready")
        silu_ready = s.sem("p6_silu_ready")
        hs_ready = s.sem("p6_hs_ready")
        hs_turned = s.sem("p6_hs_turned")
        hT_ready = s.sem("p6_hT_ready")
        shared_done = s.sem("p6_shared_done")
        acc_ready = s.sem("p6_acc_ready")
        sel_ready = s.sem("p6_sel_ready")
        ranked = s.sem("p6_ranked")
        slots_ready = s.sem("p6_slots_ready")
        n_stored = [s.sem(f"p6_n_stored{u}") for u in range(2)]
        acc_stored = s.sem("p6_acc_stored")
        table_stored = [s.sem(f"p6_table_stored{u}") for u in range(2)]
        count_ready = s.sem("p6_count_ready")
        count_stored = s.sem("p6_count_stored")
        NCONST = 10

        with nc.Block() as block:

            @block.sync
            def _(sp):
                def load(t, u):
                    sp.dma_start(oT[:, u], d["oT"][t]).then_inc(tile_in[u], 16)
                    sp.dma_start(x[:, u], d["x"][t]).then_inc(tile_in[u], 16)

                for dst, src in ((none, d["no_token"]), (ident, d["ident"]), (w_out, d["w_out"]), (w_r, d["w_router"]),
                                 (g_bc, d["g_ffn"].partition_broadcast(P)), (bias, d["router_bias"].partition_broadcast(P)),
                                 (before, d["before"]), (token, d["token"]), (e_base, d["e_base"])):
                    sp.dma_start(dst[:], src).then_inc(consts_in, 16)
                load(0, 0)
                load(1, 1)
                sp.dma_start(w_sh[:], d["w_sh"]).then_inc(consts_in, 16)
                sp.dma_start(w_dn[:], d["w_sh_down"]).then_inc(consts_in, 16)

                def step(t, u, r, more=True):
                    sp.wait_ge(h_ready, t + 1)
                    if more:
                        load(t + 2, u)
                    sp.wait_ge(n_ready, t + 1)
                    sp.dma_start(d["n2"][t], n2[:, u]).then_inc(n_stored[u], 16)
                    sp.wait_ge(acc_ready, t + 1)
                    sp.dma_start(d["acc"][t], acc[:]).then_inc(acc_stored, 16)

                tiles(sp, TP - 2, step)
                step(TP - 2, 0, 0)
                step(TP - 1, 1, 0, False)
                step(TP, 0, 0, False)
                for a in range(2):
                    sp.dma_start(d["n2"][NT + a], zeros[:]).then_inc(n_stored[a], 16)
                    sp.dma_start(d["acc"][NT + a], zeros[:]).then_inc(acc_stored, 16)
                sp.wait_ge(count_ready, 1)
                sp.dma_start(d["count"], cnt[0:1, :]).then_inc(count_stored, 16)
                sp.wait_ge(n_stored[0], 16 * (TP // 2 + 2))
                sp.wait_ge(n_stored[1], 16 * (TP // 2 + 1))
                sp.wait_ge(acc_stored, 16 * (NT + 2))
                sp.wait_ge(count_stored, 16)

            @block.tensor
            def _(pe):
                def mix(t, u, r):
                    pe.wait_ge(tile_in[u], 32 * r + 32)
                    pe.wait_ge(h_ready, t)
                    for a in range(2):
                        for k in range(KD):
                            i = pe.matmul(psH[:, 512 * a:512 * a + 512], oT[:, u, k], w_out[:, k, 512 * a:512 * a + 512],
                                          start=(k == 0), stop=(k == KD - 1))
                    i.then_inc(h_done, 1)

                def rest(t, u, r, sample=False):
                    pe.wait_ge(n_ready, t + 1)
                    pe.wait_ge(nT_ready, t)
                    for k in range(KD):
                        i = pe.transpose(psT[:, k], n2[:, u, k * P:(k + 1) * P], ident[:])
                    i.then_inc(n_turned, 1)
                    pe.wait_ge(nT_ready, t + 1)
                    pe.wait_ge(slots_ready, t)
                    for k in range(KD):
                        i = pe.matmul(psR[:, 0:E], nT[:, k], w_r[:, k], start=(k == 0), stop=(k == KD - 1))
                    i.then_inc(routed, 1)
                    pe.wait_ge(hs_ready, t)
                    for k in range(KD):
                        i = pe.matmul(psG[:], nT[:, k], w_sh[:, k], start=(k == 0), stop=(k == KD - 1))
                    i.then_inc(gated, 1)
                    pe.wait_ge(hs_ready, t + 1)
                    for k in range(2):
                        i = pe.transpose(psT[:, k], hs[:, k * P:(k + 1) * P], ident[:])
                    i.then_inc(hs_turned, 1)
                    pe.wait_ge(hT_ready, t + 1)
                    pe.wait_ge(acc_ready, t)
                    for a in range(2):
                        for k in range(2):
                            i = pe.matmul(psD[:, 512 * a:512 * a + 512], hT[:, k], w_dn[:, k, 512 * a:512 * a + 512],
                                          start=(k == 0), stop=(k == 1))
                    i.then_inc(shared_done, 1)
                    n = SR if sample else P
                    pe.wait_ge(sel_ready, t + 1)
                    pe.matmul(psR[0:n, E:2 * E], before[0:n, 0:n], sel[0:n], start=True, stop=True)
                    pe.matmul(psR[:, 2 * E:3 * E], ones[0:n], sel[0:n], start=True, stop=True).then_inc(ranked, 1)

                pe.wait_ge(consts_in, 16 * (NCONST + 2))
                mix(0, 0, 0)

                def step(t, u, r):
                    mix(t + 1, 1 - u, r + u)
                    rest(t, u, r)

                tiles(pe, TP, step)
                rest(TP, 0, TP // 2, True)

            @block.scalar
            def _(act):
                def front(t, u):
                    act.wait_ge(h_ready, t + 1)
                    act.activation(sq[:], hh[:, u], ACT.Square, accum_out=ss[:])
                    act.drain()
                    act.activation(ss[:], ss[:], ACT.Sqrt, bias=eps[:], scale=1.0 / D).then_inc(rooted, 1)

                def step(t, u, r, more=True):
                    act.wait_ge(n_turned, t + 1)
                    act.copy(nT[:, 0:4], psT[:, 0:4])
                    act.copy(nT[:, 4:8], psT[:, 4:8]).then_inc(nT_ready, 1)
                    act.wait_ge(routed, t + 1)
                    act.activation(scores[:], psR[:, 0:E], ACT.Sigmoid).then_inc(scores_ready, 1)
                    act.wait_ge(gated, t + 1)
                    act.activation(sg[:], psG[:, 0:DE], ACT.Silu).then_inc(silu_ready, 1)
                    act.wait_ge(hs_turned, t + 1)
                    act.copy(hT[:], psT[:, 0:2]).then_inc(hT_ready, 1)
                    if more:
                        front(t + 1, 1 - u)

                act.wait_ge(consts_in, 16 * (NCONST + 2))
                front(0, 0)
                tiles(act, TP, step)
                step(TP, 0, TP // 2, False)

            @block.vector
            def _(dve):
                def residual(t, u):
                    dve.wait_ge(h_done, t + 1)
                    dve.tensor_tensor(hh[:, u], x[:, u], psH[:], ALU.add).then_inc(h_ready, 1)

                def normed(t, u, stores):
                    dve.wait_ge(rooted, t + 1)
                    dve.reciprocal(ss[:], ss[:])
                    dve.drain()
                    if stores is not None:
                        dve.wait_ge(n_stored[u], stores)
                    dve.scalar_tensor_tensor(n2[:, u], hh[:, u], ss[:], g_bc[:], ALU.mult, ALU.mult).then_inc(n_ready, 1)

                def step(t, u, r, sample=False):
                    n = SR if sample else P
                    dve.wait_ge(scores_ready, t + 1)
                    dve.tensor_tensor(biased[:], scores[:], bias[:], ALU.add)
                    dve.drain()
                    for g in range(NG):
                        dve.max(g8[:, g], biased[:, g * GW:(g + 1) * GW])
                    dve.drain()
                    dve.tensor_tensor(gs[:].unsqueeze(2), g8[:, :, 0:1], g8[:, :, 1:2], ALU.add)
                    dve.drain()
                    dve.max(m8[:], gs[:])
                    dve.drain()
                    dve.memset(m8[:, TOPG:8], FAR)
                    dve.drain()
                    dve.match_replace(gr[:], m8[:], gs[:], -FAR)
                    dve.drain()
                    dve.tensor_scalar(gr[:], gr[:], -FAR, -1.0, ALU.is_equal, ALU.add)
                    dve.drain()
                    dve.scalar_tensor_tensor(biased[:].rearrange("p (g w) -> p g w", g=NG), bc(gr[:].unsqueeze(2), [P, NG, GW]),
                                             FAR, biased[:].rearrange("p (g w) -> p g w", g=NG), ALU.mult, ALU.add)
                    dve.drain()
                    dve.max(t8[:], biased[:])
                    dve.drain()
                    dve.match_replace(rep[:], t8[:], biased[:], 2 * FAR)
                    dve.drain()
                    dve.tensor_scalar(sel[:], rep[:], 2 * FAR, None, ALU.is_equal).then_inc(sel_ready, 1)
                    dve.wait_ge(gated, t + 1)
                    dve.wait_ge(silu_ready, t + 1)
                    dve.tensor_tensor(hs[:], sg[:], psG[:, DE:2 * DE], ALU.mult).then_inc(hs_ready, 1)
                    if not sample:
                        residual(t + 1, 1 - u)
                    dve.drain()
                    dve.tensor_tensor_reduce(wd[:], sel[:], scores[:], 1.0, 0.0, ALU.mult, ALU.add, ws[:])
                    dve.drain()
                    dve.tensor_scalar(ws[:], ws[:], 1e-20, None, ALU.add)
                    dve.drain()
                    dve.reciprocal(ws[:], ws[:])
                    dve.drain()
                    dve.tensor_scalar(wd[:], wd[:], ws[:], 2.5, ALU.mult, ALU.mult)
                    if not sample:
                        normed(t + 1, 1 - u, 16 * (r + u))
                    dve.wait_ge(shared_done, t + 1)
                    dve.wait_ge(acc_stored, 16 * t)
                    dve.tensor_tensor(acc[:], hh[:, u], psD[:], ALU.add).then_inc(acc_ready, 1)
                    dve.wait_ge(ranked, t + 1)
                    dve.wait_ge(table_stored[u], 128 * r)
                    dve.tensor_tensor(rk[0:n], seen[0:n], psR[0:n, E:2 * E], ALU.add)
                    dve.drain()
                    dve.tensor_tensor(seen[:], seen[:], psR[:, 2 * E:3 * E], ALU.add)
                    dve.tensor_tensor(dv[0:n], e_base[0:n, 0], rk[0:n], ALU.subtract)
                    dve.scalar_tensor_tensor(near[0:n], rk[0:n], float(CAP), sel[0:n], ALU.is_lt, ALU.mult)
                    dve.drain()
                    dve.tensor_tensor(rk[0:n], e_base[0:n, 1], rk[0:n], ALU.subtract)
                    dve.drain()
                    dve.tensor_tensor(dv[0:n], dv[0:n], sel[0:n], ALU.mult)
                    dve.tensor_tensor(rk[0:n], rk[0:n], near[0:n], ALU.mult)
                    dve.tensor_tensor(wn[0:n], wd[0:n], near[0:n], ALU.mult)
                    dve.drain()
                    dve.max(dv8[0:n, u], dv[0:n])
                    dve.max(dn8[0:n], rk[0:n])
                    dve.drain()
                    for k in range(TOPK):
                        dve.scalar_tensor_tensor(junk[0:n, 0, k], dv[0:n], dv8[0:n, u, k:k + 1], wd[0:n], ALU.is_equal,
                                                 ALU.mult, accum_out=entry[0:n, u, k, 1:2].bitcast(F32))
                        dve.scalar_tensor_tensor(junk[0:n, 1, k], rk[0:n], dn8[0:n, k:k + 1], wn[0:n], ALU.is_equal,
                                                 ALU.mult, accum_out=w8[0:n, t, k:k + 1])
                    dve.tensor_scalar(d8f[0:n], dn8[0:n], -1.0, BIG, ALU.mult, ALU.add)
                    dve.tensor_copy(entry[0:n, u, :, 0:1], bc(token[0:n, bass.ds(t, 1)].unsqueeze(1), [n, TOPK, 1]))
                    dve.drain()
                    dve.tensor_scalar(dest8[0:n, t], d8f[0:n], float(E * CAP - 1), None, ALU.min).then_inc(slots_ready, 1)

                dve.memset(seen[:], 0.0)
                dve.memset(big[:], BIG)
                dve.memset(zeros[:], 0.0)
                dve.memset(ones[:], 1.0)
                dve.memset(eps[:], EPS)
                dve.memset(dest8[:], 0)
                dve.memset(w8[:], 0.0)
                dve.drain()
                dve.sem_inc(consts_in, 16)
                dve.wait_ge(consts_in, 16 * (NCONST + 2))
                residual(0, 0)
                normed(0, 0, None)
                tiles(dve, TP, step)
                step(TP, 0, TP // 2, True)
                dve.drain()
                dve.tensor_copy(cnt[:], seen[:]).then_inc(count_ready, 1)

            @block.gpsimd
            def _(pool):
                pool.wait_ge(consts_in, 16 * (NCONST + 2))
                pool.dma_start(d["table"].rearrange("(p n) two -> p n two", p=P), none[:]).then_inc(none_stored, 16)
                pool.wait_ge(none_stored, 16)

                def step(t, u, r, sample=False):
                    n = SR if sample else P
                    pool.wait_ge(slots_ready, t + 1)
                    pool.tensor_tensor(pf[0:n], big[0:n], dv8[0:n, u], ALU.subtract)
                    pool.drain()
                    pool.tensor_copy(d8[0:n, u], pf[0:n])
                    pool.drain()
                    for k in range(TOPK):
                        pool.indirect_dma_start(d["table"], bass.IndirectOffsetOnAxis(ap=d8[0:n, u, k:k + 1], axis=0),
                                                entry[0:n, u, k], None).then_inc(table_stored[u], 16)

                tiles(pool, TP, step)
                step(TP, 0, TP // 2, True)
                pool.wait_ge(table_stored[0], 128 * (TP // 2 + 1))
                pool.wait_ge(table_stored[1], 128 * (TP // 2))


def phase_experts(nc, d):
    B = CAP - P
    HC = DE // P
    MORE = SLOTS // CAP - 1
    with ExitStack() as st, Semaphores(nc) as s:
        c = Ctx(nc, st)
        ident = c.sb("p8_ident", [P, P])
        wg = c.sb("p8_wg", [P, 2, KD, DE])
        wu = c.sb("p8_wu", [P, 2, KD, DE])
        wd = c.sb("p8_wd", [P, 2, HC, D])
        idx = c.sb("p8_idx", [P, 2, 2, 2], I32)
        rows = c.sb("p8_rows", [P, 2, 2], I32)
        zero = c.sb("p8_zero", [P, 1], I32)
        cnt = c.sb("p8_cnt", [1, E], I32)
        xg = c.sb("p8_xg", [P, 2, 2, D])
        xT = c.sb("p8_xT", [P, 2, KD, CAP])
        sg = c.sb("p8_sg", [P, HC, CAP])
        hT = c.sb("p8_hT", [P, HC, CAP])
        y = c.sb("p8_y", [P, 2, 2, D])
        pT = c.ps("p8_pT", [P, KD, P])
        pTb = pT[:].rearrange("p k n -> p (k n)")[:, 0:KD * B].rearrange("p (k n) -> p k n", k=KD)
        pG = c.ps("p8_pG", [P, HC, 256])
        pU = c.ps("p8_pU", [P, HC, 256])
        pY = c.ps("p8_pY", [P, 2, D])
        pYb = pY[:, 1, 0:KD * B].rearrange("p (k n) -> p k n", k=KD)

        consts_in = s.sem("p8_consts_in")
        idx_in = [s.sem(f"p8_idx_in{u}") for u in range(2)]
        idx_read = s.sem("p8_idx_read")
        w_in = [s.sem(f"p8_w_in{u}") for u in range(2)]
        x_in = [s.sem(f"p8_x_in{u}") for u in range(2)]
        turned_a = s.sem("p8_turned_a")
        turned_b = s.sem("p8_turned_b")
        xa_act = s.sem("p8_xa_act")
        xa_dve = s.sem("p8_xa_dve")
        xb_dve = s.sem("p8_xb_dve")
        gate_done = s.sem("p8_gate_done")
        up_done = s.sem("p8_up_done")
        silu_done = s.sem("p8_silu_done")
        h_ready = s.sem("p8_h_ready")
        ya_done = s.sem("p8_ya_done")
        yb_done = s.sem("p8_yb_done")
        ya_out = s.sem("p8_ya_out")
        yb_out = s.sem("p8_yb_out")
        y_stored = [s.sem(f"p8_y_stored{u}") for u in range(2)]
        f_load = s.sem("p8f_load")
        f_in = s.sem("p8f_in")
        f_rows = s.sem("p8f_rows")
        f_x_in = s.sem("p8f_x_in")
        f_turned = s.sem("p8f_turned")
        f_x_out = s.sem("p8f_x_out")
        f_gated = s.sem("p8f_gated")
        f_silu = s.sem("p8f_silu")
        f_h = s.sem("p8f_h")
        f_y = s.sem("p8f_y")
        f_ya_out = s.sem("p8f_ya_out")
        f_yb_out = s.sem("p8f_yb_out")
        f_done = s.sem("p8f_done")

        def load_idx(sp, e, u, first, sem):
            for a, (at, n) in enumerate(((0, P), (P, B))):
                sp.dma_start(idx[0:n, u, a], d["table"][bass.ds(e * SLOTS + (first + at), n)]).then_inc(sem, 16)

        def load_w(sp, e, u, sem):
            sp.dma_start(wg[:, u], d["w_gate"][e].rearrange("k p n -> p k n")).then_inc(sem, 16)
            sp.dma_start(wu[:, u], d["w_up"][e].rearrange("k p n -> p k n")).then_inc(sem, 16)
            sp.dma_start(wd[:, u], d["w_down"][e].rearrange("k p n -> p k n")).then_inc(sem, 16)

        def store_y(sp, e, u, sem):
            for a, (at, n) in enumerate(((0, P), (P, B))):
                sp.dma_start(d["ys"][bass.ds(e * CAP + at, n)], y[0:n, u, a]).then_inc(sem, 16)

        def gather(pool, u, sem):
            pool.tensor_tensor(rows[:, u, 0:1], idx[:, u, 0, 0:1], zero[:], ALU.add)
            i = pool.tensor_tensor(rows[0:B, u, 1:2], idx[0:B, u, 1, 0:1], zero[0:B], ALU.add)
            pool.drain()
            for a, n in enumerate((P, B)):
                pool.indirect_dma_start(xg[0:n, u, a], None, d["n2"].rearrange("t p n -> (t p) n"),
                                        bass.IndirectOffsetOnAxis(ap=rows[0:n, u, a:a + 1], axis=0)).then_inc(sem, 16)
            return i

        def turn_a(pe, u):
            for k in range(KD):
                i = pe.transpose(pT[:, k], xg[:, u, 0, k * P:(k + 1) * P], ident[:])
            return i

        def turn_b(pe, u, out=pTb):
            for k in range(KD):
                i = pe.transpose(out[:, k], xg[0:B, u, 1, k * P:(k + 1) * P], ident[0:B, 0:B])
            return i

        def hidden(pe, u, ps, w):
            for m in range(HC):
                for k in range(KD):
                    i = pe.matmul(ps[:, m, 0:CAP], w[:, u, k, m * P:(m + 1) * P], xT[:, u, k],
                                  start=(k == 0), stop=(k == KD - 1))
            return i

        def down(pe, u, a):
            at, n = ((0, P), (P, B))[a]
            for half in range(2):
                cols = slice(512 * half, 512 * half + 512)
                for k in range(HC):
                    i = pe.matmul(pY[0:n, a, cols], hT[:, k, at:at + n], wd[:, u, k, cols],
                                  start=(k == 0), stop=(k == HC - 1))
            return i

        def experts(eng, body, last):
            tiles(eng, E - 2, body)
            last(E - 2, 0, E // 2 - 1)
            last(E - 1, 1, E // 2 - 1)

        with nc.Block() as block:

            @block.sync
            def _(sp):
                sp.dma_start(ident[:], d["ident"]).then_inc(consts_in, 16)
                for e in range(2):
                    load_idx(sp, e, e, 0, idx_in[e])
                    load_w(sp, e, e, w_in[e])

                def step(e, u, r, more=True):
                    if more:
                        sp.wait_ge(idx_read, e + 1)
                        load_idx(sp, e + 2, u, 0, idx_in[u])
                    sp.wait_ge(ya_out, e + 1)
                    sp.wait_ge(yb_out, e + 1)
                    if more:
                        load_w(sp, e + 2, u, w_in[u])
                    store_y(sp, e, u, y_stored[u])

                experts(sp, step, lambda e, u, r: step(e, u, r, False))
                for u in range(2):
                    sp.wait_ge(y_stored[u], 32 * (E // 2))

            @block.gpsimd
            def _(pool):
                pool.memset(zero[:], 0)
                pool.drain()
                for e in range(2):
                    pool.wait_ge(idx_in[e], 32)
                    gather(pool, e, x_in[e]).then_inc(idx_read, 1)

                def step(e, u, r):
                    pool.wait_ge(turned_b, e + 1)
                    pool.wait_ge(idx_in[u], 32 * r + 64)
                    gather(pool, u, x_in[u]).then_inc(idx_read, 1)

                tiles(pool, E - 2, step)

            @block.tensor
            def _(pe):
                def turns(e, u, r):
                    pe.wait_ge(x_in[u], 32 * r + 32)
                    pe.wait_ge(xb_dve, e)
                    turn_a(pe, u).then_inc(turned_a, 1)

                def pT_free(e):
                    pe.wait_ge(xa_act, e + 1)
                    pe.wait_ge(xa_dve, e + 1)

                def products(e, u, r, more=True):
                    pe.wait_ge(w_in[u], 48 * r + 48)
                    pe.wait_ge(xb_dve, e + 1)
                    pe.wait_ge(h_ready, e)
                    hidden(pe, u, pG, wg).then_inc(gate_done, 1)
                    if more:
                        pT_free(e + 1)
                    hidden(pe, u, pU, wu).then_inc(up_done, 1)
                    if more:
                        turn_b(pe, 1 - u).then_inc(turned_b, 1)
                    pe.wait_ge(h_ready, e + 1)
                    pe.wait_ge(ya_out, e)
                    down(pe, u, 0).then_inc(ya_done, 1)
                    pe.wait_ge(yb_out, e)
                    down(pe, u, 1).then_inc(yb_done, 1)

                pe.wait_ge(consts_in, 16)
                turns(0, 0, 0)
                pT_free(0)
                turn_b(pe, 0).then_inc(turned_b, 1)

                def step(e, u, r):
                    turns(e + 1, 1 - u, r + u)
                    products(e, u, r)

                tiles(pe, E - 2, step)
                step(E - 2, 0, E // 2 - 1)
                products(E - 1, 1, E // 2 - 1, False)

            @block.scalar
            def _(act):
                def xa(e, u):
                    act.wait_ge(turned_a, e + 1)
                    act.copy(xT[:, u, 4:8, 0:P], pT[:, 4:8]).then_inc(xa_act, 1)

                def step(e, u, r, more=True):
                    if more:
                        act.wait_ge(up_done, e)
                        xa(e + 1, 1 - u)
                    act.wait_ge(gate_done, e + 1)
                    act.wait_ge(h_ready, e)
                    act.activation(sg[:], pG[:, :, 0:CAP], ACT.Silu).then_inc(silu_done, 1)
                    act.wait_ge(ya_done, e + 1)
                    act.wait_ge(y_stored[u], 32 * r)
                    act.copy(y[:, u, 0], pY[:, 0]).then_inc(ya_out, 1)

                xa(0, 0)
                tiles(act, E - 2, step)
                step(E - 2, 0, E // 2 - 1)
                step(E - 1, 1, E // 2 - 1, False)

            @block.vector
            def _(dve):
                def xa(e, u):
                    dve.wait_ge(turned_a, e + 1)
                    dve.tensor_copy(xT[:, u, 0:4, 0:P], pT[:, 0:4]).then_inc(xa_dve, 1)

                def xb(e, u):
                    dve.wait_ge(turned_b, e + 1)
                    dve.tensor_copy(xT[:, u, :, P:CAP], pTb).then_inc(xb_dve, 1)

                def step(e, u, r, more=True):
                    if more:
                        dve.wait_ge(up_done, e)
                        xa(e + 1, 1 - u)
                    dve.wait_ge(silu_done, e + 1)
                    dve.wait_ge(up_done, e + 1)
                    dve.wait_ge(yb_done, e)
                    dve.tensor_tensor(hT[:], sg[:], pU[:, :, 0:CAP], ALU.mult).then_inc(h_ready, 1)
                    if more:
                        xb(e + 1, 1 - u)
                    dve.wait_ge(yb_done, e + 1)
                    dve.wait_ge(y_stored[u], 32 * r)
                    dve.tensor_copy(y[0:B, u, 1], pY[0:B, 1]).then_inc(yb_out, 1)

                xa(0, 0)
                xb(0, 0)
                tiles(dve, E - 2, step)
                step(E - 2, 0, E // 2 - 1)
                step(E - 1, 1, E // 2 - 1, False)

        with nc.Block() as block:
            def further(eng, body, skip):
                with eng.Fori(0, E) as e:
                    have = eng.value_load(cnt[0:1, bass.ds(e, 1)], min_val=0, max_val=NT * P)
                    with eng.If(have > CAP):
                        with eng.Fori(1, MORE + 1) as b:
                            with eng.If(have > b * CAP):
                                body(e, b, e * MORE + b - 1)
                            with eng.Else():
                                skip(1)
                    with eng.Else():
                        skip(MORE)

            @block.sync
            def _(sp):
                sp.dma_start(cnt[:], d["count"]).then_inc(consts_in, 16)
                sp.wait_ge(consts_in, 32)

                def body(e, b, n):
                    sp.wait_ge(f_done, n)
                    load_idx(sp, e, 0, b * CAP, f_load)
                    load_w(sp, e, 0, f_load)
                    sp.wait_ge(f_load, 80)
                    sp.sem_clear(f_load)
                    sp.sem_inc(f_in, 1)

                def skip(k):
                    sp.sem_inc(f_in, k)

                further(sp, body, skip)

            @block.gpsimd
            def _(pool):
                def body(e, b, n):
                    pool.wait_ge(f_in, n + 1)
                    gather(pool, 0, f_rows)
                    pool.wait_ge(f_rows, 32)
                    pool.sem_inc(f_x_in, 1)
                    pool.wait_ge(f_ya_out, n + 1)
                    pool.wait_ge(f_yb_out, n + 1)
                    pool.tensor_tensor(rows[:, 1, 0:1], zero[:], zero[:], ALU.add)
                    for a, m in enumerate((P, B)):
                        pool.indirect_dma_start(d["acc"].rearrange("t p n -> (t p) n"),
                                                bass.IndirectOffsetOnAxis(ap=rows[0:m, 0, a:a + 1], axis=0),
                                                y[0:m, 0, a], None, compute_op=ALU.add).then_inc(f_rows, 16)
                    pool.wait_ge(f_rows, 64)
                    pool.dma_reset(range(f_rows.num, f_rows.num + 1))
                    pool.sem_clear(f_rows)
                    pool.sem_inc(f_done, 1)

                def skip(k):
                    pool.sem_inc(f_x_in, k)
                    pool.sem_inc(f_done, k)

                pool.wait_ge(consts_in, 32)
                further(pool, body, skip)

            @block.tensor
            def _(pe):
                def body(e, b, n):
                    pe.wait_ge(f_x_in, n + 1)
                    turn_a(pe, 0)
                    turn_b(pe, 0, pYb).then_inc(f_turned, 1)
                    pe.wait_ge(f_x_out, n + 1)
                    hidden(pe, 0, pG, wg)
                    hidden(pe, 0, pU, wu).then_inc(f_gated, 1)
                    pe.wait_ge(f_h, n + 1)
                    down(pe, 0, 0)
                    down(pe, 0, 1).then_inc(f_y, 1)

                def skip(k):
                    pe.drain()
                    pe.sem_inc(f_turned, k)
                    pe.sem_inc(f_gated, k)
                    pe.sem_inc(f_y, k)

                pe.wait_ge(consts_in, 32)
                further(pe, body, skip)

            @block.scalar
            def _(act):
                def body(e, b, n):
                    act.wait_ge(f_gated, n + 1)
                    act.activation(sg[:], pG[:, :, 0:CAP], ACT.Silu).then_inc(f_silu, 1)
                    act.wait_ge(f_y, n + 1)
                    act.wait_ge(f_done, n)
                    act.mul(y[:, 0, 0], pY[:, 0], idx[:, 0, 0, 1:2].bitcast(F32)).then_inc(f_ya_out, 1)

                def skip(k):
                    act.drain()
                    act.sem_inc(f_silu, k)
                    act.sem_inc(f_ya_out, k)

                act.wait_ge(consts_in, 32)
                further(act, body, skip)

            @block.vector
            def _(dve):
                def body(e, b, n):
                    dve.wait_ge(f_turned, n + 1)
                    dve.tensor_copy(xT[:, 0, :, 0:P], pT[:])
                    dve.tensor_copy(xT[:, 0, :, P:CAP], pYb).then_inc(f_x_out, 1)
                    dve.wait_ge(f_silu, n + 1)
                    dve.tensor_tensor(hT[:], sg[:], pU[:, :, 0:CAP], ALU.mult).then_inc(f_h, 1)
                    dve.wait_ge(f_y, n + 1)
                    dve.wait_ge(f_done, n)
                    dve.tensor_scalar(y[0:B, 0, 1], pY[0:B, 1], idx[0:B, 0, 1, 1:2].bitcast(F32), None,
                                      ALU.mult).then_inc(f_yb_out, 1)

                def skip(k):
                    dve.drain()
                    dve.sem_inc(f_x_out, k)
                    dve.sem_inc(f_h, k)
                    dve.sem_inc(f_yb_out, k)

                dve.wait_ge(consts_in, 32)
                further(dve, body, skip)


def phase_combine(nc, d, m):
    with ExitStack() as st, Semaphores(nc) as s:
        c = Ctx(nc, st)
        dest8, w8 = m["dest8"], m["w8"]
        ident = c.sb("p9_ident", [P, P])
        wpg = c.sb("p9_wpg", [P, KD, D])
        wpp = c.sb("p9_wpp", [P, 2, D])
        g1 = c.sb("p9_g1", [P, D])
        g2 = c.sb("p9_g2", [P, D])
        eps = c.sb("p9_eps", [P, 1])
        zero = c.sb("p9_zero", [P, TOPK], I32)
        still = c.sb("p9_still", [P, TOPK], I32)
        slot = c.sb("p9_slot", [P, 2, TOPK], I32)
        yg = c.sb("p9_yg", [P, 2, TOPK, D])
        hin = c.sb("p9_hin", [P, 2, D])
        hh = c.sb("p9_h", [P, 2, D])
        pt = c.sb("p9_p", [P, 2, R])
        sq = c.sb("p9_sq", [P, D])
        ss = c.sb("p9_ss", [P, 2])
        n3 = c.sb("p9_n3", [P, D])
        nT = c.sb("p9_nT", [P, KD + 2, P])
        gate = c.sb("p9_gate", [P, D])
        yo = c.sb("p9_y", [P, D])
        psT = c.ps("p9_psT", [P, 12, P])
        psG = c.ps("p9_psG", [P, D])
        psP = c.ps("p9_psP", [P, D])

        consts_in = s.sem("p9_consts_in")
        tile_in = [s.sem(f"p9_tile_in{u}") for u in range(2)]
        rows_in = [s.sem(f"p9_rows_in{u}") for u in range(2)]
        summed = s.sem("p9_summed")
        rooted = s.sem("p9_rooted")
        n_ready = s.sem("p9_n_ready")
        turned = s.sem("p9_turned")
        nT_ready = s.sem("p9_nT_ready")
        gated = s.sem("p9_gated")
        projected = s.sem("p9_projected")
        gate_ready = s.sem("p9_gate_ready")
        h_ready = s.sem("p9_h_ready")
        y_ready = s.sem("p9_y_ready")
        y_stored = s.sem("p9_y_stored")

        with nc.Block() as block:

            @block.sync
            def _(sp):
                def load(t, u):
                    sp.dma_start(hin[:, u], d["acc"][t]).then_inc(tile_in[u], 16)
                    sp.dma_start(pt[:, u], d["p"][t]).then_inc(tile_in[u], 16)

                load(0, 0)
                load(1, 1)
                for dst, src in ((ident, d["ident"]), (wpg, d["w_ple_gate"]), (wpp, d["w_ple_proj"]),
                                 (g1, d["g_ple"].partition_broadcast(P)), (g2, d["g_final"].partition_broadcast(P))):
                    sp.dma_start(dst[:], src).then_inc(consts_in, 16)

                def step(t, u, r, more=True):
                    if more:
                        sp.wait_ge(turned, t + 1)
                        load(t + 2, u)
                    sp.wait_ge(y_ready, t + 1)
                    sp.dma_start(d["y"][t], yo[:]).then_inc(y_stored, 16)

                tiles(sp, TP - 2, step)
                step(TP - 2, 0, 0)
                step(TP - 1, 1, 0, False)
                step(TP, 0, 0, False)
                sp.wait_ge(y_stored, 16 * NT)

            @block.gpsimd
            def _(pool):
                def gather(t, u):
                    pool.tensor_tensor(still[:], zero[:], zero[:], ALU.add)
                    pool.tensor_tensor(slot[:, u], dest8[:, t], zero[:], ALU.add)
                    pool.drain()
                    for k in range(TOPK):
                        pool.indirect_dma_start(yg[:, u, k], None, d["ys"],
                                                bass.IndirectOffsetOnAxis(ap=slot[:, u, k:k + 1], axis=0)).then_inc(rows_in[u], 16)

                pool.memset(zero[:], 0)
                pool.drain()
                gather(0, 0)
                gather(1, 1)

                def step(t, u, r):
                    pool.wait_ge(summed, t + 1)
                    gather(t + 2, u)

                tiles(pool, TP - 2, step)
                step(TP - 2, 0, 0)

            @block.tensor
            def _(pe):
                def turn(t, u, r):
                    pe.wait_ge(n_ready, t + 1)
                    pe.wait_ge(tile_in[u], 32 * r + 32)
                    for k in range(KD):
                        pe.transpose(psT[:, k], n3[:, k * P:(k + 1) * P], ident[:])
                    for k in range(2):
                        i = pe.transpose(psT[:, KD + k], pt[:, u, k * P:(k + 1) * P], ident[:])
                    i.then_inc(turned, 1)

                def products(t):
                    pe.wait_ge(nT_ready, t + 1)
                    pe.wait_ge(gate_ready, t)
                    for a in range(2):
                        cols = slice(512 * a, 512 * a + 512)
                        for k in range(KD):
                            i = pe.matmul(psG[:, cols], nT[:, k], wpg[:, k, cols], start=(k == 0), stop=(k == KD - 1))
                    i.then_inc(gated, 1)
                    pe.wait_ge(h_ready, t)
                    for a in range(2):
                        cols = slice(512 * a, 512 * a + 512)
                        for k in range(2):
                            i = pe.matmul(psP[:, cols], nT[:, KD + k], wpp[:, k, cols], start=(k == 0), stop=(k == 1))
                    i.then_inc(projected, 1)

                def step(t, u, r):
                    products(t)
                    turn(t + 1, 1 - u, r + u)

                pe.wait_ge(consts_in, 96)
                turn(0, 0, 0)
                tiles(pe, TP, step)
                products(TP)

            @block.scalar
            def _(act):
                def root(a):
                    act.drain()
                    act.activation(ss[:, a:a + 1], ss[:, a:a + 1], ACT.Sqrt, bias=eps[:], scale=1.0 / D).then_inc(rooted, 1)

                def square(t, u):
                    act.wait_ge(summed, t + 1)
                    act.activation(sq[:], hh[:, u], ACT.Square, accum_out=ss[:, 0:1])
                    root(0)

                def turn(t):
                    act.wait_ge(turned, t + 1)
                    for a in range(3):
                        w = min(4, KD + 2 - 4 * a)
                        i = act.copy(nT[:, 4 * a:4 * a + w], psT[:, 4 * a:4 * a + w])
                    i.then_inc(nT_ready, 1)

                def gates(t):
                    act.wait_ge(h_ready, t)
                    act.wait_ge(gated, t + 1)
                    act.activation(gate[:], psG[:], ACT.Sigmoid).then_inc(gate_ready, 1)

                def last_square(t, u):
                    act.wait_ge(h_ready, t + 1)
                    act.activation(sq[:], hh[:, u], ACT.Square, accum_out=ss[:, 1:2])
                    root(1)

                def step(t, u, r):
                    square(t + 1, 1 - u)
                    gates(t)
                    turn(t + 1)
                    last_square(t, u)

                act.wait_ge(consts_in, 96)
                square(0, 0)
                turn(0)
                tiles(act, TP, step)
                gates(TP)
                last_square(TP, 0)

            @block.vector
            def _(dve):
                def front(t, u, r, roots):
                    dve.drain()
                    dve.wait_ge(tile_in[u], 32 * r + 32)
                    dve.wait_ge(rows_in[u], 16 * TOPK * r + 16 * TOPK)
                    for k in range(TOPK):
                        src = hh if k else hin
                        i = dve.scalar_tensor_tensor(hh[:, u], yg[:, u, k], w8[:, t, k:k + 1], src[:, u], ALU.mult, ALU.add)
                        if k < TOPK - 1:
                            dve.drain()
                    i.then_inc(summed, 1)
                    dve.wait_ge(rooted, roots)
                    dve.reciprocal(ss[:, 0:1], ss[:, 0:1])
                    dve.drain()
                    dve.wait_ge(turned, t)
                    dve.scalar_tensor_tensor(n3[:], hh[:, u], ss[:, 0:1], g1[:], ALU.mult, ALU.mult).then_inc(n_ready, 1)

                def back(t, u, roots):
                    dve.wait_ge(gate_ready, t + 1)
                    dve.wait_ge(projected, t + 1)
                    dve.tensor_tensor(gate[:], gate[:], psP[:], ALU.mult)
                    dve.drain()
                    dve.tensor_tensor(hh[:, u], hh[:, u], gate[:], ALU.add).then_inc(h_ready, 1)
                    dve.wait_ge(rooted, roots)
                    dve.reciprocal(ss[:, 1:2], ss[:, 1:2])
                    dve.drain()
                    dve.wait_ge(y_stored, 16 * t)
                    dve.scalar_tensor_tensor(yo[:], hh[:, u], ss[:, 1:2], g2[:], ALU.mult, ALU.mult).then_inc(y_ready, 1)

                def step(t, u, r):
                    front(t + 1, 1 - u, r + u, 2 * t + 2)
                    back(t, u, 2 * t + 3)

                dve.memset(eps[:], EPS)
                dve.drain()
                dve.sem_inc(consts_in, 16)
                dve.wait_ge(consts_in, 96)
                front(0, 0, 0, 1)
                tiles(dve, TP, step)
                back(TP, 0, 2 * NT)


def constants():
    i = np.arange(P)
    tri = (i[:, None] <= i[None, :]).astype(np.float32)
    same_b = (i[:, None] // ST == i[None, :] // ST) & (i[:, None] < SR) & (i[None, :] < SR)
    tri_s = tri * same_b
    levels = np.zeros((P, LV, P), np.float32)
    for n in range(LV):
        s = 1 << n
        levels[:, n, :] = (i[:, None] // (2 * s) == i[None, :] // (2 * s)) & (i[:, None] // s % 2 == 0) & (i[None, :] // s % 2 == 1)
    half = RO // 2
    inv = 10000.0 ** (-np.arange(half, dtype=np.float32) / np.float32(half)).astype(np.float32)
    pos = np.zeros((NT, P), np.float32)
    pos[:TP] = np.arange(TP * P).reshape(TP, P)
    pos[TP, :SR] = np.tile(NPAGE * PAGE + np.arange(ST), SB)
    ang = (pos[:, :, None] * inv.astype(np.float32)).astype(np.float32)
    rows = np.arange(P)
    new = np.full((2, P, SR), NEG, np.float32)
    for g in range(2):
        b, t = 4 * g + rows // 32, rows % 8
        key = np.arange(SR)
        new[g][(key[None, :] // ST == b[:, None]) & (key[None, :] % ST <= t[:, None])] = 0.0
    return {
        "ident": np.eye(P, dtype=np.float32),
        "tri": np.ascontiguousarray(np.stack([tri, tri_s], 1)),
        "same": np.ascontiguousarray(np.stack([np.ones((P, P), np.float32), same_b.astype(np.float32)], 1)),
        "levels": levels,
        "batch_rows": (i[:, None] // ST == np.arange(SB)[None, :]).astype(np.float32),
        "causal": np.where(i[:, None] >= i[None, :], 0.0, NEG).astype(np.float32),
        "new_mask": np.ascontiguousarray(new.transpose(1, 0, 2)),
        "cos": np.cos(ang).astype(np.float32),
        "sin": np.sin(ang).astype(np.float32),
        "before": (i[:, None] < i[None, :]).astype(np.float32),
        "token": np.ascontiguousarray((np.arange(NT)[None, :] * P + i[:, None]).astype(np.int32)),
        "e_base": np.ascontiguousarray(np.broadcast_to(
            BIG - np.stack([SLOTS * np.arange(E), CAP * np.arange(E)]).astype(np.float32), (P, 2, E))),
        "no_token": np.ascontiguousarray(np.stack(
            [NT * P + np.arange(E * SLOTS) % CAP, np.zeros(E * SLOTS)], 1).astype(np.int32).reshape(P, -1, 2)),
    }


BIG = float(1 << 17)

_INS = ['x_prompt', 'x_sample', 'p_prompt', 'p_sample', 'cache_ckv', 'cache_krope', 'state_gdn', 'state_conv',
        'page_table', 'g_mix', 'w_in', 'gdn_conv_w', 'gdn_a_log', 'gdn_dt_bias', 'gdn_norm', 'mla_g_q', 'mla_w_uq',
        'mla_g_kv', 'mla_w_uk', 'mla_w_uv', 'w_out', 'g_ffn', 'w_router', 'router_bias', 'w_exp_gate', 'w_exp_up',
        'w_exp_down', 'w_sh_gate', 'w_sh_up', 'w_sh_down', 'g_ple', 'w_ple_gate', 'w_ple_proj', 'g_final']


def rows_in(w):
    return np.ascontiguousarray(w.reshape(-1, P, w.shape[-1]).transpose(1, 0, 2))


def tile_rows(a, b):
    w = a.shape[-1]
    z = np.zeros((NT * P - TP * P - SR, w), a.dtype)
    return np.concatenate([a.reshape(-1, w), b.reshape(-1, w), z]).reshape(NT, P, w)


def layout(v):
    w = v['w_in'][0]
    at = np.cumsum([0, 3 * ZW, ZW, H, H, R, R, RO])
    qkv, z, b, a, cq, ckv, kr = (w[:, at[n]:at[n + 1]] for n in range(7))
    ck = v['cache_ckv'][0]
    ins = {
        "x": tile_rows(v['x_prompt'], v['x_sample']),
        "p": tile_rows(v['p_prompt'], v['p_sample']),
        "w_nat": rows_in(np.concatenate([z, cq, ckv, kr, b, a], 1)),
        "w_qkv": rows_in(qkv),
        "conv_w": np.ascontiguousarray(v['gdn_conv_w'][0].reshape(4, CC, P).transpose(2, 1, 0)),
        "state_conv": np.ascontiguousarray(v['state_conv'][0].reshape(SB, 3, CC, P).transpose(3, 2, 0, 1)),
        "state": np.ascontiguousarray(v['state_gdn'][0].transpose(2, 0, 1, 3)),
        "g_mix": v['g_mix'][0], "g_ffn": v['g_ffn'][0], "g_ple": v['g_ple'][0], "g_final": v['g_final'],
        "a_log": v['gdn_a_log'][0], "dt_bias": v['gdn_dt_bias'][0], "gdn_norm": v['gdn_norm'][0],
        "g_q": v['mla_g_q'][0], "g_kv": v['mla_g_kv'][0],
        "w_uq": rows_in(v['mla_w_uq'][0]),
        "w_uk": np.ascontiguousarray(v['mla_w_uk'][0].transpose(2, 1, 0)),
        "w_uv": rows_in(v['mla_w_uv'][0].reshape(R, H * DK)),
        "w_out": rows_in(v['w_out'][0]),
        "w_router": rows_in(v['w_router'][0]), "router_bias": v['router_bias'][0],
        "w_sh": rows_in(np.concatenate([v['w_sh_gate'][0], v['w_sh_up'][0]], 1)),
        "w_sh_down": rows_in(v['w_sh_down'][0]),
        "w_ple_gate": rows_in(v['w_ple_gate'][0]), "w_ple_proj": rows_in(v['w_ple_proj'][0]),
        "w_gate": v['w_exp_gate'][0].reshape(E, KD, P, DE), "w_up": v['w_exp_up'][0].reshape(E, KD, P, DE),
        "w_down": v['w_exp_down'][0].reshape(E, 2, P, D),
        "cache": ck,
        "cacheT": np.concatenate([ck.reshape(-1, PAGE, 2, P).transpose(0, 3, 2, 1).reshape(-1, P, R),
                                  v['cache_krope'][0].reshape(-1, 2, PAGE // 2, RO).transpose(0, 1, 3, 2).reshape(-1, P, PAGE // 2)], 2),
        "pages": v['page_table'].reshape(2, 4, NPAGE // 4, 4).transpose(0, 2, 1, 3).reshape(1, -1),
    }
    return {n: np.ascontiguousarray(x) for n, x in ins.items()} | constants()


def outputs():
    return {"y": (NT, P, D), "ckv": (NT, P, R), "krope": (NT, P, RO), "gdn_p": (P, H, P), "gdn_s": (P, SB, H, P),
            "conv_p": (P, CC, 3), "conv_s": (P, CC, SB, 3)}


def scratch():
    return {"nat": (NT, P, NW), "yT": (NT, P, CC, P), "oT": (NT, P, KD, P), "n2": (NT + 2, P, D), "acc": (NT + 2, P, D),
            "table": [(E * SLOTS, 2), I32], "count": [(1, E), I32], "ys": (E * CAP, D)}


def program(nc, arrays):
    d = {n: nc.dram_tensor(f"in_{n}", a.shape, mybir.dt.from_np(a.dtype), kind="ExternalInput").ap() for n, a in arrays.items()}
    d |= {n: nc.dram_tensor(f"out_{n}", s, F32, kind="ExternalOutput").ap() for n, s in outputs().items()}
    for n, s in scratch().items():
        s, dt = s if isinstance(s, list) else (s, F32)
        d[n] = nc.dram_tensor(f"scratch_{n}", s, dt).ap()
    phase_project(nc, d)
    phase_gdn(nc, d)
    with ExitStack() as st:
        m = mla_tensors(Ctx(nc, st))
        phase_latents(nc, d, m)
        phase_prompt_attention(nc, d, m)
        phase_sample_attention(nc, d, m)
    with ExitStack() as st:
        m = route_tensors(Ctx(nc, st))
        phase_mix_and_route(nc, d, m)
        phase_experts(nc, d)
        phase_combine(nc, d, m)


def kernel(**inputs):
    import concourse.bacc as bacc
    from concourse.bass_utils import run_bass_kernel_spmd

    arrays = layout({n: np.asarray(inputs[n]) for n in _INS})
    nc = bacc.Bacc("TRN2", target_bir_lowering=False, num_devices=1)
    program(nc, arrays)
    r = run_bass_kernel_spmd(nc, [{f"in_{n}": a for n, a in arrays.items()}], core_ids=[0]).results[0]
    o = {n: r[f"out_{n}"] for n in outputs()}

    def split(a):
        w = a.shape[-1]
        a = a.reshape(NT * P, w)
        return a[:TP * P].reshape(1, TP * P, w), a[TP * P:TP * P + SR].reshape(SB, ST, w)

    y_p, y_s = split(o["y"])
    ckv_p, ckv_s = split(o["ckv"])
    kr_p, kr_s = split(o["krope"])
    return (y_p, y_s, ckv_p[None], kr_p[None],
            np.ascontiguousarray(o["gdn_p"].transpose(1, 0, 2))[None, None],
            np.ascontiguousarray(o["conv_p"].transpose(2, 1, 0)).reshape(1, 1, 3, CC * P),
            ckv_s[None], kr_s[None],
            np.ascontiguousarray(o["gdn_s"].transpose(1, 2, 0, 3))[None],
            np.ascontiguousarray(o["conv_s"].transpose(2, 3, 1, 0)).reshape(1, SB, 3, CC * P))
```
